# Optimizing a Trainium2 kernel written in Bass

```python
import math
import jax
import jax.numpy as jnp
from jax import lax
import numpy as np

D_MODEL = 1024
BATCH = 1
SEQ = 512
DEPTH = 2
DEC_BATCH = 8
DEC_SEQ = 4
PAST_LEN = 2048
PAGE_SIZE = 128

D_MIX = D_MODEL
H_A = 4
DK_A = 128
DV_A = 128
CONV_W = 4
DELTA_CHUNK = 64
H_B = 4
HD_B = 64
DILATED = ((128, 1), (512, 4), (2048, 16))
MAX_WINDOW = 2048
WIN_STEPS = 128
BLK = 128
H_C = 4
DC = 32
DV_C = 2 * DC
NUM_BUCKETS = 32
REL_MAX_DIST = 2048
H_BIAS = H_B + H_C
D_FF = 2816
EPS = 1e-6

A_QK = H_A * DK_A
A_V = H_A * DV_A
A_CONV_CH = 2 * A_QK + A_V
A_Z = A_V
B_W = H_B * HD_B
C_QK = H_C * 2 * DC
C_V = H_C * DV_C
PROJ_SPLITS = (A_CONV_CH, A_CONV_CH + A_Z, A_CONV_CH + A_Z + H_A, A_CONV_CH + A_Z + 2 * H_A,
               A_CONV_CH + A_Z + 2 * H_A + 3 * B_W)
D_IN = PROJ_SPLITS[-1] + 2 * C_QK + C_V

kernel_name = 'hybrid_delta_dilated_diff_decoder_step'

def rms_norm(x, w):
    xf = x.astype(jnp.float32)
    y = xf * lax.rsqrt(jnp.mean(xf * xf, axis=-1, keepdims=True) + EPS)
    return (y * w.astype(jnp.float32)).astype(x.dtype)

def l2_norm(x):
    return x * lax.rsqrt(jnp.sum(x * x, axis=-1, keepdims=True) + EPS)

def half_ffn(x, g, wg, wu, wd):
    h = rms_norm(x, g)
    return 0.5 * ((jax.nn.silu(h @ wg) * (h @ wu)) @ wd)

def rel_bucket(dist):
    dist = jnp.maximum(dist, 0)
    max_exact = NUM_BUCKETS // 2
    scaled = jnp.log(jnp.maximum(dist, 1).astype(jnp.float32) / max_exact) / math.log(REL_MAX_DIST / max_exact)
    large = jnp.minimum(max_exact + (scaled * (NUM_BUCKETS - max_exact)).astype(jnp.int32), NUM_BUCKETS - 1)
    return jnp.where(dist < max_exact, dist, large)

def split_projection(h, w_in_l):
    bsz, L = h.shape[:2]
    zp = (h @ w_in_l).astype(jnp.float32)
    a_qkv, a_z, a_b, a_a, b_qkv, c_qkv = jnp.split(zp, PROJ_SPLITS, axis=-1)
    q_b, k_b, v_b = [t.reshape(bsz, L, H_B, HD_B) for t in jnp.split(b_qkv, 3, axis=-1)]
    q_c, k_c, v_c = jnp.split(c_qkv, [C_QK, 2 * C_QK], axis=-1)
    q_c = q_c.reshape(bsz, L, H_C, 2, DC)
    k_c = k_c.reshape(bsz, L, H_C, 2 * DC)
    v_c = v_c.reshape(bsz, L, H_C, DV_C)
    return a_qkv, a_z, a_b, a_a, q_b, k_b, v_b, q_c, k_c, v_c

def gated_delta_rule(q, k, v, g, beta, s0):
    bsz, L, nh, dk = q.shape
    dv = v.shape[-1]
    c = min(DELTA_CHUNK, L)
    pad = (-L) % c
    if pad:
        def pz(t):
            return jnp.pad(t, [(0, 0), (0, pad)] + [(0, 0)] * (t.ndim - 2))
        q, k, v, g, beta = pz(q), pz(k), pz(v), pz(g), pz(beta)
    n = (L + pad) // c

    def chunks(t):
        t = t.reshape((bsz, n, c) + t.shape[2:])
        return jnp.moveaxis(jnp.moveaxis(t, 3, 2), 1, 0)

    qc, kc, vc, gc, bc = chunks(q), chunks(k), chunks(v), chunks(g), chunks(beta)
    gc = jnp.cumsum(gc, axis=-1)
    idx = jnp.arange(c)
    incl = idx[:, None] >= idx[None, :]
    strict = idx[:, None] > idx[None, :]
    diff = gc[..., :, None] - gc[..., None, :]
    decay = jnp.where(incl, jnp.exp(jnp.where(incl, diff, 0.0)), 0.0)
    kb = kc * bc[..., None]
    lmat = jnp.where(strict, jnp.einsum('nbhid,nbhjd->nbhij', kb, kc) * decay, 0.0)
    amat = lmat + jnp.eye(c, dtype=jnp.float32)
    u = lax.linalg.triangular_solve(amat, vc * bc[..., None], left_side=True, lower=True, unit_diagonal=True)
    w = lax.linalg.triangular_solve(amat, kb * jnp.exp(gc)[..., None], left_side=True, lower=True,
                                    unit_diagonal=True)
    qk = jnp.einsum('nbhid,nbhjd->nbhij', qc, kc) * decay

    def step(s, inp):
        q_i, k_i, u_i, w_i, g_i, qk_i = inp
        v_new = u_i - jnp.einsum('bhcd,bhde->bhce', w_i, s)
        o = (jnp.einsum('bhcd,bhde->bhce', q_i * jnp.exp(g_i)[..., None], s)
             + jnp.einsum('bhij,bhje->bhie', qk_i, v_new))
        g_last = g_i[..., -1]
        k_dec = k_i * jnp.exp(g_last[..., None] - g_i)[..., None]
        s = s * jnp.exp(g_last)[..., None, None] + jnp.einsum('bhcd,bhce->bhde', k_dec, v_new)
        return s, o

    s, o = lax.scan(step, s0, (qc, kc, u, w, gc, qk))
    o = jnp.moveaxis(jnp.moveaxis(o, 0, 1), 2, 3).reshape(bsz, n * c, nh, dv)[:, :L]
    return o, s

def delta_mixer(a_qkv, a_z, a_b, a_a, conv_buf, s0, lp):
    bsz, L, _ = a_qkv.shape
    xp = jnp.concatenate([conv_buf.astype(jnp.float32), a_qkv], axis=1)
    cw = lp['conv_w'].astype(jnp.float32)
    conv = sum(xp[:, j:j + L] * cw[j] for j in range(CONV_W))
    new_buf = xp[:, L:]
    q, k, v = jnp.split(jax.nn.silu(conv), [A_QK, 2 * A_QK], axis=-1)
    q = l2_norm(q.reshape(bsz, L, H_A, DK_A)) * (DK_A ** -0.5)
    k = l2_norm(k.reshape(bsz, L, H_A, DK_A))
    v = v.reshape(bsz, L, H_A, DV_A)
    beta = jax.nn.sigmoid(a_b)
    g = -jnp.exp(lp['a_log'].astype(jnp.float32)) * jax.nn.softplus(a_a + lp['dt_bias'].astype(jnp.float32))
    o, s = gated_delta_rule(q, k, v, g, beta, s0.astype(jnp.float32))
    o = rms_norm(o, lp['a_norm_w']) * jax.nn.silu(a_z.reshape(bsz, L, H_A, DV_A))
    return o.reshape(bsz, L, A_V), new_buf, s

def combine_by_denominator(lses, outs):
    wgt = jax.nn.softmax(jnp.stack(lses, 0), axis=0)
    return jnp.sum(wgt[..., None] * jnp.stack(outs, 0), axis=0)

def dilated_prompt(q, k, v, bias_tab):
    bsz, seq, nh, hd = q.shape
    scale = hd ** -0.5
    qi = jnp.arange(BLK)
    kj = jnp.arange(2 * BLK)
    rel = qi[:, None] + BLK - kj[None, :]
    lses, outs = [], []
    for window, dil in DILATED:
        lc = seq // dil
        nb = -(-lc // BLK)
        pr = nb * BLK - lc
        n = bsz * dil

        def to_cls(t):
            return t.reshape(bsz, lc, dil, nh, hd).transpose(0, 2, 1, 3, 4).reshape(n, lc, nh, hd)

        def band(t):
            tp = jnp.pad(to_cls(t), ((0, 0), (BLK, pr), (0, 0), (0, 0))).reshape(n, nb + 1, BLK, nh, hd)
            return jnp.concatenate([tp[:, :-1], tp[:, 1:]], axis=2)

        qb = jnp.pad(to_cls(q), ((0, 0), (0, pr), (0, 0), (0, 0))).reshape(n, nb, BLK, nh, hd)
        kb, vb = band(k), band(v)
        kpos = jnp.arange(nb)[:, None] * BLK - BLK + kj[None, :]
        valid = ((rel >= 0) & (rel <= window // dil))[None] & (kpos >= 0)[:, None, :]
        bias = jnp.moveaxis(bias_tab[rel_bucket(rel * dil)], -1, 0)
        logits = jnp.einsum('nbqhd,nbkhd->nbhqk', qb, kb) * scale + bias
        logits = jnp.where(valid[None, :, None], logits, -jnp.inf)
        lse = jax.nn.logsumexp(logits, axis=-1)
        o = jnp.einsum('nbhqk,nbkhd->nbqhd', jnp.exp(logits - lse[..., None]), vb)
        o = o.reshape(n, nb * BLK, nh, hd)[:, :lc]
        lse = jnp.swapaxes(lse, 2, 3).reshape(n, nb * BLK, nh)[:, :lc]
        outs.append(o.reshape(bsz, dil, lc, nh, hd).transpose(0, 2, 1, 3, 4).reshape(bsz, seq, nh, hd))
        lses.append(lse.reshape(bsz, dil, lc, nh).transpose(0, 2, 1, 3).reshape(bsz, seq, nh))
    return combine_by_denominator(lses, outs)

def dilated_sample(q, k_new, v_new, k_buf, v_buf, bias_tab):
    bsz, T, nh, hd = q.shape
    scale = hd ** -0.5
    wb = k_buf.shape[1]
    kc = jnp.concatenate([k_buf.astype(jnp.float32), k_new], axis=1)
    vc = jnp.concatenate([v_buf.astype(jnp.float32), v_new], axis=1)
    lses, outs = [], []
    for window, dil in DILATED:
        j = jnp.arange(window // dil + 1)
        idx = wb + jnp.arange(T)[:, None] - dil * j[None, :]
        valid = idx >= 0
        idxc = jnp.maximum(idx, 0)
        kg, vg = kc[:, idxc], vc[:, idxc]
        bias = bias_tab[rel_bucket(dil * j)].T
        logits = jnp.einsum('bthd,btjhd->bhtj', q, kg) * scale + bias[None, :, None, :]
        logits = jnp.where(valid[None, None], logits, -jnp.inf)
        lse = jax.nn.logsumexp(logits, axis=-1)
        outs.append(jnp.einsum('bhtj,btjhd->bthd', jnp.exp(logits - lse[..., None]), vg))
        lses.append(jnp.swapaxes(lse, 1, 2))
    return combine_by_denominator(lses, outs)

def diff_attn_core(q, k, v, q_pos, k_pos, bias_tab, lam):
    bsz, tk, nh = k.shape[:3]
    k = k.reshape(bsz, tk, nh, 2, DC)
    dist = q_pos[:, None] - k_pos[None, :]
    bias = jnp.moveaxis(bias_tab[rel_bucket(dist)], -1, 0)
    s = jnp.einsum('bqhmd,bkhmd->bmhqk', q, k) * (DC ** -0.5) + bias
    s = jnp.where(dist >= 0, s, -jnp.inf)
    p = jax.nn.softmax(s, axis=-1)
    return jnp.einsum('bhqk,bkhd->bqhd', p[:, 0] - lam * p[:, 1], v)

def diff_prompt(q, k, v, bias_tab, lam):
    bsz, seq = q.shape[:2]
    nb = seq // BLK
    qb = jnp.moveaxis(q.reshape((bsz, nb, BLK) + q.shape[2:]), 1, 0)
    qpos = jnp.arange(seq).reshape(nb, BLK)
    kpos = jnp.arange(seq)
    o = lax.map(lambda a: diff_attn_core(a[0], k, v, a[1], kpos, bias_tab, lam), (qb, qpos))
    return jnp.moveaxis(o, 0, 1).reshape(bsz, seq, H_C, DV_C)

def mixing_prompt(h, lp):
    bsz, L = h.shape[:2]
    a_qkv, a_z, a_b, a_a, q_b, k_b, v_b, q_c, k_c, v_c = split_projection(h, lp['w_in'])
    o_a, conv_state, delta_state = delta_mixer(
        a_qkv, a_z, a_b, a_a, jnp.zeros((bsz, CONV_W - 1, A_CONV_CH), jnp.float32),
        jnp.zeros((bsz, H_A, DK_A, DV_A), jnp.float32), lp)
    o_b = dilated_prompt(q_b, k_b, v_b, lp['bias_b'])
    o_c = diff_prompt(q_c, k_c, v_c, lp['bias_c'], lp['lam'])
    o_c = rms_norm(o_c, lp['c_norm_w']) * (1.0 - lp['lam_init'])
    mix = jnp.concatenate([o_a, o_b.reshape(bsz, L, B_W), o_c.reshape(bsz, L, C_V)], axis=-1)
    keep = min(MAX_WINDOW, L)
    return mix, (delta_state, conv_state, k_b[:, L - keep:], v_b[:, L - keep:], k_c, v_c)

def mixing_sample(h, lp, conv_buf, s0, win_k, win_v, pool_k, pool_v, page_table):
    bsz, T = h.shape[:2]
    a_qkv, a_z, a_b, a_a, q_b, k_b, v_b, q_c, k_c, v_c = split_projection(h, lp['w_in'])
    o_a, conv_state, delta_state = delta_mixer(a_qkv, a_z, a_b, a_a, conv_buf, s0, lp)
    o_b = dilated_sample(q_b, k_b, v_b, win_k, win_v, lp['bias_b'])
    past = page_table.shape[1] * pool_k.shape[1]
    k_past = pool_k[page_table].reshape(bsz, past, H_C, 2 * DC).astype(jnp.float32)
    v_past = pool_v[page_table].reshape(bsz, past, H_C, DV_C).astype(jnp.float32)
    k_all = jnp.concatenate([k_past, k_c], axis=1)
    v_all = jnp.concatenate([v_past, v_c], axis=1)
    qpos = past + jnp.arange(T)
    kpos = jnp.arange(past + T)
    o_c = diff_attn_core(q_c, k_all, v_all, qpos, kpos, lp['bias_c'], lp['lam'])
    o_c = rms_norm(o_c, lp['c_norm_w']) * (1.0 - lp['lam_init'])
    mix = jnp.concatenate([o_a, o_b.reshape(bsz, T, B_W), o_c.reshape(bsz, T, C_V)], axis=-1)
    return mix, (delta_state, conv_state, k_b, v_b, k_c, v_c)

def setup_inputs(seed: int = 0) -> dict:
    key = jax.random.key(seed)
    keys = iter(jax.random.split(key, 40))
    f32 = jnp.float32

    def normal(shape, scale=1.0):
        return scale * jax.random.normal(next(keys), shape, f32)

    def gain(shape):
        return 1.0 + 0.02 * jax.random.normal(next(keys), shape, f32)

    n_pages = PAST_LEN // PAGE_SIZE
    n_used = DEC_BATCH * n_pages
    n_pool = n_used + n_used // 4
    win_buf = min(MAX_WINDOW, PAST_LEN)
    page_table = jax.random.permutation(next(keys), n_pool)[:n_used].reshape(DEC_BATCH, n_pages).astype(jnp.int32)
    dt = jnp.exp(jax.random.uniform(next(keys), (DEPTH, H_A), f32, math.log(1e-3), math.log(1e-1)))
    return {
        'x_prompt': normal((BATCH, SEQ, D_MODEL)),
        'x_sample': normal((DEC_BATCH, DEC_SEQ, D_MODEL)),
        'state_delta': normal((DEPTH, DEC_BATCH, H_A, DK_A, DV_A), 0.1),
        'state_conv': normal((DEPTH, DEC_BATCH, CONV_W - 1, A_CONV_CH)),
        'cache_win_k': normal((DEPTH, DEC_BATCH, win_buf, H_B, HD_B)),
        'cache_win_v': normal((DEPTH, DEC_BATCH, win_buf, H_B, HD_B)),
        'cache_k': normal((DEPTH, n_pool, PAGE_SIZE, H_C, 2 * DC)),
        'cache_v': normal((DEPTH, n_pool, PAGE_SIZE, H_C, DV_C)),
        'page_table': page_table,
        'w_in': normal((DEPTH, D_MODEL, D_IN), D_MODEL ** -0.5),
        'conv_w': normal((DEPTH, CONV_W, A_CONV_CH), CONV_W ** -0.5),
        'a_log': jnp.log(jax.random.uniform(next(keys), (DEPTH, H_A), f32, 1.0, 16.0)),
        'dt_bias': jnp.log(jnp.expm1(dt)),
        'a_norm_w': gain((DEPTH, DV_A)),
        'lambda_q1': normal((DEPTH, DC), 0.1),
        'lambda_k1': normal((DEPTH, DC), 0.1),
        'lambda_q2': normal((DEPTH, DC), 0.1),
        'lambda_k2': normal((DEPTH, DC), 0.1),
        'c_norm_w': gain((DEPTH, DV_C)),
        'rel_bias': normal((NUM_BUCKETS, H_BIAS), 0.5),
        'w_out': normal((DEPTH, D_MIX, D_MODEL), D_MIX ** -0.5),
        'norm_ffn1': gain((DEPTH, D_MODEL)),
        'w1_gate': normal((DEPTH, D_MODEL, D_FF), D_MODEL ** -0.5),
        'w1_up': normal((DEPTH, D_MODEL, D_FF), D_MODEL ** -0.5),
        'w1_down': normal((DEPTH, D_FF, D_MODEL), D_FF ** -0.5),
        'norm_mix': gain((DEPTH, D_MODEL)),
        'norm_ffn2': gain((DEPTH, D_MODEL)),
        'w2_gate': normal((DEPTH, D_MODEL, D_FF), D_MODEL ** -0.5),
        'w2_up': normal((DEPTH, D_MODEL, D_FF), D_MODEL ** -0.5),
        'w2_down': normal((DEPTH, D_FF, D_MODEL), D_FF ** -0.5),
        'final_norm': gain((D_MODEL,)),
    }

def reference(x_prompt, x_sample, state_delta, state_conv, cache_win_k, cache_win_v, cache_k, cache_v,
              page_table, w_in, conv_w, a_log, dt_bias, a_norm_w, lambda_q1, lambda_k1, lambda_q2, lambda_k2,
              c_norm_w, rel_bias, w_out, norm_ffn1, w1_gate, w1_up, w1_down, norm_mix, norm_ffn2,
              w2_gate, w2_up, w2_down, final_norm):
    f32 = jnp.float32
    bias_b = rel_bias[:, :H_B].astype(f32)
    bias_c = rel_bias[:, H_B:].astype(f32)
    xp, xs = x_prompt, x_sample
    st_p = [[] for _ in range(6)]
    st_s = [[] for _ in range(6)]
    for l in range(DEPTH):
        xp = xp + half_ffn(xp, norm_ffn1[l], w1_gate[l], w1_up[l], w1_down[l])
        xs = xs + half_ffn(xs, norm_ffn1[l], w1_gate[l], w1_up[l], w1_down[l])
        lam_init = 0.8 - 0.6 * math.exp(-0.3 * l)
        lam = (jnp.exp(jnp.sum(lambda_q1[l].astype(f32) * lambda_k1[l].astype(f32)))
               - jnp.exp(jnp.sum(lambda_q2[l].astype(f32) * lambda_k2[l].astype(f32))) + lam_init)
        lp = dict(w_in=w_in[l], conv_w=conv_w[l], a_log=a_log[l], dt_bias=dt_bias[l], a_norm_w=a_norm_w[l],
                  c_norm_w=c_norm_w[l], lam=lam, lam_init=lam_init, bias_b=bias_b, bias_c=bias_c)
        mix_p, new_p = mixing_prompt(rms_norm(xp, norm_mix[l]), lp)
        mix_s, new_s = mixing_sample(rms_norm(xs, norm_mix[l]), lp, state_conv[l], state_delta[l],
                                     cache_win_k[l], cache_win_v[l], cache_k[l], cache_v[l], page_table)
        xp = xp + mix_p.astype(xp.dtype) @ w_out[l]
        xs = xs + mix_s.astype(xs.dtype) @ w_out[l]
        xp = xp + half_ffn(xp, norm_ffn2[l], w2_gate[l], w2_up[l], w2_down[l])
        xs = xs + half_ffn(xs, norm_ffn2[l], w2_gate[l], w2_up[l], w2_down[l])
        for i in range(6):
            st_p[i].append(new_p[i])
            st_s[i].append(new_s[i])
    y_prompt = rms_norm(xp, final_norm)
    y_sample = rms_norm(xs, final_norm)
    delta_p, conv_p, wk_p, wv_p, k_p, v_p = [jnp.stack(t, 0) for t in st_p]
    delta_s, conv_s, wk_s, wv_s, k_s, v_s = [jnp.stack(t, 0) for t in st_s]
    return (y_prompt, y_sample, delta_p, delta_s, conv_p, conv_s, wk_p, wk_s, wv_p, wv_s, k_p, k_s, v_p, v_s)


_drawn_inputs = setup_inputs


def setup_inputs(seed=0):
    import zlib

    import numpy as np

    out = dict(_drawn_inputs(seed))
    spreads = {}
    factors = {'a_norm_w': 18.812,
     'c_norm_w': 22.669,
     'norm_ffn1': 3.417,
     'norm_ffn2': 5.695,
     'final_norm': 7.67,
     'cache_win_k': 4.009,
     'cache_win_v': 3.219}
    for name, (base, spread) in spreads.items():
        noise = np.random.default_rng([zlib.crc32(name.encode()), seed]).standard_normal(out[name].shape)
        drawn = base * np.exp(spread * noise) if base else spread * noise
        out[name] = jnp.asarray(drawn.astype(out[name].dtype))
    for name, factor in factors.items():
        out[name] = (out[name] * factor).astype(out[name].dtype)
    return out
```

```python
from contextlib import ExitStack

import numpy as np

import concourse.bass as bass
from concourse import mybir

F32 = mybir.dt.float32
I32 = mybir.dt.int32
ACT = mybir.ActivationFunctionType
ALU = mybir.AluOpType
AX = mybir.AxisListType.X
ds = bass.ds

D, DEPTH, FF, EPS = 1024, 2, 2816, 1e-6
SEQ, NB_S, T_S = 512, 8, 4
NS = NB_S * T_S
NT = SEQ + NS
HALF = NT // 2
KD = D // 128
NF = FF // 128
NH, DK, CONV_CH, CONV_W = 4, 128, 1536, 4
D_IN = 3592
BA_COL, BC_COL = 2048, 2056
NZ = 28
PAST, PAGE, PAGES, POOL_PAGES = 2048, 128, 16, 160
U_TAB = 2304
U_MAX = PAST + T_S - 1
NEG = -1.0e30
KEYS_B = 896
LV = 26


def columns():
    at, where = 0, {}
    for name, n in (("ident", 128), ("ones", 128), ("tri", 128), ("neg", 128), ("blk64", 128), ("flip", 128),
                    ("lm", 7 * 128), ("tri4", 32), ("neg4", 32), ("blk4", 32), ("bsel", 8), ("comb", 64),
                    ("offc", 16), ("offb", 8), ("m0", 1), ("m1", 1), ("eps", 1), ("one", 1), ("lam0", 2), ("oml", 2)):
        where[name] = (at, at + n)
        at += n
    return where, at


def constant_arrays():
    where, n = columns()
    c = np.zeros((128, n), np.float32)

    def put(name, a):
        lo, hi = where[name]
        c[:a.shape[0], lo:hi] = a.reshape(a.shape[0], -1)

    p = np.arange(128)
    put("ident", np.eye(128))
    put("ones", np.ones((128, 128)))
    put("tri", (p[:, None] <= p[None, :]).astype(np.float32))
    put("neg", np.where(p[:, None] <= p[None, :], 0.0, NEG))
    put("blk64", (p[:, None] // 64 == p[None, :] // 64).astype(np.float32))
    put("flip", (p[:, None] + p[None, :] == 127).astype(np.float32))
    lm = np.zeros((128, 7, 128), np.float32)
    for k in range(7):
        b = 1 << k
        j, i = p[:, None], p[None, :]
        lm[:, k] = (j // (2 * b) == i // (2 * b)) & ((i // b) % 2 == 1) & ((j // b) % 2 == 0)
    put("lm", lm)
    q = np.arange(NS)
    same = q[:, None] // T_S == q[None, :] // T_S
    put("tri4", (same & (q[:, None] <= q[None, :])).astype(np.float32))
    put("neg4", np.where(same & (q[:, None] <= q[None, :]), 0.0, NEG))
    put("blk4", same.astype(np.float32))
    put("bsel", (q[:, None] // T_S == np.arange(8)[None, :]).astype(np.float32))
    b4, hh, mm, tt = p // 32, p // 8 % 4, p // 4 % 2, p % 4
    r = np.arange(64)
    put("comb", ((b4[:, None] == r[None, :] // 16) & (hh[:, None] == r[None, :] // 4 % 4)
                 & (tt[:, None] == r[None, :] % 4)).astype(np.float32))
    offc = np.zeros((128, 2, 8), np.float32)
    for g in range(2):
        offc[:, g] = np.where(np.arange(8)[None, :] == 4 * g + b4[:, None], 0.0, NEG)
    put("offc", offc)
    put("offb", np.where(np.arange(8)[None, :] == p[:, None] // 16, 0.0, NEG))
    put("m0", (mm == 0).astype(np.float32)[:, None])
    put("m1", (mm == 1).astype(np.float32)[:, None])
    put("eps", np.full((128, 1), EPS))
    put("one", np.ones((128, 1)))
    lam0 = np.array([0.8 - 0.6 * np.exp(-0.3 * l) for l in range(DEPTH)])
    put("lam0", np.tile(lam0, (128, 1)))
    put("oml", np.tile(1.0 - lam0, (128, 1)))
    dist = U_MAX - np.arange(U_TAB)
    dc = np.maximum(dist, 0)
    scaled = np.log(np.maximum(dc, 1).astype(np.float32) / np.float32(16)) / np.float32(np.log(2048 / 16))
    large = np.minimum(16 + (scaled.astype(np.float32) * np.float32(16)).astype(np.int32), 31)
    bucket = np.where(dc < 16, dc, large)
    e = np.zeros((34, U_TAB), np.float32)
    e[bucket, np.arange(U_TAB)] = 1.0
    count = ((dist >= 0) & (dist <= 128)).astype(int) + ((dist >= 0) & (dist <= 512) & (dist % 4 == 0)) \
        + ((dist >= 0) & (dist <= 2048) & (dist % 16 == 0))
    e[32] = np.where(count > 0, np.log(np.maximum(count, 1)), NEG)
    e[33] = np.where(dist >= 0, 0.0, NEG)
    pick = np.zeros((2, 8), np.float32)
    pick[0, :4] = 1.0
    pick[1, 4:] = 1.0
    return c, e, pick


SIGNALS = (
    "b_exp", "b_max", "b_out", "ba_mm", "ba_sb", "bege", "bk_free", "bk_in0", "bk_in1", "bkt_a", "bkt_v",
    "bp", "bpt_mm", "bpt_sb", "bq", "bs_mm", "bsn", "bv_free", "bv_in0", "bv_in1", "c_exp", "c_group_done",
    "c_max", "ck_free", "ck_in0", "ck_in1", "comb", "conv_acc", "conv_done", "conv_in", "conv_in_mm",
    "conv_rows", "conv_rows_mm", "conv_tail", "cpt_mm", "cpt_sb", "cq", "cs_mm", "csn", "cv_free", "cv_in0",
    "cv_in1", "decay_mm", "delta_out", "down_done", "down_free", "down_half", "dt_arg", "exp_done", "gb",
    "gdone", "gmm", "gsq", "gsqrt", "gu_done", "gu_free", "h_done", "in_bias", "in_const", "in_lam",
    "in_pages", "in_rows", "in_strip", "in_vec", "in_x", "kkqk", "kt_a", "kt_v", "kv_done", "lam_exp",
    "lam_sums", "layer_vecs", "lt_done", "m_mm", "m_sb", "mu_mm", "nw_sb", "o_mm", "out_done", "p_exp",
    "p_max", "p_mm", "p_out", "p_soft", "passed", "po_mm", "ppt_mm", "ppt_sb", "proj_a", "proj_done",
    "proj_v", "rms", "rows_a", "rows_mm", "rows_out", "rows_v", "s_mm", "setup_ev", "setup_mm", "silu",
    "soft", "sq_done", "ssq_done", "st_in", "st_new", "st_out", "staged", "state_done", "t_mm", "table_out",
    "tokm", "u_done", "vn_mm", "vn_sb", "w_loaded0", "w_loaded1", "w_mm", "x_act", "x_bege", "x_decay",
    "x_dt", "x_gb", "x_kkqk", "x_lt", "x_m", "x_mu", "x_new", "x_nw", "x_o", "x_out", "x_qe", "x_s", "x_so",
    "x_t", "x_u", "x_vb", "x_vn", "x_vnsb", "x_w", "x_ws", "y_mm", "y_out", "y_rows",
)


def trunk(nc, A, O, scratch):
    where, n_const = columns()
    with ExitStack() as ctx:
        def sb(name, *shape, dt=F32):
            return ctx.enter_context(nc.sbuf_tensor(name, [128, *shape], dt))

        xT = sb("residual", KD, NT)
        hT = sb("normed_or_mixed", KD, NT)
        work = sb("hidden_or_projected", NZ * NT)
        wslot = sb("weight_slots", 2, 2048)
        strips = sb("prompt_bias", 8, SEQ)
        bias_c = sb("sample_bias_c", U_MAX + 1)
        bias_cn = sb("sample_bias_c_new", 2, NS)
        bias_b = sb("sample_bias_b", KEYS_B)
        bias_bn = sb("sample_bias_b_new", NS)
        vtok = sb("values_by_token", 5, 512)
        con = sb("constants", n_const)
        cols_conv = sb("conv_columns", 2 * 48)
        cols_norm = sb("norm_columns", 60)
        lay_conv = sb("layer_conv", 48)
        lay_norm = sb("layer_norm", LV)
        lay_ba = sb("layer_ba_weights", KD, 8)
        all_ba = sb("ba_weights", DEPTH, KD, 8)
        small = sb("small", 160)
        pages = ctx.enter_context(nc.sbuf_tensor("page_numbers", [1, NB_S * PAGES], I32))
        arena = sb("arena", 9900)

        ps = ctx.enter_context(nc.psum_tensor("banks", [128, 8, 512], F32))
        flat = ps[:, :, :].rearrange("p b n -> p (b n)")

        def C(name, rows=128):
            lo, hi = where[name]
            return con[0:rows, lo:hi]

        def carve(tensor, start, *shape):
            n = int(np.prod(shape))
            v = tensor[:, start:start + n]
            if len(shape) == 2:
                v = v.rearrange("p (a b) -> p a b", a=shape[0])
            if len(shape) == 3:
                v = v.rearrange("p (a b c) -> p a b c", a=shape[0], b=shape[1])
            return v, start + n

        hidden, _ = carve(work, 0, NF, NT)
        gated, _ = carve(work, NF * NT, 2, NT)
        z, _ = carve(work, 0, NZ, NT)
        x_rows, _ = carve(work, 0, 5, D)
        bucket_rows, e_end = carve(work, 5 * D, U_TAB)
        table, t_end = carve(work, e_end, U_TAB)
        strip_raw, s_end = carve(work, 0, 8, SEQ)
        win_b, _ = carve(work, s_end + 1100, U_MAX + 1)
        assert s_end + 1100 >= 5 * D and s_end + 1100 + U_MAX + 1 <= NZ * NT
        vec_rows_a, r_end = carve(arena, 0, 128)
        vec_rows_b, r_end = carve(arena, r_end, 128)
        relb, r_end = carve(arena, r_end, 8)
        lam_rows, r_end = carve(arena, r_end, 4, DEPTH * 32)
        lam_prod, r_end = carve(arena, r_end, 2, DEPTH * 32)
        y_rows, _ = carve(work, 0, 5, D)

        a_log_c, dt_c = small[:, 0:8], small[:, 8:16]
        lam_sum, lam_all = small[:, 16:20], small[:, 20:22]
        lam, cnorm = small[:, 22:23], small[:, 23:24]
        ea, dtb = small[:, 24:28], small[:, 28:32]
        ba, _ = carve(small, 32, 5, 8)
        beta, _ = carve(small, 72, 5, 4)
        gdec, _ = carve(small, 92, 5, 4)
        spa, _ = carve(small, 112, 5, 4)
        spb, _ = carve(small, 132, 5, 4)
        sign = small[:, 152:153]

        at = 0
        k_rows, at = carve(arena, at, 5, 512)
        conv_tail, at = carve(arena, at, 12, 27)
        conv_out, at = carve(arena, at, CONV_CH)
        conv_in, at = carve(arena, at, CONV_CH)
        xs, at = carve(arena, at, 12, 8, 7)
        cvt, at = carve(arena, at, 2, NT)
        sq, at = carve(arena, at, 2, NT)
        rn, at = carve(arena, at, 2, NT)
        assert at <= 9900

        at = 0
        names = ("qc", "kc", "vc", "gB", "bB", "DT", "eG", "LT", "LK", "QKT", "KB", "VB", "KD", "M", "U", "T", "nW", "VN", "S")
        m = {}
        for n in names:
            m[n], at = carve(arena, at, NH, 128)
        gc, at = carve(arena, at, 4)
        kde, at = carve(arena, at, 4)
        ecol, at = carve(arena, at, 4)
        bege, at = carve(arena, at, 4)
        assert at <= 9900
        at = 0
        t = {}
        t["st"] = arena[:, 0:4096].rearrange("p (h b v) -> p h b v", h=4, b=8)
        at = 4096
        for n in ("qc", "kc", "vc", "eG", "DT", "LT", "LK", "QKT", "M", "U", "T", "nW", "QS"):
            t[n], at = carve(arena, at, NH, NS)
        for n in ("gB", "KB", "VB", "KD", "VN"):
            t[n], at = carve(arena, at, NH, 128)
        t["WQ"], at = carve(arena, at, NH, 8, 8)
        t["bB"], at = carve(arena, at, NH, NS)
        sgc, at = carve(arena, at, 4)
        skde, at = carve(arena, at, 4)
        secol, at = carve(arena, at, 4)
        sbege, at = carve(arena, at, 4)
        assert at <= 9900
        vblk = carve(work, 0, 8, 128)[0], carve(work, 1024, 8, 128)[0]

        dead = 16 * NT
        c_rows, at = carve(work, 0, 2, 4, 256)
        cv_rows, at = carve(work, at, 2, 4, 256)
        c_kt, at = carve(work, at, 2, 2, 512)
        c_s, at = carve(work, at, PAST + NS)
        assert at <= dead
        b_rows, at = carve(work, 0, 2, 7, 256)
        b_kt, at = carve(work, at, 2, 2, KEYS_B)
        b_s, at = carve(work, at, KEYS_B + NS)
        assert at <= dead
        sq2, at = carve(arena, 0, 2, NT)
        rn2, at = carve(arena, at, 2, NT)
        comb, at = carve(arena, at, 64)
        c_mx, start = carve(arena, at, 4)
        c_pt, at = carve(arena, start, 17, 64)
        qc_all, qend = arena[:, at:at + 1152], at + 1152
        b_pt, at = carve(arena, start, 8, 128)
        qb_all, at = arena[:, at:at + 2176], at + 2176
        at = max(qend, at)

        def qc_of(b, pair):
            return qc_all[:, 256 * b + 128 * pair:256 * b + 128 * pair + 128]

        def qb_of(b, pair):
            return qb_all[:, 256 * b + 128 * pair:256 * b + 128 * pair + 128]

        def maps(u):
            return 1 if u < 16 else 2

        def qk_of(u, mp):
            head = u // 4 % 4
            if u < 16:
                return 16 + head // 2, 18 + head // 2, 64 * (head % 2), 64
            return 22 + head // 2, 24 + head // 2, 64 * (head % 2) + 32 * mp, 32

        p_s = arena[:, at:at + 2048].rearrange("p (u m k) -> p u m k", u=2, m=2)
        at += 2048
        p_pt, at = carve(arena, at, 2, 4, 128)
        p_mx, at = carve(arena, at, 2, 8)
        assert at <= 9900

        s = {}
        for n in SIGNALS:
            s[n] = ctx.enter_context(nc.semaphore(n))
        block = ctx.enter_context(nc.Block())

        def alone(eng):
            eng.sem_inc(s["passed"], 1)

        def half(bank, h):
            return ps[:, bank + h, 0:HALF]

        def both(bank):
            return ps[:, bank:bank + 2, 0:HALF]

        def tok(v):
            return v.rearrange("p (h n) -> p h n", h=2)

        def over(v, n):
            return v.unsqueeze(2).broadcast_to([v.shape[0], v.shape[1], n])

        def per_head(v, n=4):
            return v.unsqueeze(1).broadcast_to([v.shape[0], n, v.shape[1]])

        @block.sync
        def _(sp):
            def ld(dst, src, name, inc=16):
                return sp.dma_start(dst, src).then_inc(s[name], inc)

            ld(con[:, :], A["consts"], "in_const")
            ld(x_rows[:, 0:4, :], A["x_prompt"][0].rearrange("(t p) d -> p t d", p=128), "in_x")
            ld(x_rows[0:NS, 4, :], A["x_sample"].rearrange("b t d -> (b t) d"), "in_x")
            ld(vec_rows_a[0:96, :], A["conv_w"].rearrange("l j (c p) -> (l j c) p", p=128), "in_vec")
            for l in range(DEPTH):
                for i, name in enumerate(("norm_ffn1", "norm_mix", "norm_ffn2")):
                    ld(vec_rows_b[LV * l + 8 * i:LV * l + 8 * i + 8, :],
                       A[name][l].rearrange("(k p) -> k p", p=128), "in_vec")
                ld(vec_rows_b[LV * l + 24:LV * l + 25, :], A["a_norm_w"][l:l + 1], "in_vec")
                for h in range(2):
                    ld(vec_rows_b[LV * l + 25:LV * l + 26, 64 * h:64 * h + 64], A["c_norm_w"][l:l + 1], "in_vec")
            ld(vec_rows_b[2 * LV:2 * LV + 8, :], A["final_norm"].rearrange("(k p) -> k p", p=128), "in_vec")
            ld(relb[0:32, :], A["rel_bias"], "in_bias")
            ld(relb[32:34, :], A["pick"], "in_bias")
            ld(bucket_rows[0:34, :], A["buckets"], "in_bias")
            for i, name in enumerate(("lambda_q1", "lambda_k1", "lambda_q2", "lambda_k2")):
                ld(lam_rows[:, i, :], A[name].rearrange("l d -> (l d)").partition_broadcast(128), "in_lam")
            ld(a_log_c, A["a_log"].rearrange("l h -> (l h)").partition_broadcast(128), "in_lam")
            ld(dt_c, A["dt_bias"].rearrange("l h -> (l h)").partition_broadcast(128), "in_lam")
            for l in range(DEPTH):
                ld(all_ba[:, l], A["w_in"][l, :, BA_COL:BC_COL].rearrange("(k p) n -> p k n", p=128), "in_lam")
            ld(pages[:, :], A["page_table"].rearrange("b n -> (b n)").unsqueeze(0), "in_pages")
            sp.wait_ge(s["setup_ev"], 11)
            ld(scratch[:, :], table[0:8, :], "table_out")
            sp.wait_ge(s["table_out"], 16)
            for h in range(8):
                src = bass.AP(tensor=scratch.tensor, offset=h * U_TAB + U_MAX - 384 - 127, ap=[[1, 128], [1, SEQ]])
                ld(strip_raw[:, h, :], src, "in_strip")
            for step in range(T_S):
                off = T_S - 1 - step
                for b in range(4):
                    ld(bias_c[32 * b + step:32 * b + 32:4, 0:PAST + T_S],
                       bass.AP(tensor=scratch.tensor, offset=4 * U_TAB + off, ap=[[U_TAB, 4], [0, 2], [1, PAST + T_S]]),
                       "in_rows")
                ld(win_b[step:128:4, 0:PAST + T_S],
                   bass.AP(tensor=scratch.tensor, offset=off, ap=[[0, 8], [U_TAB, 4], [1, PAST + T_S]]), "in_rows")

            sp.wait_ge(s["in_pages"], 16)

            def load_gate(l, w, f, slot):
                for i, name in enumerate((f"w{w + 1}_gate", f"w{w + 1}_up")):
                    dst = wslot[:, slot, 1024 * i:1024 * i + 1024].rearrange("p (k n) -> p k n", k=KD)
                    src = A[name][ds(l, 1), :, ds(f * 128, 128)].rearrange("l (k p) n -> p (l k) n", p=128)
                    ld(dst, src, f"w_loaded{slot}")

            def load_down(l, w, o, slot):
                dst = wslot[:, slot, 0:11 * 128].rearrange("p (k n) -> p k n", k=11)
                src = A[f"w{w + 1}_down"][ds(l, 1), slot * 1408:slot * 1408 + 1408, ds(o * 128, 128)]
                ld(dst, src.rearrange("l (k p) n -> p (l k) n", p=128), f"w_loaded{slot}", 32)

            def load_wide(l, name, col, slot):
                dst = wslot[:, slot, :].rearrange("p (k n) -> p k n", k=KD)
                src = A[name][ds(l, 1), :, ds(col, 256)].rearrange("l (k p) n -> p (l k) n", p=128)
                ld(dst, src, f"w_loaded{slot}", 32)

            def ffn_loads(l, w):
                it = l * 2 + w
                for slot in range(2):
                    if w == 0:
                        sp.wait_ge(s["down_half" if slot == 0 else "down_done"], it * 8 + 1)
                    else:
                        sp.wait_ge(s["out_done"], l * 8 + 6 + 2 * slot)
                    load_gate(l, w, slot, slot)
                with sp.Fori(1, 11) as j:
                    for slot in range(2):
                        sp.wait_ge(s["gu_done"], it * 22 + j * 2 + slot - 1)
                        load_gate(l, w, j * 2 + slot, slot)
                for slot in range(2):
                    sp.wait_ge(s["gu_done"], it * 22 + 21 + slot)
                    load_down(l, w, 0, slot)
                with sp.Fori(1, 8) as o:
                    for slot in range(2):
                        sp.wait_ge(s["down_half" if slot == 0 else "down_done"], it * 8 + o + 1)
                        load_down(l, w, o, slot)

            with sp.Fori(0, DEPTH) as l:
                ffn_loads(l, 0)
                for slot in range(2):
                    sp.wait_ge(s["down_half" if slot == 0 else "down_done"], l * 16 + 8 + 1)
                    load_wide(l, "w_in", slot * 256, slot)
                sp.wait_ge(s["x_new"], l * 3 + 2)
                ld(conv_in[0:24, :], A["state_conv"][ds(l, 1)].rearrange("l b j c -> (l b j) c"), "conv_in")
                with sp.Fori(1, 4) as j:
                    for slot in range(2):
                        sp.wait_ge(s["proj_done"], l * 28 + 4 * j + 2 * slot - 2)
                        load_wide(l, "w_in", j * 512 + slot * 256, slot)
                with sp.Fori(4, 7) as j:
                    for slot in range(2):
                        sp.wait_ge(s["proj_done"], l * 28 + 4 * j + 2 * slot - 2)
                        load_wide(l, "w_in", j * 512 + slot * 256 + 8, slot)
                for slot in range(2):
                    sp.wait_ge(s["proj_done"], l * 28 + 26 + 2 * slot)
                    load_wide(l, "w_out", slot * 256, slot)
                sp.wait_ge(s["state_done"], l * 5 + 5)
                for h in range(NH):
                    ld(t["st"][:, h], A["state_delta"][ds(l, 1), :, h].rearrange("l b k v -> k (l b) v"), "st_in")
                sp.wait_ge(s["gdone"], l * 14 + 14)
                alone(sp)
                with sp.Fori(0, 2) as g:
                    for name, dst, sem, free in (("cache_k", c_rows, "ck_in", "ck_free"),
                                                 ("cache_v", cv_rows, "cv_in", "cv_free")):
                        with sp.Fori(0, 8) as j:
                            for slot in range(2):
                                sp.wait_ge(s[free], (l * 2 + g) * 16 + j * 2 + slot + 1)
                                alone(sp)
                                for pg in range(4):
                                    page = sp.value_load(pages[0:1, ds(g * 64 + j * 8 + slot * 4 + pg, 1)],
                                                         min_val=0, max_val=POOL_PAGES - 1)
                                    ld(dst[:, slot, pg, :],
                                       A[name][ds(l, 1), ds(page, 1)].rearrange("l n k h d -> k (l n h d)"),
                                       f"{sem}{slot}")
                sp.wait_ge(s["c_group_done"], l * 2 + 2)
                alone(sp)
                for name in ("cache_win_k", "cache_win_v"):
                    free = "bk_free" if name == "cache_win_k" else "bv_free"
                    sem = "bk_in" if name == "cache_win_k" else "bv_in"
                    with sp.Fori(0, 4) as j:
                        for slot in range(2):
                            if name == "cache_win_k":
                                sp.wait_ge(s[free], l * 8 + j * 2 + slot + 1)
                            else:
                                sp.wait_ge(s["bk_free"], l * 8 + 8 + slot + 1)
                                alone(sp)
                                sp.wait_ge(s[free], l * 8 + j * 2 + slot + 1)
                            alone(sp)
                            rows = A[name][ds(l, 1), ds(j * 2 + slot, 1)].rearrange("l b p h d -> (l b p) (h d)")
                            far = rows[0:1536].rearrange("(q a r) c -> r a q c", a=32, r=16)
                            for r in range(4):
                                ld(b_rows[32 * r:32 * r + 32, slot, 0:3, :], far[r], f"{sem}{slot}")
                            ld(b_rows[:, slot, 3:7, :], rows[1536:2048].rearrange("(q p) c -> p q c", p=128),
                               f"{sem}{slot}")
                for slot in range(2):
                    sp.wait_ge(s["out_done"], l * 8 + 2 + 2 * slot)
                    load_wide(l, "w_out", 512 + slot * 256, slot)
                ffn_loads(l, 1)

        @block.gpsimd
        def _(gp):
            def st(dst, src, name):
                return gp.dma_start(dst, src).then_inc(s[name], 16)

            with gp.Fori(0, DEPTH) as l:
                gp.wait_ge(s["rows_a"], l * 5 + 5)
                gp.wait_ge(s["rows_v"], l * 5 + 5)
                for out_p, out_s, src in ((O["wk_p"], O["wk_s"], k_rows[:, :, 0:256]), (O["wv_p"], O["wv_s"], vtok[:, :, 0:256]),
                                          (O["k_p"], O["k_s"], k_rows[:, :, 256:512]), (O["v_p"], O["v_s"], vtok[:, :, 256:512])):
                    st(out_p[ds(l, 1)].rearrange("l b (t p) h d -> p (l b t) (h d)", p=128), src[:, 0:4, :], "rows_out")
                    st(out_s[ds(l, 1)].rearrange("l b t h d -> (l b t) (h d)"), src[0:NS, 4, :], "rows_out")
                gp.wait_ge(s["conv_rows"], l + 1)
                st(O["conv_p"][ds(l, 1)].rearrange("l b j c -> (l b j) c"), conv_out[0:3, :], "rows_out")
                st(O["conv_s"][ds(l, 1)].rearrange("l b j c -> (l b j) c"), conv_out[3:27, :], "rows_out")
                gp.wait_ge(s["state_done"], l * 5 + 5)
                st(O["delta_p"][ds(l, 1)].rearrange("l b h k v -> k (l b h) v"), m["S"][:, :, :], "delta_out")
                for h in range(NH):
                    gp.wait_ge(s["st_new"], l * 4 + h + 1)
                    st(O["delta_s"][ds(l, 1), :, h].rearrange("l b k v -> k (l b) v"), t["st"][:, h], "st_out")
            gp.wait_ge(s["y_rows"], 5)
            st(O["y_p"][0].rearrange("(t p) d -> p t d", p=128), y_rows[:, 0:4, :], "y_out")
            st(O["y_s"].rearrange("b t d -> (b t) d"), y_rows[0:NS, 4, :], "y_out")
            gp.wait_ge(s["y_out"], 32)
            gp.wait_ge(s["rows_out"], DEPTH * 160)
            gp.wait_ge(s["delta_out"], DEPTH * 16)
            gp.wait_ge(s["st_out"], DEPTH * 64)

        @block.tensor
        def _(pe):
            ident = C("ident")
            for name in ("down_half", "down_done"):
                pe.sem_inc(s[name], 1)
            for name in ("gmm", "ck_free", "cv_free", "bk_free", "bv_free", "cs_mm", "bs_mm"):
                pe.sem_inc(s[name], 2)

            def turn(out, in_, rows=128):
                return pe.transpose(out, in_, ident[0:rows, 0:rows])

            pe.wait_ge(s["in_const"], 16)
            pe.wait_ge(s["in_x"], 32)
            for i in range(1, 6):
                if i > 2:
                    pe.wait_ge(s["setup_ev"], i - 2)
                bank = 2 * (i % 2)
                n = 128 if i < 5 else NS
                for k in range(KD):
                    mm = turn(flat[:, 512 * bank + n * k:512 * bank + n * k + n],
                              x_rows[0:n, i - 1, 128 * k:128 * k + 128], n)
                mm.then_inc(s["setup_mm"], 1)
            pe.wait_ge(s["setup_ev"], 4)
            pe.wait_ge(s["in_vec"], 16 * (1 + DEPTH * 6 + 1))
            turn(ps[:, 0, 0:96], vec_rows_a[0:96, :], 96)
            turn(ps[:, 0, 96:156], vec_rows_b[0:60, :], 60).then_inc(s["setup_mm"], 1)
            pe.wait_ge(s["in_bias"], 48)
            for c in range(5):
                i, n = 7 + c, min(512, U_TAB - 512 * c)
                pe.wait_ge(s["setup_ev"], i - 2)
                pe.matmul(ps[0:8, 2 * (i % 2), 0:n], relb[0:34, :], bucket_rows[0:34, 512 * c:512 * c + n],
                          start=True, stop=True).then_inc(s["setup_mm"], 1)
            pe.wait_ge(s["in_strip"], 128)
            for h in range(8):
                i = 12 + h
                pe.wait_ge(s["setup_ev"], i - 2)
                pe.matmul(ps[:, 2 * (i % 2), :], C("flip"), strip_raw[:, h, :],
                          start=True, stop=True).then_inc(s["setup_mm"], 1)

            def norm(n):
                for k in range(KD):
                    pe.wait_ge(s["sq_done"], n * 8 + k + 1)
                    for h in range(2):
                        mm = pe.matmul(half(0, h), C("ones"), hT[:, k, h * HALF:(h + 1) * HALF],
                                       start=k == 0, stop=k == KD - 1)
                mm.then_inc(s["ssq_done"], 1)

            def ffn(l, w):
                it = l * 2 + w
                fill = l * 47 + 28 * w
                pe.wait_ge(s["h_done"], (l * 3 + 2 * w) * 8 + 8)
                alone(pe)
                with pe.Fori(0, 11) as j:
                    for slot in range(2):
                        pe.wait_ge(s[f"w_loaded{slot}"], (fill + j + 1) * 32)
                        pe.wait_ge(s["gu_free"], it * 22 + j * 2 + slot + 1)
                        for i in range(2):
                            for k in range(KD):
                                at = 1024 * i + 128 * k
                                for h in range(2):
                                    mm = pe.matmul(half(4 * slot + 2 * i, h), wslot[:, slot, at:at + 128],
                                                   hT[:, k, h * HALF:(h + 1) * HALF], start=k == 0, stop=k == KD - 1)
                        mm.then_inc(s["gu_done"], 1)
                pe.wait_ge(s["gu_free"], it * 22 + 22 + 2)
                alone(pe)
                with pe.Fori(0, 4) as j:
                    for u in range(2):
                        pe.wait_ge(s["down_free"], it * 8 + j * 2 + u + 1)
                        for part in range(2):
                            pe.wait_ge(s[f"w_loaded{part}"], (fill + 11 + j * 2 + u + 1) * 32)
                            for q in range(11):
                                for h in range(2):
                                    mm = pe.matmul(half(4 * u, h), wslot[:, part, 128 * q:128 * q + 128],
                                                   hidden[:, 11 * part + q, h * HALF:(h + 1) * HALF],
                                                   start=part == 0 and q == 0, stop=part == 1 and q == 10)
                            mm.then_inc(s["down_done" if part else "down_half"], 1)

            def project(l):
                pe.wait_ge(s["h_done"], (l * 3 + 1) * 8 + 8)
                alone(pe)
                with pe.Fori(0, 7) as j:
                    for slot in range(2):
                        pe.wait_ge(s[f"w_loaded{slot}"], (l * 47 + 19 + j + 1) * 32)
                        for u in range(2):
                            pe.wait_ge(s["proj_v" if u else "proj_a"], l * 14 + j * 2 + slot + 1)
                            for k in range(KD):
                                at = 256 * k + 128 * u
                                for h in range(2):
                                    mm = pe.matmul(half(4 * slot + 2 * u, h), wslot[:, slot, at:at + 128],
                                                   hT[:, k, h * HALF:(h + 1) * HALF], start=k == 0, stop=k == KD - 1)
                            mm.then_inc(s["proj_done"], 1)
                pe.wait_ge(s["proj_a"], l * 14 + 16)
                pe.wait_ge(s["proj_v"], l * 14 + 16)
                for b in range(5):
                    n = 128 if b < 4 else NS
                    for k in range(KD):
                        mm = pe.matmul(ps[0:n, 0, 8 * b:8 * b + 8], hT[:, k, 128 * b:128 * b + n], lay_ba[:, k, :],
                                       start=k == 0, stop=k == KD - 1)
                mm.then_inc(s["ba_mm"], 1)
                for b in range(5):
                    n = 128 if b < 4 else NS
                    a = 2 + 2 * (b % 2)
                    if b >= 2:
                        pe.wait_ge(s["rows_a"], l * 5 + b - 1)
                        pe.wait_ge(s["rows_v"], l * 5 + b - 1)
                    for i, tile in enumerate((18, 19, 20, 21, 24, 25, 26, 27)):
                        mm = turn(ps[0:n, a + i // 4, 128 * (i % 4):128 * (i % 4) + 128], z[:, tile, 128 * b:128 * b + n])
                    mm.then_inc(s["rows_mm"], 1)
                pe.wait_ge(s["conv_tail"], l + 1)
                pe.wait_ge(s["rows_v"], l * 5 + 4)
                for c in range(12):
                    mm = turn(ps[0:27, 5 + c // 4, 128 * (c % 4):128 * (c % 4) + 128], conv_tail[:, c, :])
                mm.then_inc(s["conv_rows_mm"], 1)
                pe.wait_ge(s["conv_in"], (l + 1) * 16)
                alone(pe)
                for c in range(12):
                    mm = turn(ps[:, 1, 24 * c:24 * c + 24], conv_in[0:24, 128 * c:128 * c + 128], 24)
                mm.then_inc(s["conv_in_mm"], 1)

            def square_sums(base, u, ones, sqb):
                pe.wait_ge(s["gsq"], base + u + 1)
                pe.wait_ge(s["gsqrt"], base + u + 1)
                for h in range(2):
                    mm = pe.matmul(half(2 * (u % 2), h), ones, sqb[:, u % 2, h * HALF:(h + 1) * HALF],
                                   start=True, stop=True)
                mm.then_inc(s["gmm"], 1)

            def chunk(l, c):
                it = l * 4 + c
                pe.wait_ge(s["staged"], it + 1)
                for h in range(NH):
                    turn(ps[:, 0, 128 * h:128 * h + 128], m["kc"][:, h, :])
                    mm = turn(ps[:, 1, 128 * h:128 * h + 128], m["vc"][:, h, :])
                mm.then_inc(s["tokm"], 1)
                pe.wait_ge(s["gb"], it + 1)
                for h in range(NH):
                    hs = slice(128 * h, 128 * h + 128)
                    pe.matmul(ps[:, 2, hs], m["gB"][:, h, :], C("tri"), start=True, stop=True)
                    pe.matmul(ps[:, 3, hs], m["bB"][:, h, :], ident, start=True, stop=True)
                pe.matmul(ps[:, 4, 0:4], C("tri"), m["gB"][:, :, 0], start=True, stop=True).then_inc(s["decay_mm"], 1)
                for h in range(NH):
                    hs = slice(128 * h, 128 * h + 128)
                    pe.matmul(ps[:, 5, hs], m["kc"][:, h, :], m["kc"][:, h, :], start=True, stop=True)
                    mm = pe.matmul(ps[:, 6, hs], m["kc"][:, h, :], m["qc"][:, h, :], start=True, stop=True)
                mm.then_inc(s["kkqk"], 1)
                with pe.Fori(1, 7) as k:
                    pe.wait_ge(s["u_done"], it * 7 + k)
                    for h in range(NH):
                        mm = turn(ps[:, 6, 128 * h:128 * h + 128], m["U"][:, h, :])
                    mm.then_inc(s["t_mm"], 1)
                    pe.wait_ge(s["lt_done"], it * 6 + k)
                    for h in range(NH):
                        mm = pe.matmul(ps[:, 7, 128 * h:128 * h + 128], m["LK"][:, h, :], m["T"][:, h, :], start=True, stop=True)
                    mm.then_inc(s["m_mm"], 1)
                    pe.wait_ge(s["m_sb"], it * 6 + k)
                    for h in range(NH):
                        mm = pe.matmul(ps[:, 5, 128 * h:128 * h + 128], m["M"][:, h, :], m["U"][:, h, :], start=True, stop=True)
                    mm.then_inc(s["mu_mm"], 1)
                pe.wait_ge(s["u_done"], it * 7 + 7)
                pe.wait_ge(s["kv_done"], it + 1)
                for h in range(NH):
                    mm = pe.matmul(ps[:, 7, 128 * h:128 * h + 128], m["KB"][:, h, :], m["U"][:, h, :], start=True, stop=True)
                mm.then_inc(s["w_mm"], 1)
                pe.wait_ge(s["nw_sb"], it + 1)
                for h in range(NH):
                    hs = slice(128 * h, 128 * h + 128)
                    pe.matmul(ps[:, 2, hs], m["U"][:, h, :], m["VB"][:, h, :], start=True, stop=False)
                    mm = pe.matmul(ps[:, 2, hs], m["nW"][:, h, :], m["S"][:, h, :], start=False, stop=True)
                mm.then_inc(s["vn_mm"], 1)
                pe.wait_ge(s["vn_sb"], it + 1)
                for h in range(NH):
                    hs = slice(128 * h, 128 * h + 128)
                    pe.matmul(ps[:, 3, hs], m["S"][:, h, :], m["qc"][:, h, :], start=True, stop=False)
                    mm = pe.matmul(ps[:, 3, hs], m["VN"][:, h, :], m["QKT"][:, h, :], start=False, stop=True)
                mm.then_inc(s["o_mm"], 1)
                for h in range(NH):
                    mm = pe.matmul(ps[:, 4, 128 * h:128 * h + 128], m["KD"][:, h, :], m["VN"][:, h, :], start=True, stop=True)
                mm.then_inc(s["s_mm"], 1)

            def sample_chunk(l):
                pe.wait_ge(s["x_act"], l * 5 + 1)
                for h in range(NH):
                    turn(ps[0:NS, 0, 128 * h:128 * h + 128], t["kc"][:, h, :])
                    mm = turn(ps[0:NS, 1, 128 * h:128 * h + 128], t["vc"][:, h, :])
                pe.wait_ge(s["x_gb"], l + 1)
                for h in range(NH):
                    hs = slice(NS * h, NS * h + NS)
                    pe.matmul(ps[:, 2, hs], t["gB"][0:NS, h, :], C("tri4", NS), start=True, stop=True)
                    pe.matmul(ps[0:NS, 3, hs], t["bB"][0:NS, h, :], ident[0:NS, 0:NS], start=True, stop=True)
                pe.matmul(ps[0:NS, 4, 0:4], C("tri4", NS), t["gB"][0:NS, :, 0], start=True, stop=True)
                pe.matmul(ps[0:NS, 4, 4:8], C("blk4", NS), t["gB"][0:NS, :, 0], start=True, stop=True).then_inc(s["x_decay"], 1)
                for h in range(NH):
                    hs = slice(NS * h, NS * h + NS)
                    pe.matmul(ps[0:NS, 5, hs], t["kc"][:, h, :], t["kc"][:, h, :], start=True, stop=True)
                    mm = pe.matmul(ps[0:NS, 6, hs], t["kc"][:, h, :], t["qc"][:, h, :], start=True, stop=True)
                mm.then_inc(s["x_kkqk"], 1)
                pe.wait_ge(s["x_u"], l * 2 + 1)
                alone(pe)
                for h in range(NH):
                    mm = turn(ps[0:NS, 6, NS * h:NS * h + NS], t["U"][0:NS, h, :], NS)
                mm.then_inc(s["x_t"], 1)
                pe.wait_ge(s["x_lt"], l + 1)
                alone(pe)
                for h in range(NH):
                    mm = pe.matmul(ps[0:NS, 7, NS * h:NS * h + NS], t["LK"][0:NS, h, :], t["T"][0:NS, h, :], start=True, stop=True)
                mm.then_inc(s["x_m"], 1)
                pe.wait_ge(s["x_act"], l * 5 + 4)
                alone(pe)
                for h in range(NH):
                    mm = pe.matmul(ps[0:NS, 5, NS * h:NS * h + NS], t["M"][0:NS, h, :], t["U"][0:NS, h, :], start=True, stop=True)
                mm.then_inc(s["x_mu"], 1)
                pe.wait_ge(s["x_u"], l * 2 + 2)
                for h in range(NH):
                    mm = pe.matmul(ps[:, 7, NS * h:NS * h + NS], t["KB"][0:NS, h, :], t["U"][0:NS, h, :], start=True, stop=True)
                mm.then_inc(s["x_w"], 1)
                pe.wait_ge(s["x_act"], l * 5 + 5)
                pe.wait_ge(s["x_qe"], l + 1)
                pe.wait_ge(s["st_in"], l * 64 + 64)
                for h in range(NH):
                    for b in range(NB_S):
                        mm = pe.matmul(ps[:, 2, 64 * h + 8 * b:64 * h + 8 * b + 8], t["st"][:, h, b, :], t["WQ"][:, h, b, :],
                                       start=True, stop=True)
                mm.then_inc(s["x_ws"], 1)
                pe.wait_ge(s["x_nw"], l + 1)
                alone(pe)
                for h in range(NH):
                    hs = slice(128 * h, 128 * h + 128)
                    pe.matmul(ps[0:NS, 3, hs], t["U"][0:NS, h, :], t["VB"][0:NS, h, :], start=True, stop=False)
                    mm = pe.matmul(ps[0:NS, 3, hs], t["nW"][:, h, :], ident, start=False, stop=True)
                mm.then_inc(s["x_vn"], 1)
                pe.wait_ge(s["x_vnsb"], l + 1)
                alone(pe)
                for h in range(NH):
                    mm = pe.matmul(ps[:, 4, NS * h:NS * h + NS], t["VN"][0:NS, h, :], t["QKT"][0:NS, h, :], start=True, stop=True)
                mm.then_inc(s["x_o"], 1)
                for h in range(NH):
                    pe.wait_ge(s["x_vb"], l * 4 + h + 1)
                    if h >= 2:
                        pe.wait_ge(s["st_new"], l * 4 + h - 1)
                    for i in range(2):
                        mm = pe.matmul(ps[:, (6 if h % 2 else 0) + i, :], t["KD"][0:NS, h, :],
                                       vblk[h % 2][0:NS, 4 * i:4 * i + 4, :], start=True, stop=True)
                    mm.then_inc(s["x_s"], 1)

            def group_c(l, g):
                G = l * 2 + g
                pe.wait_ge(s["cq"], G + 1)

                def scores(n):
                    pe.wait_ge(s["kt_a"], G * 16 + n + 1)
                    pe.wait_ge(s["kt_v"], G * 16 + n + 1)
                    for pair in range(2):
                        mm = pe.matmul(ps[:, n % 4, :], qc_of(n // 4, pair), c_kt[:, n % 2, pair, :],
                                       start=n < 4 and pair == 0, stop=n >= 12 and pair == 1)
                    mm.then_inc(s["cs_mm"], 1)

                for n in range(16):
                    pe.wait_ge(s[f"ck_in{n % 2}"], (G * 8 + n // 2 + 1) * 64)
                    if n >= 2:
                        pe.wait_ge(s["kt_a"], G * 16 + n - 1)
                        pe.wait_ge(s["kt_v"], G * 16 + n - 1)
                    for pair in range(2):
                        for pg in range(4):
                            mm = turn(ps[:, 4 + 2 * (n % 2) + pair, 128 * pg:128 * pg + 128],
                                      c_rows[:, n % 2, pg, 128 * pair:128 * pair + 128])
                    mm.then_inc(s["ck_free"], 1)
                    if n >= 1:
                        scores(n - 1)
                scores(15)
                for b in range(4):
                    for pair in range(2):
                        mm = pe.matmul(ps[:, 4, 0:NS], qc_of(b, pair), z[:, 24 + pair, SEQ:NT],
                                       start=b == 0 and pair == 0, stop=b == 3 and pair == 1)
                mm.then_inc(s["csn"], 1)
                pe.wait_ge(s["comb"], G + 1)
                for blk in range(16):
                    pe.matmul(ps[:, blk // 8, 64 * (blk % 8):64 * (blk % 8) + 64], c_s[:, 128 * blk:128 * blk + 128],
                              comb[:, :], start=True, stop=True)
                pe.matmul(ps[0:NS, 2, 0:64], c_s[:, PAST:PAST + NS], comb[:, :], start=True, stop=True).then_inc(s["cpt_mm"], 1)
                pe.wait_ge(s["cpt_sb"], G + 1)
                for n in range(16):
                    b, kc = n // 4, n % 4
                    pe.wait_ge(s[f"cv_in{n % 2}"], (G * 8 + n // 2 + 1) * 64)
                    if kc == 0:
                        for pair in range(2):
                            pe.matmul(ps[:, 4 + pair, 8 * b:8 * b + 8], vtok[0:NS, 4, 256 + 128 * pair:384 + 128 * pair],
                                      c_pt[0:NS, 16, 16 * b + 8 * pair:16 * b + 8 * pair + 8], start=True, stop=False)
                    for pg in range(4):
                        for pair in range(2):
                            mm = pe.matmul(ps[:, 4 + pair, 8 * b:8 * b + 8], cv_rows[:, n % 2, pg, 128 * pair:128 * pair + 128],
                                           c_pt[:, 4 * kc + pg, 16 * b + 8 * pair:16 * b + 8 * pair + 8],
                                           start=False, stop=kc == 3 and pg == 3)
                    mm.then_inc(s["cv_free"], 1)

            def sample_b(l):
                pe.wait_ge(s["bq"], l + 1)

                def scores(b):
                    pe.wait_ge(s["bkt_a"], l * 8 + b + 1)
                    pe.wait_ge(s["bkt_v"], l * 8 + b + 1)
                    for pair in range(2):
                        for i, n in ((0, 512), (1, 384)):
                            mm = pe.matmul(ps[:, i, 0:n], qb_of(b, pair), b_kt[:, b % 2, pair, 512 * i:512 * i + n],
                                           start=b == 0 and pair == 0, stop=b == 7 and pair == 1)
                    mm.then_inc(s["bs_mm"], 1)

                for b in range(NB_S):
                    pe.wait_ge(s[f"bk_in{b % 2}"], (l * 4 + b // 2 + 1) * 80)
                    if b >= 1:
                        pe.wait_ge(s["bkt_a"], l * 8 + b)
                        pe.wait_ge(s["bkt_v"], l * 8 + b)
                    for pair in range(2):
                        for blk in range(7):
                            at = 2048 + 1024 * pair + 128 * blk
                            mm = turn(flat[:, at:at + 128], b_rows[:, b % 2, blk, 128 * pair:128 * pair + 128])
                    mm.then_inc(s["bk_free"], 1)
                    if b >= 1:
                        scores(b - 1)
                scores(7)
                for b in range(NB_S):
                    for pair in range(2):
                        mm = pe.matmul(ps[:, 2, 0:NS], qb_of(b, pair), z[:, 18 + pair, SEQ:NT],
                                       start=b == 0 and pair == 0, stop=b == 7 and pair == 1)
                mm.then_inc(s["bsn"], 1)
                pe.wait_ge(s["bp"], l + 1)
                for blk in range(7):
                    turn(flat[:, 128 * blk:128 * blk + 128], b_s[:, 128 * blk:128 * blk + 128])
                turn(ps[0:NS, 2, 0:128], b_s[:, KEYS_B:KEYS_B + NS]).then_inc(s["bpt_mm"], 1)
                pe.wait_ge(s["bpt_sb"], l + 1)
                for b in range(NB_S):
                    pe.wait_ge(s[f"bv_in{b % 2}"], (l * 4 + b // 2 + 1) * 80)
                    for pair in range(2):
                        pe.matmul(ps[:, 4 + pair, 8 * b:8 * b + 8], vtok[0:NS, 4, 128 * pair:128 * pair + 128],
                                  b_pt[0:NS, 7, 16 * b + 8 * pair:16 * b + 8 * pair + 8], start=True, stop=False)
                        for blk in range(7):
                            mm = pe.matmul(ps[:, 4 + pair, 8 * b:8 * b + 8], b_rows[:, b % 2, blk, 128 * pair:128 * pair + 128],
                                           b_pt[:, blk, 16 * b + 8 * pair:16 * b + 8 * pair + 8],
                                           start=False, stop=blk == 6)
                    mm.then_inc(s["bv_free"], 1)

            def prompt(l):
                def scores(u):
                    if u >= 2:
                        pe.wait_ge(s["p_max"], l * 32 + u - 1)
                    for mp in range(maps(u)):
                        tq, tk, lo, n = qk_of(u, mp)
                        q0, wid = 128 * (u % 4), 128 * (u % 4 + 1)
                        mm = pe.matmul(ps[:, 2 * (u % 2) + mp, 0:wid], z[lo:lo + n, tq, q0:q0 + 128], z[lo:lo + n, tk, 0:wid],
                                       start=True, stop=True)
                    mm.then_inc(s["p_mm"], 1)

                def turned(u):
                    pe.wait_ge(s["p_soft"], l * 32 + u + 1)
                    if u >= 2:
                        pe.wait_ge(s["ppt_sb"], l * 32 + u - 1)
                    for kb in range(u % 4 + 1):
                        mm = turn(ps[:, 4 + u % 2, 128 * kb:128 * kb + 128], p_s[:, u % 2, 0, 128 * kb:128 * kb + 128])
                    mm.then_inc(s["ppt_mm"], 1)

                def values(u):
                    pe.wait_ge(s["ppt_sb"], l * 32 + u + 1)
                    if u >= 2:
                        pe.wait_ge(s["p_out"], l * 32 + u - 1)
                    v0 = 128 * (u // 8)
                    for kb in range(u % 4 + 1):
                        mm = pe.matmul(ps[:, 6 + u % 2, 0:128], vtok[:, kb, v0:v0 + 128], p_pt[:, u % 2, kb, :],
                                       start=kb == 0, stop=kb == u % 4)
                    mm.then_inc(s["po_mm"], 1)

                pe.wait_ge(s["b_out"], l + 1)
                for u in range(32 + 2):
                    if u < 32:
                        scores(u)
                    if 1 <= u < 33:
                        turned(u - 1)
                    if u >= 2:
                        values(u - 2)

            def w_out(l):
                pe.wait_ge(s["gdone"], l * 14 + 16)
                for o in range(8):
                    slot = o // 2 % 2
                    pe.wait_ge(s[f"w_loaded{slot}"], (l * 47 + 26 + o // 4 + 1) * 32)
                    if o >= 4:
                        pe.wait_ge(s["x_out"], l * 8 + o - 3)
                    for k in range(KD):
                        at = 256 * k + 128 * (o % 2)
                        for h in range(2):
                            mm = pe.matmul(half(2 * (o % 4), h), wslot[:, slot, at:at + 128],
                                           hT[:, k, h * HALF:(h + 1) * HALF], start=k == 0, stop=k == KD - 1)
                    mm.then_inc(s["out_done"], 1)

            with pe.Fori(0, DEPTH) as l:
                pe.wait_ge(s["layer_vecs"], l + 1)
                norm(l * 3)
                ffn(l, 0)
                norm(l * 3 + 1)
                project(l)
                for base in (0, 4):
                    with pe.Fori(0, 2) as j:
                        for u in range(2):
                            square_sums(l * 14 + base + j * 2, u, C("ones"), sq)
                with pe.Fori(0, 4) as c:
                    chunk(l, c)
                sample_chunk(l)
                with pe.Fori(0, 2) as j:
                    for u in range(2):
                        square_sums(l * 14 + 8 + j * 2, u, C("ones"), sq2)
                with pe.Fori(0, 2) as g:
                    group_c(l, g)
                sample_b(l)
                prompt(l)
                for u in range(2):
                    square_sums(l * 14 + 12, u, C("blk64"), sq2)
                w_out(l)
                norm(l * 3 + 2)
                ffn(l, 1)
            norm(6)
            pe.wait_ge(s["h_done"], 56)
            for b in range(5):
                n = 128 if b < 4 else NS
                if b >= 2:
                    pe.wait_ge(s["y_rows"], b - 1)
                for k in range(KD):
                    at = 1024 * (b % 2) + 128 * k
                    mm = turn(flat[0:n, at:at + 128], hT[:, k, 128 * b:128 * b + n])
                mm.then_inc(s["y_mm"], 1)

        @block.scalar
        def _(act):
            for name in ("gsqrt", "conv_done", "proj_a"):
                act.sem_inc(s[name], 2)
            eps, one = C("eps"), C("one")

            def copy(out, in_, scale=1.0):
                return act.activation(out, in_, ACT.Copy, scale=scale)

            act.wait_ge(s["in_lam"], 16 * 8)
            act.wait_ge(s["in_const"], 16)
            act.activation(a_log_c, a_log_c, ACT.Exp)
            act.wait_ge(s["lam_sums"], 1)
            act.activation(lam_sum, lam_sum, ACT.Exp).then_inc(s["lam_exp"], 1)

            def norm(n):
                act.wait_ge(s["x_new"], n + 1)
                for k in range(KD):
                    act.activation(hT[:, k, :], xT[:, k, :], ACT.Square).then_inc(s["sq_done"], 1)
                act.wait_ge(s["ssq_done"], n + 1)
                act.activation(tok(gated[:, 0, :]), both(0), ACT.Sqrt, bias=eps, scale=1.0 / D).then_inc(s["rms"], 1)

            def ffn(l, w):
                it = l * 2 + w
                with act.Fori(0, 11) as j:
                    for slot in range(2):
                        act.wait_ge(s["gu_done"], it * 22 + j * 2 + slot + 1)
                        act.wait_ge(s["gu_free"], it * 22 + j * 2 + slot + 1)
                        act.activation(tok(gated[:, slot, :]), both(4 * slot), ACT.Silu).then_inc(s["silu"], 1)

            def project(l):
                with act.Fori(0, 7) as j:
                    for slot in range(2):
                        act.wait_ge(s["proj_done"], l * 28 + j * 4 + slot * 2 + 1)
                        dst = z[:, ds(j * 4 + slot * 2, 1), :].rearrange("p a (h n) -> p (a h) n", h=2)
                        copy(dst, both(4 * slot)).then_inc(s["proj_a"], 1)
                act.wait_ge(s["ba_sb"], l + 1)
                act.activation(beta[:, :, :], ba[:, :, 0:4], ACT.Sigmoid)
                act.activation(spa[:, :, :], spa[:, :, :], ACT.Exp)
                act.drain()
                act.activation(spa[:, :, :], spa[:, :, :], ACT.Ln, bias=one).then_inc(s["soft"], 1)
                for b in range(5):
                    n = 128 if b < 4 else NS
                    act.wait_ge(s["rows_mm"], l * 5 + b + 1)
                    a = 3 + 2 * (b % 2)
                    copy(k_rows[0:n, b, 256:512], ps[0:n, a, 0:256])
                    copy(vtok[0:n, b, 256:512], ps[0:n, a, 256:512]).then_inc(s["rows_v"], 1)
                act.wait_ge(s["conv_rows_mm"], l + 1)
                copy(conv_out[0:27, :], flat[0:27, 2560:2560 + CONV_CH]).then_inc(s["conv_rows"], 1)
                with act.Fori(0, 6) as j:
                    for u in range(2):
                        act.wait_ge(s["conv_acc"], l * 12 + j * 2 + u + 1)
                        dst = z[:, ds(j * 2 + u, 1), :].rearrange("p a n -> p (a n)")
                        act.activation(dst, cvt[:, u, :], ACT.Silu).then_inc(s["conv_done"], 1)

            def squares(base, src, sqb, rnb, scale):
                for u in range(2):
                    act.wait_ge(s["gmm"], base + u + 1)
                    act.activation(sqb[:, u, :], src(u), ACT.Square).then_inc(s["gsq"], 1)
                for u in range(2):
                    act.wait_ge(s["gmm"], base + u + 3)
                    act.wait_ge(s["gdone"], base + u + 1)
                    act.activation(tok(rnb[:, u, :]), both(2 * u), ACT.Sqrt, bias=eps, scale=scale).then_inc(s["gsqrt"], 1)

            def tile_of(v, i):
                return v[:, ds(i, 1), :].rearrange("p a n -> p (a n)")

            def chunk(l, c):
                it = l * 4 + c
                act.wait_ge(s["state_done"], l * 5 + c + 1)
                for i, name in enumerate(("qc", "kc", "vc")):
                    last = copy(m[name][:, :, :], z[:, 4 * i:4 * i + 4, ds(c * 128, 128)])
                last.then_inc(s["staged"], 1)
                act.wait_ge(s["dt_arg"], it + 1)
                act.activation(m["DT"][:, :, :], m["DT"][:, :, :], ACT.Exp)
                act.activation(m["eG"][:, :, :], ps[:, 2, :].rearrange("p (h n) -> p h n", h=4), ACT.Exp)
                act.activation(ecol[:, :], gc[:, :], ACT.Exp)
                act.activation(kde[:, :], kde[:, :], ACT.Exp).then_inc(s["exp_done"], 1)
                act.wait_ge(s["bege"], it + 1)
                act.wait_ge(s["tokm"], it + 1)
                for h in range(NH):
                    hs = slice(128 * h, 128 * h + 128)
                    copy(m["KB"][:, h, :], ps[:, 0, hs], bege[:, h:h + 1])
                    copy(m["KD"][:, h, :], ps[:, 0, hs], kde[:, h:h + 1])
                    last = copy(m["VB"][:, h, :], ps[:, 1, hs], m["bB"][:, h, 0:1])
                last.then_inc(s["kv_done"], 1)
                with act.Fori(1, 7) as k:
                    act.wait_ge(s["m_mm"], it * 6 + k)
                    copy(m["M"][:, :, :], ps[:, 7, :].rearrange("p (h n) -> p h n", h=4)).then_inc(s["m_sb"], 1)
                act.wait_ge(s["w_mm"], it + 1)
                copy(m["nW"][:, :, :], ps[:, 7, :].rearrange("p (h n) -> p h n", h=4), -1.0).then_inc(s["nw_sb"], 1)
                act.wait_ge(s["o_mm"], it + 1)
                copy(hT[:, 0:4, ds(c * 128, 128)], ps[:, 3, :].rearrange("p (h n) -> p h n", h=4))

            def sample_chunk(l):
                act.wait_ge(s["state_done"], l * 5 + 5)
                for i, name in enumerate(("qc", "kc", "vc")):
                    last = copy(t[name][:, :, :], z[:, 4 * i:4 * i + 4, SEQ:NT])
                last.then_inc(s["x_act"], 1)
                act.wait_ge(s["x_dt"], l + 1)
                act.activation(t["DT"][0:NS], t["DT"][0:NS], ACT.Exp)
                act.activation(t["eG"][:, :, :], ps[:, 2, 0:128].rearrange("p (h n) -> p h n", h=4), ACT.Exp)
                act.activation(secol[0:NS, :], sgc[0:NS, :], ACT.Exp)
                act.activation(skde[0:NS, :], skde[0:NS, :], ACT.Exp).then_inc(s["x_act"], 1)
                act.wait_ge(s["x_bege"], l + 1)
                for h in range(NH):
                    hs = slice(128 * h, 128 * h + 128)
                    copy(t["KB"][0:NS, h, :], ps[0:NS, 0, hs], sbege[0:NS, h:h + 1])
                    copy(t["KD"][0:NS, h, :], ps[0:NS, 0, hs], skde[0:NS, h:h + 1])
                    last = copy(t["VB"][0:NS, h, :], ps[0:NS, 1, hs], t["bB"][0:NS, h, 0:1])
                last.then_inc(s["x_act"], 1)
                act.wait_ge(s["x_m"], l + 1)
                copy(t["M"][0:NS], ps[0:NS, 7, 0:128].rearrange("p (h n) -> p h n", h=4)).then_inc(s["x_act"], 1)
                act.wait_ge(s["x_w"], l + 1)
                copy(t["WQ"][:, :, :, 0:4], ps[:, 7, 0:128].rearrange("p (h b t) -> p h b t", h=4, b=8)).then_inc(s["x_act"], 1)

            def group_c(l, g):
                G = l * 2 + g
                for n in range(16):
                    act.wait_ge(s["ck_free"], G * 16 + n + 3)
                    act.wait_ge(s["cs_mm"], G * 16 + n + 1)
                    copy(c_kt[:, n % 2, 0, :], ps[:, 4 + 2 * (n % 2), :]).then_inc(s["kt_a"], 1)
                act.wait_ge(s["c_max"], G + 1)
                act.activation(c_s[:, :], c_s[:, :], ACT.Exp, bias=c_mx[:, 1:2], accum_out=c_mx[:, 2:3]).then_inc(s["c_exp"], 1)
                act.wait_ge(s["cpt_mm"], G + 1)
                copy(c_pt[:, 0:16, :], flat[:, 0:1024].rearrange("p (k n) -> p k n", k=16))
                copy(c_pt[0:NS, 16, :], ps[0:NS, 2, 0:64]).then_inc(s["cpt_sb"], 1)

            def sample_b(l):
                for b in range(NB_S):
                    act.wait_ge(s["bk_free"], l * 8 + b + 3)
                    act.wait_ge(s["bs_mm"], l * 8 + b + 1)
                    copy(b_kt[:, b % 2, 0, :], flat[:, 2048:2048 + KEYS_B]).then_inc(s["bkt_a"], 1)
                act.wait_ge(s["b_max"], l + 1)
                act.activation(b_s[:, :], b_s[:, :], ACT.Exp, bias=c_mx[:, 1:2], accum_out=c_mx[:, 2:3]).then_inc(s["b_exp"], 1)
                act.wait_ge(s["bpt_mm"], l + 1)
                copy(b_pt[:, 0:7, :], flat[:, 0:KEYS_B].rearrange("p (k n) -> p k n", k=7))
                copy(b_pt[0:NS, 7, :], ps[0:NS, 2, 0:128]).then_inc(s["bpt_sb"], 1)

            def prompt(l):
                for u in range(33):
                    if u < 32:
                        wid = 128 * (u % 4 + 1)
                        act.wait_ge(s["p_max"], l * 32 + u + 1)
                        for mp in range(maps(u)):
                            row = p_s[:, u % 2, mp, 0:wid]
                            last = act.activation(row, row, ACT.Exp, bias=p_mx[:, u % 2, 2 + mp:3 + mp],
                                                  accum_out=p_mx[:, u % 2, 4 + mp:5 + mp])
                        last.then_inc(s["p_exp"], 1)
                    if u >= 1:
                        v = u - 1
                        n = v % 4 + 1
                        act.wait_ge(s["ppt_mm"], l * 32 + v + 1)
                        if v >= 2:
                            act.wait_ge(s["po_mm"], l * 32 + v - 1)
                        copy(p_pt[:, v % 2, 0:n, :], ps[:, 4 + v % 2, 0:128 * n].rearrange("p (k n) -> p k n", k=n))\
                            .then_inc(s["ppt_sb"], 1)

            with act.Fori(0, DEPTH) as l:
                norm(l * 3)
                ffn(l, 0)
                norm(l * 3 + 1)
                project(l)
                for base in (0, 4):
                    with act.Fori(0, 2) as j:
                        act.drain()
                        squares(l * 14 + base + j * 2, lambda u: tile_of(z, j * 2 + base + u), sq, rn, 1.0)
                act.wait_ge(s["gdone"], l * 14 + 10)
                act.wait_ge(s["rows_out"], l * 160 + 160)
                with act.Fori(0, 4) as c:
                    chunk(l, c)
                sample_chunk(l)
                act.activation(z[:, 12:16, :], z[:, 12:16, :], ACT.Silu)
                act.wait_ge(s["x_so"], l + 1)
                act.wait_ge(s["st_out"], l * 64 + 64)
                alone(act)
                act.drain()
                with act.Fori(0, 2) as j:
                    squares(l * 14 + 8 + j * 2, lambda u: tile_of(hT, j * 2 + u), sq2, rn2, 1.0 / DK)
                with act.Fori(0, 2) as g:
                    group_c(l, g)
                sample_b(l)
                prompt(l)
                act.wait_ge(s["p_out"], l * 32 + 32)
                squares(l * 14 + 12, lambda u: hT[:, 6 + u, :], sq2, rn2, 1.0 / 64)
                norm(l * 3 + 2)
                ffn(l, 1)
            norm(6)

        @block.vector
        def _(dve):
            for name in ("gu_free", "down_free", "proj_v", "gdone"):
                dve.sem_inc(s[name], 2)
            cp = dve.tensor_copy
            stt = dve.scalar_tensor_tensor

            dve.memset(small[:, 32:160], 0.0)
            dve.drain()
            dve.wait_ge(s["in_const"], 16)
            dve.wait_ge(s["in_lam"], 16 * 8)
            for i in range(2):
                dve.tensor_tensor(lam_prod[:, i, :], lam_rows[:, 2 * i, :], lam_rows[:, 2 * i + 1, :], ALU.mult)
            dve.drain()
            for i in range(2):
                for l in range(DEPTH):
                    last = dve.reduce_sum(small[:, 16 + 2 * i + l:17 + 2 * i + l], lam_prod[:, i, 32 * l:32 * l + 32], AX)
            last.then_inc(s["lam_sums"], 1)
            dve.wait_ge(s["lam_exp"], 1)
            dve.tensor_tensor(lam_all, lam_sum[:, 0:2], lam_sum[:, 2:4], ALU.subtract)
            dve.drain()
            dve.tensor_tensor(lam_all, lam_all, C("lam0"), ALU.add)
            for i in range(1, 6):
                n = 128 if i < 5 else NS
                dve.wait_ge(s["setup_mm"], i)
                at = 1024 * (i % 2)
                cp(xT[:, :, 128 * (i - 1):128 * (i - 1) + n],
                   flat[:, at:at + 8 * n].rearrange("p (k n) -> p k n", k=KD)).then_inc(s["setup_ev"], 1)
            dve.drain().then_inc(s["x_new"], 1)
            dve.wait_ge(s["setup_mm"], 6)
            cp(cols_conv[:, :], ps[:, 0, 0:96])
            cp(cols_norm[:, :], ps[:, 0, 96:156]).then_inc(s["setup_ev"], 1)
            for c in range(5):
                i, n = 7 + c, min(512, U_TAB - 512 * c)
                dve.wait_ge(s["setup_mm"], i)
                cp(table[0:8, 512 * c:512 * c + n], ps[0:8, 2 * (i % 2), 0:n]).then_inc(s["setup_ev"], 1)
            for h in range(8):
                i = 12 + h
                dve.wait_ge(s["setup_mm"], i)
                cp(strips[:, h, :], ps[:, 2 * (i % 2), :]).then_inc(s["setup_ev"], 1)
            dve.wait_ge(s["in_rows"], 16 * 5 * T_S)
            for g in range(2):
                dve.tensor_tensor(bias_cn[:, g, :].rearrange("p (b t) -> p b t", b=8), per_head(bias_c[:, PAST:PAST + T_S], 8),
                                  over(C("offc")[:, 8 * g:8 * g + 8], T_S), ALU.add)
            dve.tensor_tensor(bias_bn[:, :].rearrange("p (b t) -> p b t", b=8), per_head(win_b[:, PAST:PAST + T_S], 8),
                              over(C("offb"), T_S), ALU.add)
            cp(bias_b[:, 0:384].rearrange("p (q r a) -> p q r a", q=3, r=4),
               win_b[:, 0:1536].rearrange("p (q a r) -> p q r a", q=3, a=32)[:, :, 0:4, :])
            cp(bias_b[:, 384:KEYS_B], win_b[:, 1536:PAST])
            dve.drain()

            def norm(n, gains):
                dve.wait_ge(s["rms"], n + 1)
                rstd = gated[:, 0, :]
                dve.reciprocal(rstd, rstd)
                dve.drain()
                for k in range(KD):
                    stt(hT[:, k, :], xT[:, k, :], gains[:, k:k + 1], rstd, ALU.mult, ALU.mult).then_inc(s["h_done"], 1)

            def ffn(l, w):
                it = l * 2 + w
                with dve.Fori(0, 11) as j:
                    for slot in range(2):
                        dve.wait_ge(s["silu"], it * 22 + j * 2 + slot + 1)
                        dst = hidden[:, ds(j * 2 + slot, 1), :].rearrange("p a (h n) -> p (a h) n", h=2)
                        dve.tensor_tensor(dst, tok(gated[:, slot, :]), both(4 * slot + 2), ALU.mult).then_inc(s["gu_free"], 1)
                with dve.Fori(0, 4) as j:
                    for u in range(2):
                        dve.wait_ge(s["down_done"], it * 8 + j * 2 + u + 2)
                        x = xT[:, ds(j * 2 + u, 1), :].rearrange("p a (h n) -> p (a h) n", h=2)
                        stt(x, both(4 * u), 0.5, x, ALU.mult, ALU.add).then_inc(s["down_free"], 1)
                dve.drain().then_inc(s["x_new"], 1)

            def project(l):
                with dve.Fori(0, 7) as j:
                    for slot in range(2):
                        dve.wait_ge(s["proj_done"], l * 28 + j * 4 + slot * 2 + 2)
                        dst = z[:, ds(j * 4 + slot * 2 + 1, 1), :].rearrange("p a (h n) -> p (a h) n", h=2)
                        cp(dst, both(4 * slot + 2)).then_inc(s["proj_v"], 1)
                dve.wait_ge(s["ba_mm"], l + 1)
                cp(ba[:, 0:4, :], ps[:, 0, 0:32].rearrange("p (b n) -> p b n", b=4))
                cp(ba[0:NS, 4, :], ps[0:NS, 0, 32:40])
                dve.drain()
                dve.tensor_tensor(spb[:, :, :], ba[:, :, 4:8], per_head(dtb, 5), ALU.add)
                dve.drain()
                stt(spa[:, :, :], spb[:, :, :], -1.0, spb[:, :, :], ALU.mult, ALU.min).then_inc(s["ba_sb"], 1)
                dve.wait_ge(s["proj_a"], l * 14 + 16)
                cp(conv_tail[:, :, 0:3], z[:, 0:12, SEQ - 3:SEQ])
                cp(conv_tail[:, :, 3:27].rearrange("p c (b j) -> p c b j", b=8),
                   z[:, 0:12, SEQ:NT].rearrange("p c (b t) -> p c b t", b=8)[:, :, :, 1:4]).then_inc(s["conv_tail"], 1)
                cp(xs[:, :, :, 3:7], z[:, 0:12, SEQ:NT].rearrange("p c (b t) -> p c b t", b=8))
                for b in range(5):
                    n = 128 if b < 4 else NS
                    dve.wait_ge(s["rows_mm"], l * 5 + b + 1)
                    a = 2 + 2 * (b % 2)
                    cp(k_rows[0:n, b, 0:256], ps[0:n, a, 0:256])
                    cp(vtok[0:n, b, 0:256], ps[0:n, a, 256:512]).then_inc(s["rows_a"], 1)
                dve.wait_ge(s["soft"], l + 1)
                stt(spb[:, :, :], spb[:, :, :], 0.0, spa[:, :, :], ALU.max, ALU.add)
                dve.drain()
                stt(gdec[:, :, :], spb[:, :, :], -1.0, per_head(ea, 5), ALU.mult, ALU.mult)
                dve.wait_ge(s["conv_in_mm"], l + 1)
                cp(xs[:, :, :, 0:3], ps[:, 1, 0:288].rearrange("p (c b j) -> p c b j", c=12, b=8))
                dve.drain()
                with dve.Fori(0, 6) as j:
                    for u in range(2):
                        c = j * 2 + u
                        acc = cvt[:, u, :]
                        acc_s = acc[:, SEQ:NT].rearrange("p (b t) -> p b t", b=8)
                        zc = z[:, ds(c, 1), :].rearrange("p a n -> p (a n)")
                        xc = xs[:, ds(c, 1), :, :].rearrange("p a b t -> p (a b) t")
                        dve.wait_ge(s["conv_done"], l * 12 + j * 2 + u + 1)
                        for tap in (3, 2, 1, 0):
                            cw = lay_conv[:, ds(c + 12 * tap, 1)]
                            d = 3 - tap
                            if tap == 3:
                                dve.tensor_scalar(acc[:, 0:SEQ], zc[:, 0:SEQ], cw, None, ALU.mult)
                                last = dve.tensor_scalar(acc_s, xc[:, :, 3:7], cw, None, ALU.mult)
                            else:
                                dve.drain()
                                stt(acc[:, d:SEQ], zc[:, 0:SEQ - d], cw, acc[:, d:SEQ], ALU.mult, ALU.add)
                                last = stt(acc_s, xc[:, :, tap:tap + 4], cw, acc_s, ALU.mult, ALU.add)
                        last.then_inc(s["conv_acc"], 1)

            def inverse_root(base, u, rnb):
                dve.wait_ge(s["gsqrt"], base + u + 3)
                dve.reciprocal(rnb[:, u, :], rnb[:, u, :])
                dve.drain()

            def tile_of(v, i):
                return v[:, ds(i, 1), :].rearrange("p a n -> p (a n)")

            def four(bank, n=128):
                return ps[:, bank, 0:4 * n].rearrange("p (h n) -> p h n", h=4)

            def chunk(l, c):
                it = l * 4 + c
                cp(m["gB"][:, :, :], over(gdec[:, ds(c, 1), :].rearrange("p a h -> p (a h)"), 128))
                cp(m["bB"][:, :, :], over(beta[:, ds(c, 1), :].rearrange("p a h -> p (a h)"), 128)).then_inc(s["gb"], 1)
                dve.wait_ge(s["decay_mm"], it + 1)
                cp(gc[:, :], ps[:, 4, 0:4])
                dve.drain()
                for h in range(NH):
                    stt(m["DT"][:, h, :], ps[:, 2, 128 * h:128 * h + 128], gc[:, h:h + 1], C("neg"), ALU.subtract, ALU.add)
                dve.tensor_tensor(kde[:, :], four(2)[:, :, 127], gc[:, :], ALU.subtract).then_inc(s["dt_arg"], 1)
                dve.wait_ge(s["exp_done"], it + 1)
                dve.tensor_tensor(bege[:, :], m["bB"][:, :, 0], ecol[:, :], ALU.mult).then_inc(s["bege"], 1)
                dve.wait_ge(s["kkqk"], it + 1)
                dve.tensor_tensor(m["LT"][:, :, :], m["DT"][:, :, :], four(5), ALU.mult)
                dve.tensor_tensor(m["QKT"][:, :, :], m["DT"][:, :, :], four(6), ALU.mult)
                dve.tensor_tensor(m["qc"][:, :, :], m["qc"][:, :, :], m["eG"][:, :, :], ALU.mult)
                dve.drain()
                dve.tensor_tensor(m["LT"][:, :, :], m["LT"][:, :, :], four(3), ALU.mult)
                dve.drain()
                dve.tensor_tensor(m["LK"][:, :, :], m["LT"][:, :, :], per_head(C("lm")[:, 0:128]), ALU.mult)
                dve.drain()
                dve.tensor_tensor(m["U"][:, :, :], per_head(C("ident")), m["LK"][:, :, :], ALU.subtract).then_inc(s["u_done"], 1)
                with dve.Fori(1, 7) as k:
                    lmk = C("lm")[:, ds(k * 128, 128)]
                    dve.drain()
                    dve.tensor_tensor(m["LK"][:, :, :], m["LT"][:, :, :], per_head(lmk), ALU.mult)
                    dve.wait_ge(s["t_mm"], it * 6 + k)
                    cp(m["T"][:, :, :], four(6)).then_inc(s["lt_done"], 1)
                    dve.wait_ge(s["mu_mm"], it * 6 + k)
                    dve.tensor_tensor(m["U"][:, :, :], m["U"][:, :, :], four(5), ALU.subtract).then_inc(s["u_done"], 1)
                dve.wait_ge(s["vn_mm"], it + 1)
                cp(m["VN"][:, :, :], four(2)).then_inc(s["vn_sb"], 1)
                dve.wait_ge(s["s_mm"], it + 1)
                for h in range(NH):
                    last = stt(m["S"][:, h, :], m["S"][:, h, :], m["eG"][:, h, 127:128], ps[:, 4, 128 * h:128 * h + 128],
                               ALU.mult, ALU.add)
                last.then_inc(s["state_done"], 1)

            def sample_chunk(l):
                q = slice(0, NS)

                def four_s(bank):
                    return ps[0:NS, bank, 0:128].rearrange("p (h n) -> p h n", h=4)

                cp(t["gB"][q], over(gdec[q, 4, :], 128))
                cp(t["bB"][q], over(beta[q, 4, :], NS)).then_inc(s["x_gb"], 1)
                dve.wait_ge(s["x_decay"], l + 1)
                cp(sgc[q, :], ps[q, 4, 0:4])
                dve.drain()
                for h in range(NH):
                    stt(t["DT"][q, h, :], ps[q, 2, NS * h:NS * h + NS], sgc[q, h:h + 1], C("neg4", NS), ALU.subtract, ALU.add)
                dve.tensor_tensor(skde[q, :], ps[q, 4, 4:8], sgc[q, :], ALU.subtract).then_inc(s["x_dt"], 1)
                dve.wait_ge(s["x_act"], l * 5 + 2)
                dve.tensor_tensor(sbege[q, :], t["bB"][q, :, 0], secol[q, :], ALU.mult).then_inc(s["x_bege"], 1)
                dve.wait_ge(s["x_kkqk"], l + 1)
                dve.tensor_tensor(t["LT"][q], t["DT"][q], four_s(5), ALU.mult)
                dve.tensor_tensor(t["QKT"][q], t["DT"][q], four_s(6), ALU.mult)
                dve.drain()
                dve.tensor_tensor(t["LT"][q], t["LT"][q], four_s(3), ALU.mult)
                dve.drain()
                dve.tensor_tensor(t["LK"][q], t["LT"][q], per_head(C("lm", NS)[:, 0:NS]), ALU.mult)
                dve.drain()
                dve.tensor_tensor(t["U"][q], per_head(C("ident", NS)[:, 0:NS]), t["LK"][q], ALU.subtract).then_inc(s["x_u"], 1)
                dve.drain()
                dve.tensor_tensor(t["LK"][q], t["LT"][q], per_head(C("lm", NS)[:, 128:128 + NS]), ALU.mult)
                dve.wait_ge(s["x_t"], l + 1)
                cp(t["T"][q], four_s(6)).then_inc(s["x_lt"], 1)
                dve.wait_ge(s["x_mu"], l + 1)
                dve.tensor_tensor(t["U"][q], t["U"][q], four_s(5), ALU.subtract).then_inc(s["x_u"], 1)
                dve.tensor_tensor(t["WQ"][:, :, :, 4:8], t["qc"][:, :, :].rearrange("p h (b t) -> p h b t", b=8),
                                  t["eG"][:, :, :].rearrange("p h (b t) -> p h b t", b=8), ALU.mult).then_inc(s["x_qe"], 1)
                dve.wait_ge(s["x_ws"], l + 1)
                wsq = ps[:, 2, 0:256].rearrange("p (h b u) -> p h b u", h=4, b=8)
                cp(t["QS"][:, :, :].rearrange("p h (b t) -> p h b t", b=8), wsq[:, :, :, 4:8])
                dve.tensor_scalar(t["nW"][:, :, :].rearrange("p h (b t) -> p h b t", b=8), wsq[:, :, :, 0:4], -1.0, None,
                                  ALU.mult).then_inc(s["x_nw"], 1)
                for h in range(NH):
                    last = t["eG"][:, h, :].rearrange("p (b t) -> p b t", b=8)[:, :, 3]
                    dve.tensor_tensor(t["st"][:, h], t["st"][:, h], over(last, 128), ALU.mult)
                dve.wait_ge(s["x_vn"], l + 1)
                cp(t["VN"][q], ps[q, 3, :].rearrange("p (h n) -> p h n", h=4)).then_inc(s["x_vnsb"], 1)
                dve.wait_ge(s["x_o"], l + 1)
                dve.tensor_tensor(hT[:, 0:4, SEQ:NT], t["QS"][:, :, :], four(4, NS), ALU.add).then_inc(s["x_so"], 1)
                dve.drain()
                for h in range(NH):
                    if h >= 2:
                        dve.wait_ge(s["x_s"], l * 4 + h - 1)
                    dve.tensor_tensor(vblk[h % 2][q], per_head(t["VN"][q, h, :], 8), over(C("bsel", NS), 128),
                                      ALU.mult).then_inc(s["x_vb"], 1)
                    if h >= 1:
                        add_state(l, h - 1)
                add_state(l, 3)
                dve.wait_ge(s["delta_out"], l * 16 + 16)
                alone(dve)

            def add_state(l, h):
                dve.wait_ge(s["x_s"], l * 4 + h + 1)
                at = 3072 if h % 2 else 0
                dve.tensor_tensor(t["st"][:, h], t["st"][:, h], flat[:, at:at + 1024].rearrange("p (b v) -> p b v", b=8),
                                  ALU.add).then_inc(s["st_new"], 1)

            def group_c(l, g):
                G = l * 2 + g
                scale = 32 ** -0.5
                for pair in range(2):
                    for quad in range(4):
                        h2, mp = quad // 2, quad % 2
                        rows = slice(32 * quad, 32 * quad + 32)
                        off = 128 * pair + (2 * pair + h2) * 8 + mp * 4
                        dst = qc_all.rearrange("p (b x) -> p b x", b=4)[rows, :, off:off + 4]
                        src = z[rows, 22 + pair, ds(g * 16 + SEQ, 16)].rearrange("p (b t) -> p b t", b=4)
                        last = cp(dst, src)
                last.then_inc(s["cq"], 1)
                for n in range(16):
                    dve.wait_ge(s["ck_free"], G * 16 + n + 3)
                    dve.wait_ge(s["cs_mm"], G * 16 + n + 1)
                    cp(c_kt[:, n % 2, 1, :], ps[:, 5 + 2 * (n % 2), :]).then_inc(s["kt_v"], 1)
                dve.wait_ge(s["csn"], G + 1)
                stt(c_s[:, 0:PAST], flat[:, 0:PAST], scale, bias_c[:, 0:PAST], ALU.mult, ALU.add)
                stt(c_s[:, PAST:PAST + NS], ps[:, 4, 0:NS], scale, bias_cn[:, ds(g, 1), :].rearrange("p a n -> p (a n)"),
                    ALU.mult, ALU.add)
                dve.drain()
                dve.reduce_max(c_mx[:, 0:1], c_s[:, :], AX)
                dve.drain()
                dve.tensor_scalar(c_mx[:, 1:2], c_mx[:, 0:1], -1.0, None, ALU.mult).then_inc(s["c_max"], 1)
                dve.wait_ge(s["c_exp"], G + 1)
                dve.reciprocal(c_mx[:, 3:4], c_mx[:, 2:3])
                dve.drain()
                dve.tensor_scalar(comb[:, :], C("comb"), c_mx[:, 3:4], sign, ALU.mult, ALU.mult).then_inc(s["comb"], 1)
                dve.wait_ge(s["cv_free"], G * 16 + 18)
                for pair in range(2):
                    for h2 in range(2):
                        rows = slice(64 * h2, 64 * h2 + 64)
                        dst = hT[rows, 6 + pair, ds(g * 16 + SEQ, 16)].rearrange("p (b t) -> p b t", b=4)
                        src = ps[rows, 4 + pair, 0:32].rearrange("p (b x) -> p b x", b=4)[:, :, 4 * h2:4 * h2 + 4]
                        last = cp(dst, src)
                last.then_inc(s["c_group_done"], 1)

            def sample_b(l):
                scale = 64 ** -0.5
                dve.memset(qb_all, 0.0)
                dve.drain()
                for pair in range(2):
                    for h2 in range(2):
                        rows = slice(64 * h2, 64 * h2 + 64)
                        off = 128 * pair + (2 * pair + h2) * 4
                        dst = qb_all.rearrange("p (b x) -> p b x", b=8)[rows, :, off:off + 4]
                        last = cp(dst, z[rows, 16 + pair, SEQ:NT].rearrange("p (b t) -> p b t", b=8))
                last.then_inc(s["bq"], 1)
                for b in range(NB_S):
                    dve.wait_ge(s["bk_free"], l * 8 + b + 3)
                    dve.wait_ge(s["bs_mm"], l * 8 + b + 1)
                    cp(b_kt[:, b % 2, 1, :], flat[:, 3072:3072 + KEYS_B]).then_inc(s["bkt_v"], 1)
                dve.wait_ge(s["bsn"], l + 1)
                stt(b_s[:, 0:KEYS_B], flat[:, 0:KEYS_B], scale, bias_b[:, :], ALU.mult, ALU.add)
                stt(b_s[:, KEYS_B:KEYS_B + NS], ps[:, 2, 0:NS], scale, bias_bn[:, :], ALU.mult, ALU.add)
                dve.drain()
                dve.reduce_max(c_mx[:, 0:1], b_s[:, :], AX)
                dve.drain()
                dve.tensor_scalar(c_mx[:, 1:2], c_mx[:, 0:1], -1.0, None, ALU.mult).then_inc(s["b_max"], 1)
                dve.wait_ge(s["b_exp"], l + 1)
                dve.reciprocal(c_mx[:, 3:4], c_mx[:, 2:3])
                dve.drain()
                dve.tensor_scalar(b_s[:, :], b_s[:, :], c_mx[:, 3:4], None, ALU.mult).then_inc(s["bp"], 1)
                dve.wait_ge(s["bv_free"], l * 8 + 10)
                for pair in range(2):
                    for h2 in range(2):
                        rows = slice(64 * h2, 64 * h2 + 64)
                        dst = hT[rows, 4 + pair, SEQ:NT].rearrange("p (b t) -> p b t", b=8)
                        src = ps[rows, 4 + pair, 0:64].rearrange("p (b x) -> p b x", b=8)[:, :, 4 * h2:4 * h2 + 4]
                        last = cp(dst, src)
                last.then_inc(s["b_out"], 1)

            def prompt(l):
                def logits(u):
                    par, wid, n = u % 2, 128 * (u % 4 + 1), maps(u)
                    dve.wait_ge(s["p_mm"], l * 32 + u + 1)
                    if u >= 2:
                        dve.wait_ge(s["ppt_mm"], l * 32 + u - 1)
                    scale = (64 if u < 16 else 32) ** -0.5
                    for mp in range(n):
                        stt(p_s[:, par, mp, 0:wid], ps[:, 2 * par + mp, 0:wid], scale, strips[:, u // 4, SEQ - wid:SEQ],
                            ALU.mult, ALU.add)
                    dve.drain()
                    dve.reduce_max(p_mx[:, par, 0:n], p_s[:, par, 0:n, 0:wid], AX)
                    dve.drain()
                    dve.tensor_scalar(p_mx[:, par, 2:2 + n], p_mx[:, par, 0:n], -1.0, None, ALU.mult).then_inc(s["p_max"], 1)

                def weights(u):
                    par, wid, n = u % 2, 128 * (u % 4 + 1), maps(u)
                    dve.wait_ge(s["p_exp"], l * 32 + u + 1)
                    dve.reciprocal(p_mx[:, par, 6:6 + n], p_mx[:, par, 4:4 + n])
                    dve.drain()
                    p0, p1 = p_s[:, par, 0, 0:wid], p_s[:, par, 1, 0:wid]
                    last = dve.tensor_scalar(p0, p0, p_mx[:, par, 6:7], None, ALU.mult)
                    if n == 2:
                        dve.tensor_scalar(p_mx[:, par, 5:6], p_mx[:, par, 7:8], lam, -1.0, ALU.mult, ALU.mult)
                        dve.drain()
                        last = stt(p0, p1, p_mx[:, par, 5:6], p0, ALU.mult, ALU.add)
                    last.then_inc(s["p_soft"], 1)

                def result(u):
                    head = u // 4
                    rows = slice(64 * (head % 2), 64 * (head % 2) + 64)
                    dve.wait_ge(s["po_mm"], l * 32 + u + 1)
                    cp(hT[rows, 4 + head // 2, 128 * (u % 4):128 * (u % 4) + 128], ps[rows, 6 + u % 2, 0:128])\
                        .then_inc(s["p_out"], 1)

                for u in range(34):
                    if u < 32:
                        logits(u)
                    if 1 <= u < 33:
                        weights(u - 1)
                    if u >= 2:
                        result(u - 2)

            with dve.Fori(0, DEPTH) as l:
                cp(lay_conv[:, :], cols_conv[:, ds(l * 48, 48)])
                cp(lay_norm[:, :], cols_norm[:, ds(l * LV, LV)])
                cp(lam, lam_all[:, ds(l, 1)])
                cp(ea, a_log_c[:, ds(l * 4, 4)])
                cp(dtb, dt_c[:, ds(l * 4, 4)])
                cp(lay_ba[:, :, :], all_ba[:, ds(l, 1)].rearrange("p l k n -> p (l k) n"))
                dve.drain()
                dve.tensor_scalar(sign, C("m1"), lam, -1.0, ALU.mult, ALU.mult)
                dve.tensor_tensor(cnorm, lay_norm[:, 25:26], C("oml")[:, ds(l, 1)], ALU.mult)
                dve.drain()
                dve.tensor_tensor(sign, sign, C("m0"), ALU.add).then_inc(s["layer_vecs"], 1)
                norm(l * 3, lay_norm[:, 0:8])
                ffn(l, 0)
                norm(l * 3 + 1, lay_norm[:, 8:16])
                project(l)
                with dve.Fori(0, 2) as j:
                    for u in range(2):
                        inverse_root(l * 14 + j * 2, u, rn)
                        q = tile_of(z, j * 2 + u)
                        stt(q, q, DK ** -0.5, rn[:, u, :], ALU.mult, ALU.mult).then_inc(s["gdone"], 1)
                with dve.Fori(0, 2) as j:
                    for u in range(2):
                        inverse_root(l * 14 + 4 + j * 2, u, rn)
                        k = tile_of(z, j * 2 + u + 4)
                        dve.tensor_tensor(k, k, rn[:, u, :], ALU.mult).then_inc(s["gdone"], 1)
                dve.wait_ge(s["rows_out"], l * 160 + 160)
                alone(dve)
                dve.drain()
                dve.memset(m["S"][:, :, :], 0.0).then_inc(s["state_done"], 1)
                with dve.Fori(0, 4) as c:
                    chunk(l, c)
                sample_chunk(l)
                with dve.Fori(0, 2) as j:
                    for u in range(2):
                        inverse_root(l * 14 + 8 + j * 2, u, rn2)
                        o = tile_of(hT, j * 2 + u)
                        stt(o, o, lay_norm[:, 24:25], rn2[:, u, :], ALU.mult, ALU.mult)
                        dve.drain()
                        dve.tensor_tensor(o, o, tile_of(z, j * 2 + u + 12), ALU.mult).then_inc(s["gdone"], 1)
                dve.memset(qc_all, 0.0)
                dve.drain()
                with dve.Fori(0, 2) as g:
                    group_c(l, g)
                sample_b(l)
                prompt(l)
                for u in range(2):
                    inverse_root(l * 14 + 12, u, rn2)
                    o = hT[:, 6 + u, :]
                    stt(o, o, cnorm, rn2[:, u, :], ALU.mult, ALU.mult).then_inc(s["gdone"], 1)
                for o in range(8):
                    dve.wait_ge(s["out_done"], l * 8 + o + 1)
                    dve.tensor_tensor(tok(xT[:, o, :]), tok(xT[:, o, :]), both(2 * (o % 4)), ALU.add).then_inc(s["x_out"], 1)
                dve.drain().then_inc(s["x_new"], 1)
                norm(l * 3 + 2, lay_norm[:, 16:24])
                ffn(l, 1)
            norm(6, cols_norm[:, 2 * LV:2 * LV + 8])
            for b in range(5):
                n = 128 if b < 4 else NS
                dve.wait_ge(s["y_mm"], b + 1)
                at = 1024 * (b % 2)
                cp(y_rows[0:n, b, :], flat[0:n, at:at + 1024]).then_inc(s["y_rows"], 1)


NAMES = ("x_prompt", "x_sample", "state_delta", "state_conv", "cache_win_k", "cache_win_v", "cache_k", "cache_v",
         "page_table", "w_in", "conv_w", "a_log", "dt_bias", "a_norm_w", "lambda_q1", "lambda_k1", "lambda_q2",
         "lambda_k2", "c_norm_w", "rel_bias", "w_out", "norm_ffn1", "w1_gate", "w1_up", "w1_down", "norm_mix",
         "norm_ffn2", "w2_gate", "w2_up", "w2_down", "final_norm")
OUTS = (("y_p", (1, SEQ, D)), ("y_s", (NB_S, T_S, D)), ("delta_p", (DEPTH, 1, NH, DK, DK)),
        ("delta_s", (DEPTH, NB_S, NH, DK, DK)), ("conv_p", (DEPTH, 1, 3, CONV_CH)), ("conv_s", (DEPTH, NB_S, 3, CONV_CH)),
        ("wk_p", (DEPTH, 1, SEQ, 4, 64)), ("wk_s", (DEPTH, NB_S, T_S, 4, 64)), ("wv_p", (DEPTH, 1, SEQ, 4, 64)),
        ("wv_s", (DEPTH, NB_S, T_S, 4, 64)), ("k_p", (DEPTH, 1, SEQ, 4, 64)), ("k_s", (DEPTH, NB_S, T_S, 4, 64)),
        ("v_p", (DEPTH, 1, SEQ, 4, 64)), ("v_s", (DEPTH, NB_S, T_S, 4, 64)))


def kernel(**inputs):
    import concourse.bacc as bacc
    from concourse.bass_utils import run_bass_kernel_spmd

    nc = bacc.Bacc("TRN2", target_bir_lowering=False, num_devices=1)
    consts, buckets, pick = constant_arrays()
    given = {name: inputs[name] for name in NAMES}
    given.update(consts=consts, buckets=buckets, pick=pick)
    arrays, handles = {}, {}
    for name, value in given.items():
        a = np.ascontiguousarray(value)
        arrays["in_" + name] = a
        handles[name] = nc.dram_tensor("in_" + name, a.shape, mybir.dt.from_np(a.dtype), kind="ExternalInput").ap()
    outs = {name: nc.dram_tensor("out_" + name, shape, F32, kind="ExternalOutput").ap() for name, shape in OUTS}
    scratch = nc.dram_tensor("bias_tables", (8, U_TAB), F32, kind="Internal").ap()
    trunk(nc, handles, outs, scratch)
    r = run_bass_kernel_spmd(nc, [arrays], core_ids=[0])
    return tuple(r.results[0]["out_" + name] for name, _ in OUTS)
```

```python
from contextlib import ExitStack

import numpy as np

import concourse.bass as bass
from concourse import mybir

F32 = mybir.dt.float32
I32 = mybir.dt.int32
U32 = mybir.dt.uint32
ACT = mybir.ActivationFunctionType
ALU = mybir.AluOpType
AX = mybir.AxisListType.X
ds = bass.ds

D, DEPTH, FF, EPS = 1024, 2, 2816, 1e-6
SEQ, NB_S, T_S = 512, 8, 4
NS = NB_S * T_S
NT = SEQ + NS
HALF = NT // 2
KD = D // 128
NF = FF // 128
NH, DK, CONV_CH, CONV_W = 4, 128, 1536, 4
D_IN = 3592
BA_COL, BC_COL = 2048, 2056
NZ = 28
PAST, PAGE, PAGES, POOL_PAGES = 2048, 128, 16, 160
U_TAB = 2304
U_MAX = PAST + T_S - 1
NEG = -1.0e30
RING = 4
KEYS_B = 896
LV = 26


def columns():
    at, where = 0, {}
    for name, n in (("ident", 128), ("ones", 128), ("tri", 128), ("neg", 128), ("blk64", 128), ("flip", 128),
                    ("lm", 7 * 128), ("tri4", 32), ("neg4", 32), ("blk4", 32), ("bsel", 8), ("comb", 64),
                    ("offc", 16), ("offb", 8), ("m0", 1), ("m1", 1), ("eps", 1), ("one", 1), ("lam0", 2), ("oml", 2), ("p32", 1)):
        where[name] = (at, at + n)
        at += n
    return where, at


def constant_arrays():
    where, n = columns()
    c = np.zeros((128, n), np.float32)

    def put(name, a):
        lo, hi = where[name]
        c[:a.shape[0], lo:hi] = a.reshape(a.shape[0], -1)

    p = np.arange(128)
    put("ident", np.eye(128))
    put("ones", np.ones((128, 128)))
    put("tri", (p[:, None] <= p[None, :]).astype(np.float32))
    put("neg", np.where(p[:, None] <= p[None, :], 0.0, NEG))
    put("blk64", (p[:, None] // 64 == p[None, :] // 64).astype(np.float32))
    put("flip", (p[:, None] + p[None, :] == 127).astype(np.float32))
    lm = np.zeros((128, 7, 128), np.float32)
    for k in range(7):
        b = 1 << k
        j, i = p[:, None], p[None, :]
        lm[:, k] = (j // (2 * b) == i // (2 * b)) & ((i // b) % 2 == 1) & ((j // b) % 2 == 0)
    put("lm", lm)
    q = np.arange(NS)
    same = q[:, None] // T_S == q[None, :] // T_S
    put("tri4", (same & (q[:, None] <= q[None, :])).astype(np.float32))
    put("neg4", np.where(same & (q[:, None] <= q[None, :]), 0.0, NEG))
    put("blk4", same.astype(np.float32))
    put("bsel", (q[:, None] // T_S == np.arange(8)[None, :]).astype(np.float32))
    b4, hh, mm, tt = p // 32, p // 8 % 4, p // 4 % 2, p % 4
    r = np.arange(64)
    put("comb", ((b4[:, None] == r[None, :] // 16) & (hh[:, None] == r[None, :] // 4 % 4)
                 & (tt[:, None] == r[None, :] % 4)).astype(np.float32))
    offc = np.zeros((128, 2, 8), np.float32)
    for g in range(2):
        offc[:, g] = np.where(np.arange(8)[None, :] == 4 * g + b4[:, None], 0.0, NEG)
    put("offc", offc)
    put("offb", np.where(np.arange(8)[None, :] == p[:, None] // 16, 0.0, NEG))
    put("m0", (mm == 0).astype(np.float32)[:, None])
    put("m1", (mm == 1).astype(np.float32)[:, None])
    put("eps", np.full((128, 1), EPS))
    put("one", np.ones((128, 1)))
    lam0 = np.array([0.8 - 0.6 * np.exp(-0.3 * l) for l in range(DEPTH)])
    put("lam0", np.tile(lam0, (128, 1)))
    put("oml", np.tile(1.0 - lam0, (128, 1)))
    put("p32", (p % 32)[:, None])
    dist = U_MAX - np.arange(U_TAB)
    dc = np.maximum(dist, 0)
    scaled = np.log(np.maximum(dc, 1).astype(np.float32) / np.float32(16)) / np.float32(np.log(2048 / 16))
    large = np.minimum(16 + (scaled.astype(np.float32) * np.float32(16)).astype(np.int32), 31)
    bucket = np.where(dc < 16, dc, large)
    e = np.zeros((34, U_TAB), np.float32)
    e[bucket, np.arange(U_TAB)] = 1.0
    count = ((dist >= 0) & (dist <= 128)).astype(int) + ((dist >= 0) & (dist <= 512) & (dist % 4 == 0)) \
        + ((dist >= 0) & (dist <= 2048) & (dist % 16 == 0))
    e[32] = np.where(count > 0, np.log(np.maximum(count, 1)), NEG)
    e[33] = np.where(dist >= 0, 0.0, NEG)
    pick = np.zeros((2, 8), np.float32)
    pick[0, :4] = 1.0
    pick[1, 4:] = 1.0
    return c, e, pick


SIGNALS = (
    "b_exp", "b_max", "b_out", "b_pv", "b_pv_mm", "ba_mm", "ba_sb", "bege", "bk_free", "bk_in0", "bk_in1",
    "bkt_a", "bkt_v", "bp", "bpt_mm", "bpt_sb", "bq", "bs_mm", "bsn", "bv_free", "bv_in0", "bv_in1", "c_exp",
    "c_group_done", "c_max", "c_pv", "c_pv_mm", "ck_free", "ck_in0", "ck_in1", "ck_in2", "ck_in3", "comb",
    "conv_acc", "conv_done", "conv_in", "conv_in_mm", "conv_rows", "conv_rows_mm", "conv_tail", "cpt_mm",
    "cpt_sb", "cq", "cs_mm", "csn", "cv_free", "cv_in0", "cv_in1", "cv_in2", "cv_in3", "decay_mm",
    "delta_out", "down_done", "down_free", "down_half", "dt_arg", "exp_done", "gb", "gdone", "gmm", "gsq",
    "gsqrt", "gu_done", "gu_free", "h_done", "in_bias", "in_const", "in_lam", "in_pages", "in_rows",
    "in_strip", "in_vec", "in_x", "kkqk", "kt_a", "kt_v", "kv_done", "lam_exp", "lam_sums", "layer_vecs",
    "m_mm", "m_sb", "mu_mm", "nw_sb", "o_mm", "out_done", "p_exp", "p_max", "p_mm", "p_out", "p_soft",
    "passed", "po_mm", "ppt_mm", "ppt_sb", "proj_a", "proj_done", "proj_v", "rms", "rows_a", "rows_mm",
    "rows_out", "rows_v", "s_mm", "setup_ev", "setup_mm", "silu", "soft", "sq_done", "ssq_done", "st_in",
    "st_new", "st_out", "staged", "state_done", "t_mm", "t_up", "table_out", "tm_mm", "tokm", "u_up",
    "vn_mm", "vn_sb", "w_loaded0", "w_loaded1", "w_mm", "x_act", "x_bege", "x_decay", "x_dt", "x_gb",
    "x_kkqk", "x_lt", "x_m", "x_mu", "x_new", "x_nw", "x_o", "x_out", "x_qe", "x_s", "x_so", "x_t", "x_u",
    "x_vb", "x_vn", "x_vnsb", "x_w", "x_ws", "y_mm", "y_out", "y_rows",
)


def trunk(nc, A, O, scratch):
    where, n_const = columns()
    with ExitStack() as ctx:
        def sb(name, *shape, dt=F32):
            return ctx.enter_context(nc.sbuf_tensor(name, [128, *shape], dt))

        xT = sb("residual", KD, NT)
        hT = sb("normed_or_mixed", KD, NT)
        work = sb("hidden_or_projected", NZ * NT)
        wslot = sb("weight_slots", 2, 2048)
        strips = sb("prompt_bias", 8, SEQ)
        bias_c = sb("sample_bias_c", PAST)
        bias_cn = sb("sample_bias_c_new", 2, NS)
        bias_b = sb("sample_bias_b", KEYS_B)
        bias_bn = sb("sample_bias_b_new", NS)
        vtok = sb("values_by_token", 5, 512)
        con = sb("constants", n_const)
        cols_conv = sb("conv_columns", 2 * 48)
        cols_norm = sb("norm_columns", 60)
        lay_conv = sb("layer_conv", 48)
        lay_norm = sb("layer_norm", LV)
        lay_ba = sb("layer_ba_weights", KD, 8)
        all_ba = sb("ba_weights", DEPTH, KD, 8)
        small = sb("small", 160)
        page_of = sb("page_of_row", 32, dt=I32)
        key_rows = sb("cache_rows", DEPTH, 32, dt=U32)
        lay_rows = sb("layer_cache_rows", 32, dt=U32)
        row_f = sb("cache_rows_f32", 32)
        arena = sb("arena", 9900)

        ps = ctx.enter_context(nc.psum_tensor("banks", [128, 8, 512], F32))
        flat = ps[:, :, :].rearrange("p b n -> p (b n)")

        def C(name, rows=128):
            lo, hi = where[name]
            return con[0:rows, lo:hi]

        def carve(tensor, start, *shape):
            n = int(np.prod(shape))
            v = tensor[:, start:start + n]
            if len(shape) == 2:
                v = v.rearrange("p (a b) -> p a b", a=shape[0])
            if len(shape) == 3:
                v = v.rearrange("p (a b c) -> p a b c", a=shape[0], b=shape[1])
            return v, start + n

        hidden, _ = carve(work, 0, NF, NT)
        gated, _ = carve(work, NF * NT, 2, NT)
        z, _ = carve(work, 0, NZ, NT)
        x_rows, _ = carve(work, 0, 5, D)
        bucket_rows, e_end = carve(work, 5 * D, U_TAB)
        table, t_end = carve(work, e_end, U_TAB)
        strip_raw, s_end = carve(work, 0, 8, SEQ)
        win_b, _ = carve(work, s_end + 1100, U_MAX + 1)
        win_c, _ = carve(work, t_end, U_MAX + 1)
        assert s_end + 1100 >= 5 * D and s_end + 1100 + U_MAX + 1 <= NZ * NT
        vec_rows_a, r_end = carve(arena, 0, 128)
        vec_rows_b, r_end = carve(arena, r_end, 128)
        relb, r_end = carve(arena, r_end, 8)
        lam_rows, r_end = carve(arena, r_end, 4, DEPTH * 32)
        lam_prod, r_end = carve(arena, r_end, 2, DEPTH * 32)
        y_rows, _ = carve(work, 0, 5, D)

        a_log_c, dt_c = small[:, 0:8], small[:, 8:16]
        lam_sum, lam_all = small[:, 16:20], small[:, 20:22]
        lam, cnorm = small[:, 22:23], small[:, 23:24]
        ea, dtb = small[:, 24:28], small[:, 28:32]
        ba, _ = carve(small, 32, 5, 8)
        beta, _ = carve(small, 72, 5, 4)
        gdec, _ = carve(small, 92, 5, 4)
        spa, _ = carve(small, 112, 5, 4)
        spb, _ = carve(small, 132, 5, 4)
        sign = small[:, 152:153]

        at = 0
        k_rows, at = carve(arena, at, 5, 512)
        conv_tail, at = carve(arena, at, 12, 27)
        conv_out, at = carve(arena, at, CONV_CH)
        conv_in, at = carve(arena, at, CONV_CH)
        xs, at = carve(arena, at, 12, 8, 7)
        cvt, at = carve(arena, at, 2, NT)
        sq, at = carve(arena, at, 2, NT)
        rn, at = carve(arena, at, 2, NT)
        assert at <= 9900

        at = 0
        names = ("qc", "kc", "vc", "gB", "bB", "DT", "eG", "LT", "LK", "QKT", "KB", "VB", "KD", "M", "U", "T", "nW", "VN", "S")
        m = {}
        for n in names:
            m[n], at = carve(arena, at, NH, 128)
        gc, at = carve(arena, at, 4)
        kde, at = carve(arena, at, 4)
        ecol, at = carve(arena, at, 4)
        bege, at = carve(arena, at, 4)
        assert at <= 9900
        at = 0
        t = {}
        t["st"] = arena[:, 0:4096].rearrange("p (h b v) -> p h b v", h=4, b=8)
        at = 4096
        for n in ("qc", "kc", "vc", "eG", "DT", "LT", "LK", "QKT", "M", "U", "T", "nW", "QS"):
            t[n], at = carve(arena, at, NH, NS)
        for n in ("gB", "KB", "VB", "KD", "VN"):
            t[n], at = carve(arena, at, NH, 128)
        t["WQ"], at = carve(arena, at, NH, 8, 8)
        t["bB"], at = carve(arena, at, NH, NS)
        sgc, at = carve(arena, at, 4)
        skde, at = carve(arena, at, 4)
        secol, at = carve(arena, at, 4)
        sbege, at = carve(arena, at, 4)
        assert at <= 9900
        vblk = carve(work, 0, 8, 128)[0], carve(work, 1024, 8, 128)[0]

        dead = 16 * NT
        c_rows, at = carve(work, 0, RING, 4, 256)
        c_kt, at = carve(work, at, 2, 2, 512)
        c_s, at = carve(work, at, PAST + NS)
        assert at <= dead
        b_rows, at = carve(work, 0, 2, 8, 256)
        b_kt, at = carve(work, at, 2, 2, KEYS_B)
        b_s, at = carve(work, at, KEYS_B + NS)
        assert at <= dead
        pv_rows, at = carve(work, RING * 1024, 8, 256)
        assert RING * 1024 == 2 * 8 * 256
        sq2, at = carve(arena, 0, 2, NT)
        rn2, at = carve(arena, at, 2, NT)
        comb, at = carve(arena, at, 64)
        c_mx, start = carve(arena, at, 4)
        c_pt, at = carve(arena, start, 17, 64)
        qc_all, qend = arena[:, at:at + 1152], at + 1152
        b_pt, at = carve(arena, start, 9, 128)
        qb_all, at = arena[:, at:at + 2176], at + 2176
        at = max(qend, at)
        cv_rows, v_end = carve(arena, at, RING, 4, 256)
        bv_rows, v_end2 = carve(arena, at, 2, 8, 256)
        assert max(v_end, v_end2) <= 9900

        def qc_of(b, pair):
            return qc_all[:, 256 * b + 128 * pair:256 * b + 128 * pair + 128]

        def qb_of(b, pair):
            return qb_all[:, 256 * b + 128 * pair:256 * b + 128 * pair + 128]

        def maps(u):
            return 1 if u < 16 else 2

        def qk_of(u, mp):
            head = u // 4 % 4
            if u < 16:
                return 16 + head // 2, 18 + head // 2, 64 * (head % 2), 64
            return 22 + head // 2, 24 + head // 2, 64 * (head % 2) + 32 * mp, 32

        p_s = arena[:, at:at + 2048].rearrange("p (u m k) -> p u m k", u=2, m=2)
        at += 2048
        p_pt, at = carve(arena, at, 2, 4, 128)
        p_mx, at = carve(arena, at, 2, 8)
        assert at <= 9900

        s = {}
        for n in SIGNALS:
            s[n] = ctx.enter_context(nc.semaphore(n))
        block = ctx.enter_context(nc.Block())

        def alone(eng):
            eng.sem_inc(s["passed"], 1)

        def window_block(blk):
            return (128 * blk, 128) if blk < 4 else (512 + 96 * (blk - 4), 96)

        def half(bank, h):
            return ps[:, bank + h, 0:HALF]

        def both(bank):
            return ps[:, bank:bank + 2, 0:HALF]

        def tok(v):
            return v.rearrange("p (h n) -> p h n", h=2)

        def over(v, n):
            return v.unsqueeze(2).broadcast_to([v.shape[0], v.shape[1], n])

        def per_head(v, n=4):
            return v.unsqueeze(1).broadcast_to([v.shape[0], n, v.shape[1]])

        @block.sync
        def _(sp):
            def ld(dst, src, name, inc=16):
                return sp.dma_start(dst, src).then_inc(s[name], inc)

            ld(con[:, :], A["consts"], "in_const")
            ld(x_rows[:, 0:4, :], A["x_prompt"][0].rearrange("(t p) d -> p t d", p=128), "in_x")
            ld(x_rows[0:NS, 4, :], A["x_sample"].rearrange("b t d -> (b t) d"), "in_x")
            ld(vec_rows_a[0:96, :], A["conv_w"].rearrange("l j (c p) -> (l j c) p", p=128), "in_vec")
            for l in range(DEPTH):
                for i, name in enumerate(("norm_ffn1", "norm_mix", "norm_ffn2")):
                    ld(vec_rows_b[LV * l + 8 * i:LV * l + 8 * i + 8, :],
                       A[name][l].rearrange("(k p) -> k p", p=128), "in_vec")
                ld(vec_rows_b[LV * l + 24:LV * l + 25, :], A["a_norm_w"][l:l + 1], "in_vec")
                for h in range(2):
                    ld(vec_rows_b[LV * l + 25:LV * l + 26, 64 * h:64 * h + 64], A["c_norm_w"][l:l + 1], "in_vec")
            ld(vec_rows_b[2 * LV:2 * LV + 8, :], A["final_norm"].rearrange("(k p) -> k p", p=128), "in_vec")
            ld(relb[0:32, :], A["rel_bias"], "in_bias")
            ld(relb[32:34, :], A["pick"], "in_bias")
            ld(bucket_rows[0:34, :], A["buckets"], "in_bias")
            for i, name in enumerate(("lambda_q1", "lambda_k1", "lambda_q2", "lambda_k2")):
                ld(lam_rows[:, i, :], A[name].rearrange("l d -> (l d)").partition_broadcast(128), "in_lam")
            ld(a_log_c, A["a_log"].rearrange("l h -> (l h)").partition_broadcast(128), "in_lam")
            ld(dt_c, A["dt_bias"].rearrange("l h -> (l h)").partition_broadcast(128), "in_lam")
            for l in range(DEPTH):
                ld(all_ba[:, l], A["w_in"][l, :, BA_COL:BC_COL].rearrange("(k p) n -> p k n", p=128), "in_lam")
            for pg in range(4):
                src = bass.AP(tensor=A["page_table"].tensor, offset=pg, ap=[[0, 32], [4, 32]])
                sp.dma_start(page_of[32 * pg:32 * pg + 32, :], src, allow_slow_non_contiguous=True).then_inc(s["in_pages"], 16)
            sp.wait_ge(s["setup_ev"], 11)
            ld(scratch[:, :], table[0:8, :], "table_out")
            sp.wait_ge(s["table_out"], 16)
            for h in range(8):
                src = bass.AP(tensor=scratch.tensor, offset=h * U_TAB + U_MAX - 384 - 127, ap=[[1, 128], [1, SEQ]])
                ld(strip_raw[:, h, :], src, "in_strip")
            for step in range(T_S):
                off = T_S - 1 - step
                for b in range(4):
                    ld(win_c[32 * b + step:32 * b + 32:4, 0:PAST + T_S],
                       bass.AP(tensor=scratch.tensor, offset=4 * U_TAB + off, ap=[[U_TAB, 4], [0, 2], [1, PAST + T_S]]),
                       "in_rows")
                ld(win_b[step:128:4, 0:PAST + T_S],
                   bass.AP(tensor=scratch.tensor, offset=off, ap=[[0, 8], [U_TAB, 4], [1, PAST + T_S]]), "in_rows")

            def load_gate(l, w, f, slot):
                for i, name in enumerate((f"w{w + 1}_gate", f"w{w + 1}_up")):
                    dst = wslot[:, slot, 1024 * i:1024 * i + 1024].rearrange("p (k n) -> p k n", k=KD)
                    src = A[name][ds(l, 1), :, ds(f * 128, 128)].rearrange("l (k p) n -> p (l k) n", p=128)
                    ld(dst, src, f"w_loaded{slot}")

            def load_down(l, w, o, slot):
                dst = wslot[:, slot, 0:11 * 128].rearrange("p (k n) -> p k n", k=11)
                src = A[f"w{w + 1}_down"][ds(l, 1), slot * 1408:slot * 1408 + 1408, ds(o * 128, 128)]
                ld(dst, src.rearrange("l (k p) n -> p (l k) n", p=128), f"w_loaded{slot}", 32)

            def load_wide(l, name, col, slot):
                dst = wslot[:, slot, :].rearrange("p (k n) -> p k n", k=KD)
                src = A[name][ds(l, 1), :, ds(col, 256)].rearrange("l (k p) n -> p (l k) n", p=128)
                ld(dst, src, f"w_loaded{slot}", 32)

            def ffn_loads(l, w):
                it = l * 2 + w
                for slot in range(2):
                    if w == 0:
                        sp.wait_ge(s["down_half" if slot == 0 else "down_done"], it * 8 + 1)
                    else:
                        sp.wait_ge(s["out_done"], l * 8 + 6 + 2 * slot)
                    load_gate(l, w, slot, slot)
                with sp.Fori(1, 11) as j:
                    for slot in range(2):
                        sp.wait_ge(s["gu_done"], it * 22 + j * 2 + slot - 1)
                        load_gate(l, w, j * 2 + slot, slot)
                for slot in range(2):
                    sp.wait_ge(s["gu_done"], it * 22 + 21 + slot)
                    load_down(l, w, 0, slot)
                with sp.Fori(1, 8) as o:
                    for slot in range(2):
                        sp.wait_ge(s["down_half" if slot == 0 else "down_done"], it * 8 + o + 1)
                        load_down(l, w, o, slot)

            with sp.Fori(0, DEPTH) as l:
                sp.wait_ge(s["x_new"], l * 3 + 1)
                ld(conv_in[0:24, :], A["state_conv"][ds(l, 1)].rearrange("l b j c -> (l b j) c"), "conv_in")
                ffn_loads(l, 0)
                for slot in range(2):
                    sp.wait_ge(s["down_half" if slot == 0 else "down_done"], l * 16 + 8 + 1)
                    load_wide(l, "w_in", slot * 256, slot)
                with sp.Fori(1, 4) as j:
                    for slot in range(2):
                        sp.wait_ge(s["proj_done"], l * 28 + 4 * j + 2 * slot - 2)
                        load_wide(l, "w_in", j * 512 + slot * 256, slot)
                with sp.Fori(4, 7) as j:
                    for slot in range(2):
                        sp.wait_ge(s["proj_done"], l * 28 + 4 * j + 2 * slot - 2)
                        load_wide(l, "w_in", j * 512 + slot * 256 + 8, slot)
                for slot in range(2):
                    sp.wait_ge(s["proj_done"], l * 28 + 26 + 2 * slot)
                    load_wide(l, "w_out", slot * 256, slot)
                sp.wait_ge(s["state_done"], l * 5 + 5)
                for h in range(NH):
                    ld(t["st"][:, h], A["state_delta"][ds(l, 1), :, h].rearrange("l b k v -> k (l b) v"), "st_in")
                def load_window(name, dst, n, slot, sem):
                    rows = A[name][ds(l, 1), ds(n, 1)].rearrange("l b p h d -> (l b p) (h d)")
                    ld(dst[:, slot, 0:4, :], rows[1536:2048].rearrange("(p r) c -> p r c", r=4), sem)
                    ld(dst[0:96, slot, 4:8, :], rows[0:1536].rearrange("(a r) c -> a r c", r=16)[:, 0:4, :], sem)

                sp.wait_ge(s["ck_free"], l * 32 + 32 + 4)
                for slot in range(2):
                    load_window("cache_win_k", b_rows, slot, slot, f"bk_in{slot}")
                sp.wait_ge(s["cv_free"], l * 32 + 32 + 4)
                for slot in range(2):
                    load_window("cache_win_v", bv_rows, slot, slot, f"bv_in{slot}")
                for name, dst, tag in (("cache_win_k", b_rows, "bk"), ("cache_win_v", bv_rows, "bv")):
                    with sp.Fori(1, 4) as j:
                        for slot in range(2):
                            sp.wait_ge(s[tag + "_free"], l * 8 + j * 2 + slot + 1)
                            alone(sp)
                            load_window(name, dst, j * 2 + slot, slot, f"{tag}_in{slot}")
                for slot in range(2):
                    sp.wait_ge(s["out_done"], l * 8 + 2 + 2 * slot)
                    load_wide(l, "w_out", 512 + slot * 256, slot)
                ffn_loads(l, 1)

        @block.gpsimd
        def _(gp):
            def st(dst, src, name):
                return gp.dma_start(dst, src).then_inc(s[name], 16)

            with gp.Fori(0, DEPTH) as l:
                gp.wait_ge(s["rows_a"], l * 5 + 5)
                gp.wait_ge(s["rows_v"], l * 5 + 5)
                for out_p, out_s, src in ((O["wk_p"], O["wk_s"], k_rows[:, :, 0:256]), (O["wv_p"], O["wv_s"], vtok[:, :, 0:256]),
                                          (O["k_p"], O["k_s"], k_rows[:, :, 256:512]), (O["v_p"], O["v_s"], vtok[:, :, 256:512])):
                    st(out_p[ds(l, 1)].rearrange("l b (t p) h d -> p (l b t) (h d)", p=128), src[:, 0:4, :], "rows_out")
                    st(out_s[ds(l, 1)].rearrange("l b t h d -> (l b t) (h d)"), src[0:NS, 4, :], "rows_out")
                gp.wait_ge(s["conv_rows"], l + 1)
                st(O["conv_p"][ds(l, 1)].rearrange("l b j c -> (l b j) c"), conv_out[0:3, :], "rows_out")
                st(O["conv_s"][ds(l, 1)].rearrange("l b j c -> (l b j) c"), conv_out[3:27, :], "rows_out")
                gp.wait_ge(s["state_done"], l * 5 + 5)
                st(O["delta_p"][ds(l, 1)].rearrange("l b h k v -> k (l b h) v"), m["S"][:, :, :], "delta_out")
                for h in range(NH):
                    gp.wait_ge(s["st_new"], l * 4 + h + 1)
                    st(O["delta_s"][ds(l, 1), :, h].rearrange("l b k v -> k (l b) v"), t["st"][:, h], "st_out")

                def load_chunk(name, n):
                    tag, dst = ("ck", c_rows) if name == "cache_k" else ("cv", cv_rows)
                    gp.wait_ge(s[tag + "_free"], l * 32 + n + 1)
                    alone(gp)
                    rows = A[name].rearrange("l n (k r) h d -> (l n k) (r h d)", r=4)
                    gp.indirect_dma_start(dst[:, n % RING].rearrange("p r c -> p (r c)"), None, rows,
                                          bass.IndirectOffsetOnAxis(ap=lay_rows[:, n:n + 1], axis=0))\
                        .then_inc(s[f"{tag}_in{n % RING}"], 16)

                gp.wait_ge(s["layer_vecs"], l + 1)
                gp.wait_ge(s["gdone"], l * 14 + 14)
                for n in range(0, 12):
                    load_chunk("cache_k", n)
                for n in range(4):
                    load_chunk("cache_v", n)
                    load_chunk("cache_k", 12 + n)
                for n in range(4):
                    load_chunk("cache_v", 4 + n)
                    load_chunk("cache_k", 16 + n)
                for n in range(8, 16):
                    load_chunk("cache_v", n)
                for n in range(20, 28):
                    load_chunk("cache_k", n)
                for n in range(4):
                    load_chunk("cache_v", 16 + n)
                    load_chunk("cache_k", 28 + n)
                for n in range(20, 32):
                    load_chunk("cache_v", n)
            gp.wait_ge(s["y_rows"], 5)
            st(O["y_p"][0].rearrange("(t p) d -> p t d", p=128), y_rows[:, 0:4, :], "y_out")
            st(O["y_s"].rearrange("b t d -> (b t) d"), y_rows[0:NS, 4, :], "y_out")
            gp.wait_ge(s["y_out"], 32)
            gp.wait_ge(s["rows_out"], DEPTH * 160)
            gp.wait_ge(s["delta_out"], DEPTH * 16)
            gp.wait_ge(s["st_out"], DEPTH * 64)

        @block.tensor
        def _(pe):
            ident = C("ident")
            for name in ("down_half", "down_done"):
                pe.sem_inc(s[name], 1)
            for name in ("gmm", "bk_free", "bv_free", "cs_mm", "bs_mm"):
                pe.sem_inc(s[name], 2)
            for name in ("ck_free", "cv_free"):
                pe.sem_inc(s[name], RING)

            def turn(out, in_, rows=128):
                return pe.transpose(out, in_, ident[0:rows, 0:rows])

            pe.wait_ge(s["in_const"], 16)
            pe.wait_ge(s["in_x"], 32)
            for i in range(1, 6):
                if i > 2:
                    pe.wait_ge(s["setup_ev"], i - 2)
                bank = 2 * (i % 2)
                n = 128 if i < 5 else NS
                for k in range(KD):
                    mm = turn(flat[:, 512 * bank + n * k:512 * bank + n * k + n],
                              x_rows[0:n, i - 1, 128 * k:128 * k + 128], n)
                mm.then_inc(s["setup_mm"], 1)
            pe.wait_ge(s["setup_ev"], 4)
            pe.wait_ge(s["in_vec"], 16 * (1 + DEPTH * 6 + 1))
            turn(ps[:, 0, 0:96], vec_rows_a[0:96, :], 96)
            turn(ps[:, 0, 96:156], vec_rows_b[0:60, :], 60).then_inc(s["setup_mm"], 1)
            pe.wait_ge(s["in_bias"], 48)
            for c in range(5):
                i, n = 7 + c, min(512, U_TAB - 512 * c)
                pe.wait_ge(s["setup_ev"], i - 2)
                pe.matmul(ps[0:8, 2 * (i % 2), 0:n], relb[0:34, :], bucket_rows[0:34, 512 * c:512 * c + n],
                          start=True, stop=True).then_inc(s["setup_mm"], 1)
            pe.wait_ge(s["in_strip"], 128)
            for h in range(8):
                i = 12 + h
                pe.wait_ge(s["setup_ev"], i - 2)
                pe.matmul(ps[:, 2 * (i % 2), :], C("flip"), strip_raw[:, h, :],
                          start=True, stop=True).then_inc(s["setup_mm"], 1)

            def norm(n):
                for k in range(KD):
                    pe.wait_ge(s["sq_done"], n * 8 + k + 1)
                    for h in range(2):
                        mm = pe.matmul(half(0, h), C("ones"), hT[:, k, h * HALF:(h + 1) * HALF],
                                       start=k == 0, stop=k == KD - 1)
                mm.then_inc(s["ssq_done"], 1)

            def ffn(l, w):
                it = l * 2 + w
                fill = l * 47 + 28 * w
                pe.wait_ge(s["h_done"], (l * 3 + 2 * w) * 8 + 8)
                alone(pe)
                with pe.Fori(0, 11) as j:
                    for slot in range(2):
                        pe.wait_ge(s[f"w_loaded{slot}"], (fill + j + 1) * 32)
                        pe.wait_ge(s["gu_free"], it * 22 + j * 2 + slot + 1)
                        for i in range(2):
                            for k in range(KD):
                                at = 1024 * i + 128 * k
                                for h in range(2):
                                    mm = pe.matmul(half(4 * slot + 2 * i, h), wslot[:, slot, at:at + 128],
                                                   hT[:, k, h * HALF:(h + 1) * HALF], start=k == 0, stop=k == KD - 1)
                        mm.then_inc(s["gu_done"], 1)
                pe.wait_ge(s["gu_free"], it * 22 + 22 + 2)
                alone(pe)
                with pe.Fori(0, 4) as j:
                    for u in range(2):
                        pe.wait_ge(s["down_free"], it * 8 + j * 2 + u + 1)
                        for part in range(2):
                            pe.wait_ge(s[f"w_loaded{part}"], (fill + 11 + j * 2 + u + 1) * 32)
                            for q in range(11):
                                for h in range(2):
                                    mm = pe.matmul(half(4 * u, h), wslot[:, part, 128 * q:128 * q + 128],
                                                   hidden[:, 11 * part + q, h * HALF:(h + 1) * HALF],
                                                   start=part == 0 and q == 0, stop=part == 1 and q == 10)
                            mm.then_inc(s["down_done" if part else "down_half"], 1)

            def project(l):
                pe.wait_ge(s["h_done"], (l * 3 + 1) * 8 + 8)
                alone(pe)
                with pe.Fori(0, 7) as j:
                    for slot in range(2):
                        pe.wait_ge(s[f"w_loaded{slot}"], (l * 47 + 19 + j + 1) * 32)
                        for u in range(2):
                            pe.wait_ge(s["proj_v" if u else "proj_a"], l * 14 + j * 2 + slot + 1)
                            for k in range(KD):
                                at = 256 * k + 128 * u
                                for h in range(2):
                                    mm = pe.matmul(half(4 * slot + 2 * u, h), wslot[:, slot, at:at + 128],
                                                   hT[:, k, h * HALF:(h + 1) * HALF], start=k == 0, stop=k == KD - 1)
                            mm.then_inc(s["proj_done"], 1)
                pe.wait_ge(s["proj_a"], l * 14 + 16)
                pe.wait_ge(s["proj_v"], l * 14 + 16)
                for b in range(5):
                    n = 128 if b < 4 else NS
                    for k in range(KD):
                        mm = pe.matmul(ps[0:n, 0, 8 * b:8 * b + 8], hT[:, k, 128 * b:128 * b + n], lay_ba[:, k, :],
                                       start=k == 0, stop=k == KD - 1)
                mm.then_inc(s["ba_mm"], 1)
                for b in range(5):
                    n = 128 if b < 4 else NS
                    a = 2 + 2 * (b % 2)
                    if b >= 2:
                        pe.wait_ge(s["rows_a"], l * 5 + b - 1)
                        pe.wait_ge(s["rows_v"], l * 5 + b - 1)
                    for i, tile in enumerate((18, 19, 20, 21, 24, 25, 26, 27)):
                        mm = turn(ps[0:n, a + i // 4, 128 * (i % 4):128 * (i % 4) + 128], z[:, tile, 128 * b:128 * b + n])
                    mm.then_inc(s["rows_mm"], 1)
                pe.wait_ge(s["conv_tail"], l + 1)
                pe.wait_ge(s["rows_v"], l * 5 + 4)
                for c in range(12):
                    mm = turn(ps[0:27, 5 + c // 4, 128 * (c % 4):128 * (c % 4) + 128], conv_tail[:, c, :])
                mm.then_inc(s["conv_rows_mm"], 1)

            def square_sums(base, u, ones, sqb):
                pe.wait_ge(s["gsq"], base + u + 1)
                pe.wait_ge(s["gsqrt"], base + u + 1)
                for h in range(2):
                    mm = pe.matmul(half(2 * (u % 2), h), ones, sqb[:, u % 2, h * HALF:(h + 1) * HALF],
                                   start=True, stop=True)
                mm.then_inc(s["gmm"], 1)

            def chunk(l, c):
                it = l * 4 + c
                pe.wait_ge(s["staged"], it + 1)
                for h in range(NH):
                    turn(ps[:, 0, 128 * h:128 * h + 128], m["kc"][:, h, :])
                    mm = turn(ps[:, 1, 128 * h:128 * h + 128], m["vc"][:, h, :])
                mm.then_inc(s["tokm"], 1)
                pe.wait_ge(s["gb"], it + 1)
                for h in range(NH):
                    hs = slice(128 * h, 128 * h + 128)
                    pe.matmul(ps[:, 2, hs], m["gB"][:, h, :], C("tri"), start=True, stop=True)
                    pe.matmul(ps[:, 3, hs], m["bB"][:, h, :], ident, start=True, stop=True)
                pe.matmul(ps[:, 4, 0:4], C("tri"), m["gB"][:, :, 0], start=True, stop=True).then_inc(s["decay_mm"], 1)
                for h in range(NH):
                    hs = slice(128 * h, 128 * h + 128)
                    pe.matmul(ps[:, 5, hs], m["kc"][:, h, :], m["kc"][:, h, :], start=True, stop=True)
                    mm = pe.matmul(ps[:, 6, hs], m["kc"][:, h, :], m["qc"][:, h, :], start=True, stop=True)
                mm.then_inc(s["kkqk"], 1)
                pe.wait_ge(s["u_up"], it * 14 + 2)
                for h in range(NH):
                    mm = turn(ps[:, 2 + h // 2, 128 * (h % 2):128 * (h % 2) + 128], m["U"][:, h, :])
                mm.then_inc(s["t_mm"], 1)

                def level(k, last=False):
                    for a in range(2):
                        pe.wait_ge(s["t_up"], it * 12 + k * 2 + a - 1)
                        for i in range(2):
                            mm = pe.matmul(ps[:, 4 if a else 7, 128 * i:128 * i + 128], m["LK"][:, 2 * a + i, :],
                                           m["T"][:, 2 * a + i, :], start=True, stop=True)
                        mm.then_inc(s["m_mm"], 1)
                    for a in range(2):
                        pe.wait_ge(s["m_sb"], it * 12 + k * 2 + a - 1)
                        pe.wait_ge(s["u_up"], it * 14 + k * 2 + a - 1)
                        if not last:
                            for i in range(2):
                                mm = pe.matmul(ps[:, 2 + a, 128 * i:128 * i + 128], m["U"][:, 2 * a + i, :],
                                               m["M"][:, 2 * a + i, :], start=True, stop=True)
                            mm.then_inc(s["tm_mm"], 1)
                        for i in range(2):
                            mm = pe.matmul(ps[:, 5 + a, 128 * i:128 * i + 128], m["M"][:, 2 * a + i, :],
                                           m["U"][:, 2 * a + i, :], start=True, stop=True)
                        mm.then_inc(s["mu_mm"], 1)

                with pe.Fori(1, 6) as k:
                    level(k)
                level(6, last=True)
                pe.wait_ge(s["u_up"], it * 14 + 14)
                pe.wait_ge(s["kv_done"], it + 1)
                for h in range(NH):
                    mm = pe.matmul(ps[:, 7, 128 * h:128 * h + 128], m["KB"][:, h, :], m["U"][:, h, :], start=True, stop=True)
                mm.then_inc(s["w_mm"], 1)
                pe.wait_ge(s["nw_sb"], it + 1)
                for h in range(NH):
                    hs = slice(128 * h, 128 * h + 128)
                    pe.matmul(ps[:, 2, hs], m["U"][:, h, :], m["VB"][:, h, :], start=True, stop=False)
                    mm = pe.matmul(ps[:, 2, hs], m["nW"][:, h, :], m["S"][:, h, :], start=False, stop=True)
                mm.then_inc(s["vn_mm"], 1)
                pe.wait_ge(s["vn_sb"], it + 1)
                for h in range(NH):
                    hs = slice(128 * h, 128 * h + 128)
                    pe.matmul(ps[:, 3, hs], m["S"][:, h, :], m["qc"][:, h, :], start=True, stop=False)
                    mm = pe.matmul(ps[:, 3, hs], m["VN"][:, h, :], m["QKT"][:, h, :], start=False, stop=True)
                mm.then_inc(s["o_mm"], 1)
                for h in range(NH):
                    mm = pe.matmul(ps[:, 4, 128 * h:128 * h + 128], m["KD"][:, h, :], m["VN"][:, h, :], start=True, stop=True)
                mm.then_inc(s["s_mm"], 1)

            def sample_chunk(l):
                pe.wait_ge(s["x_act"], l * 5 + 1)
                for h in range(NH):
                    turn(ps[0:NS, 0, 128 * h:128 * h + 128], t["kc"][:, h, :])
                    mm = turn(ps[0:NS, 1, 128 * h:128 * h + 128], t["vc"][:, h, :])
                pe.wait_ge(s["x_gb"], l + 1)
                for h in range(NH):
                    hs = slice(NS * h, NS * h + NS)
                    pe.matmul(ps[:, 2, hs], t["gB"][0:NS, h, :], C("tri4", NS), start=True, stop=True)
                    pe.matmul(ps[0:NS, 3, hs], t["bB"][0:NS, h, :], ident[0:NS, 0:NS], start=True, stop=True)
                pe.matmul(ps[0:NS, 4, 0:4], C("tri4", NS), t["gB"][0:NS, :, 0], start=True, stop=True)
                pe.matmul(ps[0:NS, 4, 4:8], C("blk4", NS), t["gB"][0:NS, :, 0], start=True, stop=True).then_inc(s["x_decay"], 1)
                for h in range(NH):
                    hs = slice(NS * h, NS * h + NS)
                    pe.matmul(ps[0:NS, 5, hs], t["kc"][:, h, :], t["kc"][:, h, :], start=True, stop=True)
                    mm = pe.matmul(ps[0:NS, 6, hs], t["kc"][:, h, :], t["qc"][:, h, :], start=True, stop=True)
                mm.then_inc(s["x_kkqk"], 1)
                pe.wait_ge(s["x_u"], l * 2 + 1)
                alone(pe)
                for h in range(NH):
                    mm = turn(ps[0:NS, 6, NS * h:NS * h + NS], t["U"][0:NS, h, :], NS)
                mm.then_inc(s["x_t"], 1)
                pe.wait_ge(s["x_lt"], l + 1)
                alone(pe)
                for h in range(NH):
                    mm = pe.matmul(ps[0:NS, 7, NS * h:NS * h + NS], t["LK"][0:NS, h, :], t["T"][0:NS, h, :], start=True, stop=True)
                mm.then_inc(s["x_m"], 1)
                pe.wait_ge(s["x_act"], l * 5 + 4)
                alone(pe)
                for h in range(NH):
                    mm = pe.matmul(ps[0:NS, 5, NS * h:NS * h + NS], t["M"][0:NS, h, :], t["U"][0:NS, h, :], start=True, stop=True)
                mm.then_inc(s["x_mu"], 1)
                pe.wait_ge(s["x_u"], l * 2 + 2)
                for h in range(NH):
                    mm = pe.matmul(ps[:, 7, NS * h:NS * h + NS], t["KB"][0:NS, h, :], t["U"][0:NS, h, :], start=True, stop=True)
                mm.then_inc(s["x_w"], 1)
                pe.wait_ge(s["x_act"], l * 5 + 5)
                pe.wait_ge(s["x_qe"], l + 1)
                pe.wait_ge(s["st_in"], l * 64 + 64)
                for h in range(NH):
                    for b in range(NB_S):
                        mm = pe.matmul(ps[:, 2, 64 * h + 8 * b:64 * h + 8 * b + 8], t["st"][:, h, b, :], t["WQ"][:, h, b, :],
                                       start=True, stop=True)
                mm.then_inc(s["x_ws"], 1)
                pe.wait_ge(s["x_nw"], l + 1)
                alone(pe)
                for h in range(NH):
                    hs = slice(128 * h, 128 * h + 128)
                    pe.matmul(ps[0:NS, 3, hs], t["U"][0:NS, h, :], t["VB"][0:NS, h, :], start=True, stop=False)
                    mm = pe.matmul(ps[0:NS, 3, hs], t["nW"][:, h, :], ident, start=False, stop=True)
                mm.then_inc(s["x_vn"], 1)
                pe.wait_ge(s["x_vnsb"], l + 1)
                alone(pe)
                for h in range(NH):
                    mm = pe.matmul(ps[:, 4, NS * h:NS * h + NS], t["VN"][0:NS, h, :], t["QKT"][0:NS, h, :], start=True, stop=True)
                mm.then_inc(s["x_o"], 1)
                for h in range(NH):
                    pe.wait_ge(s["x_vb"], l * 4 + h + 1)
                    if h >= 2:
                        pe.wait_ge(s["st_new"], l * 4 + h - 1)
                    for i in range(2):
                        mm = pe.matmul(ps[:, (6 if h % 2 else 0) + i, :], t["KD"][0:NS, h, :],
                                       vblk[h % 2][0:NS, 4 * i:4 * i + 4, :], start=True, stop=True)
                    mm.then_inc(s["x_s"], 1)

            def group_c(l, g):
                G = l * 2 + g
                pe.wait_ge(s["cq"], G + 1)

                def scores(n):
                    pe.wait_ge(s["kt_a"], G * 16 + n + 1)
                    pe.wait_ge(s["kt_v"], G * 16 + n + 1)
                    for pair in range(2):
                        mm = pe.matmul(ps[:, n % 4, :], qc_of(n // 4, pair), c_kt[:, n % 2, pair, :],
                                       start=n < 4 and pair == 0, stop=n >= 12 and pair == 1)
                    mm.then_inc(s["cs_mm"], 1)

                for n in range(16):
                    pe.wait_ge(s[f"ck_in{n % RING}"], (G * 4 + n // RING + 1) * 16)
                    if n >= 2:
                        pe.wait_ge(s["kt_a"], G * 16 + n - 1)
                        pe.wait_ge(s["kt_v"], G * 16 + n - 1)
                    for pair in range(2):
                        for pg in range(4):
                            mm = turn(ps[:, 4 + 2 * (n % 2) + pair, 128 * pg:128 * pg + 128],
                                      c_rows[:, n % RING, pg, 128 * pair:128 * pair + 128])
                    mm.then_inc(s["ck_free"], 1)
                    if n >= 1:
                        scores(n - 1)
                scores(15)
                for b in range(4):
                    for pair in range(2):
                        mm = pe.matmul(ps[:, 4, 0:NS], qc_of(b, pair), z[:, 24 + pair, SEQ:NT],
                                       start=b == 0 and pair == 0, stop=b == 3 and pair == 1)
                mm.then_inc(s["csn"], 1)
                pe.wait_ge(s["comb"], G + 1)
                for blk in range(16):
                    pe.matmul(ps[:, blk // 8, 64 * (blk % 8):64 * (blk % 8) + 64], c_s[:, 128 * blk:128 * blk + 128],
                              comb[:, :], start=True, stop=True)
                pe.matmul(ps[0:NS, 2, 0:64], c_s[:, PAST:PAST + NS], comb[:, :], start=True, stop=True).then_inc(s["cpt_mm"], 1)
                pe.wait_ge(s["cpt_sb"], G + 1)
                for n in range(16):
                    b, kc = n // 4, n % 4
                    pe.wait_ge(s[f"cv_in{n % RING}"], (G * 4 + n // RING + 1) * 16)
                    out = ps[0:16, 4 + b // 2, 256 * (b % 2):256 * (b % 2) + 256]
                    if kc == 0:
                        alone(pe)
                        pe.matmul(out, c_pt[0:NS, 16, 16 * b:16 * b + 16], vtok[0:NS, 4, 256:512], start=True, stop=False)
                    for pg in range(4):
                        mm = pe.matmul(out, c_pt[:, 4 * kc + pg, 16 * b:16 * b + 16], cv_rows[:, n % RING, pg, :],
                                       start=False, stop=kc == 3 and pg == 3)
                    mm.then_inc(s["cv_free"], 1)
                pe.wait_ge(s["c_pv"], G + 1)
                alone(pe)
                for b in range(4):
                    for pair in range(2):
                        mm = turn(ps[:, 6, 32 * b + 16 * pair:32 * b + 16 * pair + 16],
                                  pv_rows[0:16, b, 128 * pair:128 * pair + 128], 16)
                mm.then_inc(s["c_pv_mm"], 1)

            def sample_b(l):
                pe.wait_ge(s["bq"], l + 1)

                def scores(b):
                    pe.wait_ge(s["bkt_a"], l * 8 + b + 1)
                    pe.wait_ge(s["bkt_v"], l * 8 + b + 1)
                    for pair in range(2):
                        for i, n in ((0, 512), (1, 384)):
                            mm = pe.matmul(ps[:, i, 0:n], qb_of(b, pair), b_kt[:, b % 2, pair, 512 * i:512 * i + n],
                                           start=b == 0 and pair == 0, stop=b == 7 and pair == 1)
                    mm.then_inc(s["bs_mm"], 1)

                for b in range(NB_S):
                    pe.wait_ge(s[f"bk_in{b % 2}"], (l * 4 + b // 2 + 1) * 32)
                    if b >= 1:
                        pe.wait_ge(s["bkt_a"], l * 8 + b)
                        pe.wait_ge(s["bkt_v"], l * 8 + b)
                    for pair in range(2):
                        for blk in range(8):
                            lo, n = window_block(blk)
                            at = 2048 + 1024 * pair + lo
                            mm = turn(flat[:, at:at + n], b_rows[0:n, b % 2, blk, 128 * pair:128 * pair + 128], n)
                    mm.then_inc(s["bk_free"], 1)
                    if b >= 1:
                        scores(b - 1)
                scores(7)
                for b in range(NB_S):
                    for pair in range(2):
                        mm = pe.matmul(ps[:, 2, 0:NS], qb_of(b, pair), z[:, 18 + pair, SEQ:NT],
                                       start=b == 0 and pair == 0, stop=b == 7 and pair == 1)
                mm.then_inc(s["bsn"], 1)
                pe.wait_ge(s["bp"], l + 1)
                for blk in range(8):
                    lo, n = window_block(blk)
                    turn(flat[0:n, 128 * blk:128 * blk + 128], b_s[:, lo:lo + n])
                turn(ps[0:NS, 2, 0:128], b_s[:, KEYS_B:KEYS_B + NS]).then_inc(s["bpt_mm"], 1)
                pe.wait_ge(s["bpt_sb"], l + 1)
                for b in range(NB_S):
                    pe.wait_ge(s[f"bv_in{b % 2}"], (l * 4 + b // 2 + 1) * 32)
                    out = ps[0:16, 4 + b // 2, 256 * (b % 2):256 * (b % 2) + 256]
                    alone(pe)
                    pe.matmul(out, b_pt[0:NS, 8, 16 * b:16 * b + 16], vtok[0:NS, 4, 0:256], start=True, stop=False)
                    for blk in range(8):
                        n = window_block(blk)[1]
                        mm = pe.matmul(out, b_pt[0:n, blk, 16 * b:16 * b + 16], bv_rows[0:n, b % 2, blk, :],
                                       start=False, stop=blk == 7)
                    mm.then_inc(s["bv_free"], 1)
                pe.wait_ge(s["b_pv"], l + 1)
                alone(pe)
                for b in range(NB_S):
                    for pair in range(2):
                        mm = turn(ps[:, 0, 32 * b + 16 * pair:32 * b + 16 * pair + 16],
                                  pv_rows[0:16, b, 128 * pair:128 * pair + 128], 16)
                mm.then_inc(s["b_pv_mm"], 1)

            def prompt(l):
                def scores(u):
                    if u >= 2:
                        pe.wait_ge(s["p_max"], l * 32 + u - 1)
                    for mp in range(maps(u)):
                        tq, tk, lo, n = qk_of(u, mp)
                        q0, wid = 128 * (u % 4), 128 * (u % 4 + 1)
                        mm = pe.matmul(ps[:, 2 * (u % 2) + mp, 0:wid], z[lo:lo + n, tq, q0:q0 + 128], z[lo:lo + n, tk, 0:wid],
                                       start=True, stop=True)
                    mm.then_inc(s["p_mm"], 1)

                def turned(u):
                    pe.wait_ge(s["p_soft"], l * 32 + u + 1)
                    if u >= 2:
                        pe.wait_ge(s["ppt_sb"], l * 32 + u - 1)
                    for kb in range(u % 4 + 1):
                        mm = turn(ps[:, 4 + u % 2, 128 * kb:128 * kb + 128], p_s[:, u % 2, 0, 128 * kb:128 * kb + 128])
                    mm.then_inc(s["ppt_mm"], 1)

                def values(u):
                    pe.wait_ge(s["ppt_sb"], l * 32 + u + 1)
                    if u >= 2:
                        pe.wait_ge(s["p_out"], l * 32 + u - 1)
                    v0 = 128 * (u // 8)
                    for kb in range(u % 4 + 1):
                        mm = pe.matmul(ps[:, 6 + u % 2, 0:128], vtok[:, kb, v0:v0 + 128], p_pt[:, u % 2, kb, :],
                                       start=kb == 0, stop=kb == u % 4)
                    mm.then_inc(s["po_mm"], 1)

                pe.wait_ge(s["b_out"], l + 1)
                for u in range(32 + 2):
                    if u < 32:
                        scores(u)
                    if 1 <= u < 33:
                        turned(u - 1)
                    if u >= 2:
                        values(u - 2)

            def w_out(l):
                pe.wait_ge(s["gdone"], l * 14 + 16)
                for o in range(8):
                    slot = o // 2 % 2
                    pe.wait_ge(s[f"w_loaded{slot}"], (l * 47 + 26 + o // 4 + 1) * 32)
                    if o >= 4:
                        pe.wait_ge(s["x_out"], l * 8 + o - 3)
                    for k in range(KD):
                        at = 256 * k + 128 * (o % 2)
                        for h in range(2):
                            mm = pe.matmul(half(2 * (o % 4), h), wslot[:, slot, at:at + 128],
                                           hT[:, k, h * HALF:(h + 1) * HALF], start=k == 0, stop=k == KD - 1)
                    mm.then_inc(s["out_done"], 1)

            with pe.Fori(0, DEPTH) as l:
                pe.wait_ge(s["layer_vecs"], l + 1)
                norm(l * 3)
                ffn(l, 0)
                pe.wait_ge(s["conv_in"], (l + 1) * 16)
                alone(pe)
                for c in range(12):
                    mm = turn(ps[:, 6, 24 * c:24 * c + 24], conv_in[0:24, 128 * c:128 * c + 128], 24)
                mm.then_inc(s["conv_in_mm"], 1)
                norm(l * 3 + 1)
                project(l)
                pe.wait_ge(s["rows_a"], l * 5 + 5)
                pe.wait_ge(s["rows_v"], l * 5 + 5)
                alone(pe)
                for base in (0, 4):
                    with pe.Fori(0, 2) as j:
                        for u in range(2):
                            square_sums(l * 14 + base + j * 2, u, C("ones"), sq)
                with pe.Fori(0, 4) as c:
                    chunk(l, c)
                sample_chunk(l)
                with pe.Fori(0, 2) as j:
                    for u in range(2):
                        square_sums(l * 14 + 8 + j * 2, u, C("ones"), sq2)
                with pe.Fori(0, 2) as g:
                    group_c(l, g)
                sample_b(l)
                prompt(l)
                for u in range(2):
                    square_sums(l * 14 + 12, u, C("blk64"), sq2)
                w_out(l)
                norm(l * 3 + 2)
                ffn(l, 1)
            norm(6)
            pe.wait_ge(s["h_done"], 56)
            for b in range(5):
                n = 128 if b < 4 else NS
                if b >= 2:
                    pe.wait_ge(s["y_rows"], b - 1)
                for k in range(KD):
                    at = 1024 * (b % 2) + 128 * k
                    mm = turn(flat[0:n, at:at + 128], hT[:, k, 128 * b:128 * b + n])
                mm.then_inc(s["y_mm"], 1)

        @block.scalar
        def _(act):
            for name in ("gsqrt", "conv_done", "proj_a"):
                act.sem_inc(s[name], 2)
            eps, one = C("eps"), C("one")

            def copy(out, in_, scale=1.0):
                return act.activation(out, in_, ACT.Copy, scale=scale)

            act.wait_ge(s["in_lam"], 16 * 8)
            act.wait_ge(s["in_const"], 16)
            act.activation(a_log_c, a_log_c, ACT.Exp)
            act.wait_ge(s["lam_sums"], 1)
            act.activation(lam_sum, lam_sum, ACT.Exp).then_inc(s["lam_exp"], 1)

            def norm(n):
                act.wait_ge(s["x_new"], n + 1)
                for k in range(KD):
                    act.activation(hT[:, k, :], xT[:, k, :], ACT.Square).then_inc(s["sq_done"], 1)
                act.wait_ge(s["ssq_done"], n + 1)
                act.activation(tok(gated[:, 0, :]), both(0), ACT.Sqrt, bias=eps, scale=1.0 / D).then_inc(s["rms"], 1)

            def ffn(l, w):
                it = l * 2 + w
                with act.Fori(0, 11) as j:
                    for slot in range(2):
                        act.wait_ge(s["gu_done"], it * 22 + j * 2 + slot + 1)
                        act.wait_ge(s["gu_free"], it * 22 + j * 2 + slot + 1)
                        act.activation(tok(gated[:, slot, :]), both(4 * slot), ACT.Silu).then_inc(s["silu"], 1)

            def tile_of(v, i):
                return v[:, ds(i, 1), :].rearrange("p a n -> p (a n)")

            def project(l):
                def evacuate(j, slot):
                    act.wait_ge(s["proj_done"], l * 28 + j * 4 + slot * 2 + 1)
                    dst = z[:, ds(j * 4 + slot * 2, 1), :].rearrange("p a (h n) -> p (a h) n", h=2)
                    copy(dst, both(4 * slot)).then_inc(s["proj_a"], 1)

                with act.Fori(0, 3) as j:
                    for slot in range(2):
                        evacuate(j, slot)
                        for u in range(2):
                            act.wait_ge(s["conv_acc"], l * 12 + j * 4 + slot * 2 + u + 1)
                            alone(act)
                            act.activation(tile_of(z, j * 4 + slot * 2 + u), cvt[:, u, :], ACT.Silu)\
                                .then_inc(s["conv_done"], 1)
                with act.Fori(3, 7) as j:
                    for slot in range(2):
                        evacuate(j, slot)
                act.wait_ge(s["ba_sb"], l + 1)
                act.activation(beta[:, :, :], ba[:, :, 0:4], ACT.Sigmoid)
                act.activation(spa[:, :, :], spa[:, :, :], ACT.Exp)
                act.drain()
                act.activation(spa[:, :, :], spa[:, :, :], ACT.Ln, bias=one).then_inc(s["soft"], 1)
                for b in range(5):
                    n = 128 if b < 4 else NS
                    act.wait_ge(s["rows_mm"], l * 5 + b + 1)
                    a = 3 + 2 * (b % 2)
                    copy(k_rows[0:n, b, 256:512], ps[0:n, a, 0:256])
                    copy(vtok[0:n, b, 256:512], ps[0:n, a, 256:512]).then_inc(s["rows_v"], 1)
                act.wait_ge(s["conv_rows_mm"], l + 1)
                copy(conv_out[0:27, :], flat[0:27, 2560:2560 + CONV_CH]).then_inc(s["conv_rows"], 1)

            def squares(base, src, sqb, rnb, scale):
                for u in range(2):
                    act.wait_ge(s["gmm"], base + u + 1)
                    act.activation(sqb[:, u, :], src(u), ACT.Square).then_inc(s["gsq"], 1)
                for u in range(2):
                    act.wait_ge(s["gmm"], base + u + 3)
                    act.wait_ge(s["gdone"], base + u + 1)
                    act.activation(tok(rnb[:, u, :]), both(2 * u), ACT.Sqrt, bias=eps, scale=scale).then_inc(s["gsqrt"], 1)

            def two(bank):
                return ps[:, bank, 0:256].rearrange("p (h n) -> p h n", h=2)

            def chunk(l, c):
                it = l * 4 + c
                act.wait_ge(s["state_done"], l * 5 + c + 1)
                for i, name in enumerate(("qc", "kc", "vc")):
                    last = copy(m[name][:, :, :], z[:, 4 * i:4 * i + 4, ds(c * 128, 128)])
                last.then_inc(s["staged"], 1)
                act.wait_ge(s["dt_arg"], it + 1)
                act.activation(m["DT"][:, :, :], m["DT"][:, :, :], ACT.Exp)
                act.activation(m["eG"][:, :, :], ps[:, 2, :].rearrange("p (h n) -> p h n", h=4), ACT.Exp)
                act.activation(ecol[:, :], gc[:, :], ACT.Exp)
                act.activation(kde[:, :], kde[:, :], ACT.Exp).then_inc(s["exp_done"], 1)
                act.wait_ge(s["bege"], it + 1)
                act.wait_ge(s["tokm"], it + 1)
                for h in range(NH):
                    hs = slice(128 * h, 128 * h + 128)
                    copy(m["KB"][:, h, :], ps[:, 0, hs], bege[:, h:h + 1])
                    copy(m["KD"][:, h, :], ps[:, 0, hs], kde[:, h:h + 1])
                    last = copy(m["VB"][:, h, :], ps[:, 1, hs], m["bB"][:, h, 0:1])
                last.then_inc(s["kv_done"], 1)
                with act.Fori(1, 7) as k:
                    for a in range(2):
                        act.wait_ge(s["m_mm"], it * 12 + k * 2 + a - 1)
                        copy(m["M"][:, 2 * a:2 * a + 2, :], two(4 if a else 7)).then_inc(s["m_sb"], 1)
                act.wait_ge(s["w_mm"], it + 1)
                copy(m["nW"][:, :, :], ps[:, 7, :].rearrange("p (h n) -> p h n", h=4), -1.0).then_inc(s["nw_sb"], 1)
                act.wait_ge(s["o_mm"], it + 1)
                copy(hT[:, 0:4, ds(c * 128, 128)], ps[:, 3, :].rearrange("p (h n) -> p h n", h=4))

            def sample_chunk(l):
                act.wait_ge(s["state_done"], l * 5 + 5)
                for i, name in enumerate(("qc", "kc", "vc")):
                    last = copy(t[name][:, :, :], z[:, 4 * i:4 * i + 4, SEQ:NT])
                last.then_inc(s["x_act"], 1)
                act.wait_ge(s["x_dt"], l + 1)
                act.activation(t["DT"][0:NS], t["DT"][0:NS], ACT.Exp)
                act.activation(t["eG"][:, :, :], ps[:, 2, 0:128].rearrange("p (h n) -> p h n", h=4), ACT.Exp)
                act.activation(secol[0:NS, :], sgc[0:NS, :], ACT.Exp)
                act.activation(skde[0:NS, :], skde[0:NS, :], ACT.Exp).then_inc(s["x_act"], 1)
                act.wait_ge(s["x_bege"], l + 1)
                for h in range(NH):
                    hs = slice(128 * h, 128 * h + 128)
                    copy(t["KB"][0:NS, h, :], ps[0:NS, 0, hs], sbege[0:NS, h:h + 1])
                    copy(t["KD"][0:NS, h, :], ps[0:NS, 0, hs], skde[0:NS, h:h + 1])
                    last = copy(t["VB"][0:NS, h, :], ps[0:NS, 1, hs], t["bB"][0:NS, h, 0:1])
                last.then_inc(s["x_act"], 1)
                act.wait_ge(s["x_m"], l + 1)
                copy(t["M"][0:NS], ps[0:NS, 7, 0:128].rearrange("p (h n) -> p h n", h=4)).then_inc(s["x_act"], 1)
                act.wait_ge(s["x_w"], l + 1)
                copy(t["WQ"][:, :, :, 0:4], ps[:, 7, 0:128].rearrange("p (h b t) -> p h b t", h=4, b=8)).then_inc(s["x_act"], 1)

            def group_c(l, g):
                G = l * 2 + g
                for n in range(16):
                    act.wait_ge(s["ck_free"], G * 16 + n + 5)
                    act.wait_ge(s["cs_mm"], G * 16 + n + 1)
                    copy(c_kt[:, n % 2, 0, :], ps[:, 4 + 2 * (n % 2), :]).then_inc(s["kt_a"], 1)
                act.wait_ge(s["c_max"], G + 1)
                act.activation(c_s[:, :], c_s[:, :], ACT.Exp, bias=c_mx[:, 1:2], accum_out=c_mx[:, 2:3]).then_inc(s["c_exp"], 1)
                act.wait_ge(s["cpt_mm"], G + 1)
                copy(c_pt[:, 0:16, :], flat[:, 0:1024].rearrange("p (k n) -> p k n", k=16))
                copy(c_pt[0:NS, 16, :], ps[0:NS, 2, 0:64]).then_inc(s["cpt_sb"], 1)
                act.wait_ge(s["cv_free"], G * 16 + 20)
                copy(pv_rows[0:16, 0:4, :], flat[0:16, 2048:3072].rearrange("p (b n) -> p b n", b=4)).then_inc(s["c_pv"], 1)

            def sample_b(l):
                for b in range(NB_S):
                    act.wait_ge(s["bk_free"], l * 8 + b + 3)
                    act.wait_ge(s["bs_mm"], l * 8 + b + 1)
                    copy(b_kt[:, b % 2, 0, :], flat[:, 2048:2048 + KEYS_B]).then_inc(s["bkt_a"], 1)
                act.wait_ge(s["b_max"], l + 1)
                act.activation(b_s[:, :], b_s[:, :], ACT.Exp, bias=c_mx[:, 1:2], accum_out=c_mx[:, 2:3]).then_inc(s["b_exp"], 1)
                act.wait_ge(s["bpt_mm"], l + 1)
                copy(b_pt[:, 0:4, :], flat[:, 0:512].rearrange("p (k n) -> p k n", k=4))
                copy(b_pt[0:96, 4:8, :], flat[0:96, 512:1024].rearrange("p (k n) -> p k n", k=4))
                copy(b_pt[0:NS, 8, :], ps[0:NS, 2, 0:128]).then_inc(s["bpt_sb"], 1)
                act.wait_ge(s["bv_free"], l * 8 + 10)
                copy(pv_rows[0:16, :, :], flat[0:16, 2048:4096].rearrange("p (b n) -> p b n", b=8)).then_inc(s["b_pv"], 1)

            def prompt(l):
                for u in range(33):
                    if u < 32:
                        wid = 128 * (u % 4 + 1)
                        act.wait_ge(s["p_max"], l * 32 + u + 1)
                        for mp in range(maps(u)):
                            row = p_s[:, u % 2, mp, 0:wid]
                            last = act.activation(row, row, ACT.Exp, bias=p_mx[:, u % 2, 2 + mp:3 + mp],
                                                  accum_out=p_mx[:, u % 2, 4 + mp:5 + mp])
                        last.then_inc(s["p_exp"], 1)
                    if u >= 1:
                        v = u - 1
                        n = v % 4 + 1
                        act.wait_ge(s["ppt_mm"], l * 32 + v + 1)
                        if v >= 2:
                            act.wait_ge(s["po_mm"], l * 32 + v - 1)
                        copy(p_pt[:, v % 2, 0:n, :], ps[:, 4 + v % 2, 0:128 * n].rearrange("p (k n) -> p k n", k=n))\
                            .then_inc(s["ppt_sb"], 1)

            with act.Fori(0, DEPTH) as l:
                norm(l * 3)
                ffn(l, 0)
                norm(l * 3 + 1)
                project(l)
                for base in (0, 4):
                    with act.Fori(0, 2) as j:
                        act.drain()
                        squares(l * 14 + base + j * 2, lambda u: tile_of(z, j * 2 + base + u), sq, rn, 1.0)
                act.wait_ge(s["gdone"], l * 14 + 10)
                act.wait_ge(s["rows_out"], l * 160 + 160)
                with act.Fori(0, 4) as c:
                    chunk(l, c)
                sample_chunk(l)
                act.activation(z[:, 12:16, :], z[:, 12:16, :], ACT.Silu)
                act.wait_ge(s["x_so"], l + 1)
                act.wait_ge(s["st_out"], l * 64 + 64)
                alone(act)
                act.drain()
                with act.Fori(0, 2) as j:
                    squares(l * 14 + 8 + j * 2, lambda u: tile_of(hT, j * 2 + u), sq2, rn2, 1.0 / DK)
                with act.Fori(0, 2) as g:
                    group_c(l, g)
                sample_b(l)
                prompt(l)
                act.wait_ge(s["p_out"], l * 32 + 32)
                squares(l * 14 + 12, lambda u: hT[:, 6 + u, :], sq2, rn2, 1.0 / 64)
                norm(l * 3 + 2)
                ffn(l, 1)
            norm(6)

        @block.vector
        def _(dve):
            for name in ("gu_free", "down_free", "proj_v", "gdone"):
                dve.sem_inc(s[name], 2)
            cp = dve.tensor_copy
            stt = dve.scalar_tensor_tensor

            dve.memset(small[:, 32:160], 0.0)
            dve.drain()
            dve.wait_ge(s["in_const"], 16)
            dve.wait_ge(s["in_lam"], 16 * 8)
            for i in range(2):
                dve.tensor_tensor(lam_prod[:, i, :], lam_rows[:, 2 * i, :], lam_rows[:, 2 * i + 1, :], ALU.mult)
            dve.drain()
            for i in range(2):
                for l in range(DEPTH):
                    last = dve.reduce_sum(small[:, 16 + 2 * i + l:17 + 2 * i + l], lam_prod[:, i, 32 * l:32 * l + 32], AX)
            last.then_inc(s["lam_sums"], 1)
            dve.wait_ge(s["lam_exp"], 1)
            dve.tensor_tensor(lam_all, lam_sum[:, 0:2], lam_sum[:, 2:4], ALU.subtract)
            dve.drain()
            dve.tensor_tensor(lam_all, lam_all, C("lam0"), ALU.add)
            for i in range(1, 6):
                n = 128 if i < 5 else NS
                dve.wait_ge(s["setup_mm"], i)
                at = 1024 * (i % 2)
                cp(xT[:, :, 128 * (i - 1):128 * (i - 1) + n],
                   flat[:, at:at + 8 * n].rearrange("p (k n) -> p k n", k=KD)).then_inc(s["setup_ev"], 1)
            dve.drain().then_inc(s["x_new"], 1)
            dve.wait_ge(s["setup_mm"], 6)
            cp(cols_conv[:, :], ps[:, 0, 0:96])
            cp(cols_norm[:, :], ps[:, 0, 96:156]).then_inc(s["setup_ev"], 1)
            for c in range(5):
                i, n = 7 + c, min(512, U_TAB - 512 * c)
                dve.wait_ge(s["setup_mm"], i)
                cp(table[0:8, 512 * c:512 * c + n], ps[0:8, 2 * (i % 2), 0:n]).then_inc(s["setup_ev"], 1)
            for h in range(8):
                i = 12 + h
                dve.wait_ge(s["setup_mm"], i)
                cp(strips[:, h, :], ps[:, 2 * (i % 2), :]).then_inc(s["setup_ev"], 1)
            dve.wait_ge(s["in_rows"], 16 * 5 * T_S)
            for g in range(2):
                dve.tensor_tensor(bias_cn[:, g, :].rearrange("p (b t) -> p b t", b=8), per_head(win_c[:, PAST:PAST + T_S], 8),
                                  over(C("offc")[:, 8 * g:8 * g + 8], T_S), ALU.add)
            dve.tensor_tensor(bias_bn[:, :].rearrange("p (b t) -> p b t", b=8), per_head(win_b[:, PAST:PAST + T_S], 8),
                              over(C("offb"), T_S), ALU.add)
            cp(bias_b[:, 0:512].rearrange("p (r k) -> p r k", r=4), win_b[:, 1536:PAST].rearrange("p (k r) -> p r k", r=4))
            cp(bias_b[:, 512:KEYS_B].rearrange("p (r k) -> p r k", r=4),
               win_b[:, 0:1536].rearrange("p (k r) -> p r k", r=16)[:, 0:4, :])
            cp(bias_c[:, 0:PAST].rearrange("p (c r k) -> p c r k", c=4, r=4),
               win_c[:, 0:PAST].rearrange("p (c k r) -> p c r k", c=4, r=4))
            dve.wait_ge(s["in_pages"], 64)
            cp(row_f[:, :], page_of[:, :])
            dve.drain()
            dve.tensor_scalar(row_f[:, :], row_f[:, :], float(PAGE // 4), C("p32"), ALU.mult, ALU.add)
            dve.drain()
            for l in range(DEPTH):
                dve.tensor_scalar(key_rows[:, l, :], row_f[:, :], float(l * POOL_PAGES * PAGE // 4), None, ALU.add)
            dve.drain()

            def norm(n, gains):
                dve.wait_ge(s["rms"], n + 1)
                rstd = gated[:, 0, :]
                dve.reciprocal(rstd, rstd)
                dve.drain()
                for k in range(KD):
                    stt(hT[:, k, :], xT[:, k, :], gains[:, k:k + 1], rstd, ALU.mult, ALU.mult).then_inc(s["h_done"], 1)

            def ffn(l, w):
                it = l * 2 + w
                with dve.Fori(0, 11) as j:
                    for slot in range(2):
                        dve.wait_ge(s["silu"], it * 22 + j * 2 + slot + 1)
                        dst = hidden[:, ds(j * 2 + slot, 1), :].rearrange("p a (h n) -> p (a h) n", h=2)
                        dve.tensor_tensor(dst, tok(gated[:, slot, :]), both(4 * slot + 2), ALU.mult).then_inc(s["gu_free"], 1)
                with dve.Fori(0, 4) as j:
                    for u in range(2):
                        dve.wait_ge(s["down_done"], it * 8 + j * 2 + u + 2)
                        x = xT[:, ds(j * 2 + u, 1), :].rearrange("p a (h n) -> p (a h) n", h=2)
                        stt(x, both(4 * u), 0.5, x, ALU.mult, ALU.add).then_inc(s["down_free"], 1)
                dve.drain().then_inc(s["x_new"], 1)

            def tile_of(v, i):
                return v[:, ds(i, 1), :].rearrange("p a n -> p (a n)")

            def project(l):
                def evacuate(j, slot):
                    dve.wait_ge(s["proj_done"], l * 28 + j * 4 + slot * 2 + 2)
                    dst = z[:, ds(j * 4 + slot * 2 + 1, 1), :].rearrange("p a (h n) -> p (a h) n", h=2)
                    cp(dst, both(4 * slot + 2)).then_inc(s["proj_v"], 1)

                def convolve(c, u):
                    zc, acc = tile_of(z, c), cvt[:, u, :]
                    zs = zc[:, SEQ:NT].rearrange("p (b t) -> p b t", b=8)
                    acc_s = acc[:, SEQ:NT].rearrange("p (b t) -> p b t", b=8)
                    xc = xs[:, ds(c, 1), :, :].rearrange("p a b t -> p (a b) t")
                    tail = conv_tail[:, ds(c, 1), :].rearrange("p a n -> p (a n)")
                    cp(tail[:, 0:3], zc[:, SEQ - 3:SEQ])
                    cp(tail[:, 3:27].rearrange("p (b j) -> p b j", b=8), zs[:, :, 1:4])
                    cp(xc[:, :, 3:7], zs)
                    dve.wait_ge(s["conv_done"], l * 12 + c + 1)
                    for tap in (3, 2, 1, 0):
                        cw = lay_conv[:, ds(c + 12 * tap, 1)]
                        d = 3 - tap
                        if tap == 3:
                            dve.tensor_scalar(acc[:, 0:SEQ], zc[:, 0:SEQ], cw, None, ALU.mult)
                            dve.drain()
                            last = dve.tensor_scalar(acc_s, xc[:, :, 3:7], cw, None, ALU.mult)
                        else:
                            dve.drain()
                            stt(acc[:, d:SEQ], zc[:, 0:SEQ - d], cw, acc[:, d:SEQ], ALU.mult, ALU.add)
                            last = stt(acc_s, xc[:, :, tap:tap + 4], cw, acc_s, ALU.mult, ALU.add)
                    last.then_inc(s["conv_acc"], 1)

                with dve.Fori(0, 3) as j:
                    for slot in range(2):
                        evacuate(j, slot)
                        dve.wait_ge(s["proj_a"], l * 14 + j * 2 + slot + 3)
                        convolve(j * 4 + slot * 2, 0)
                        convolve(j * 4 + slot * 2 + 1, 1)
                with dve.Fori(3, 7) as j:
                    for slot in range(2):
                        evacuate(j, slot)
                dve.drain().then_inc(s["conv_tail"], 1)
                dve.wait_ge(s["ba_mm"], l + 1)
                cp(ba[:, 0:4, :], ps[:, 0, 0:32].rearrange("p (b n) -> p b n", b=4))
                cp(ba[0:NS, 4, :], ps[0:NS, 0, 32:40])
                dve.drain()
                dve.tensor_tensor(spb[:, :, :], ba[:, :, 4:8], per_head(dtb, 5), ALU.add)
                dve.drain()
                stt(spa[:, :, :], spb[:, :, :], -1.0, spb[:, :, :], ALU.mult, ALU.min).then_inc(s["ba_sb"], 1)
                for b in range(5):
                    n = 128 if b < 4 else NS
                    dve.wait_ge(s["rows_mm"], l * 5 + b + 1)
                    a = 2 + 2 * (b % 2)
                    cp(k_rows[0:n, b, 0:256], ps[0:n, a, 0:256])
                    cp(vtok[0:n, b, 0:256], ps[0:n, a, 256:512]).then_inc(s["rows_a"], 1)
                dve.wait_ge(s["soft"], l + 1)
                stt(spb[:, :, :], spb[:, :, :], 0.0, spa[:, :, :], ALU.max, ALU.add)
                dve.drain()
                stt(gdec[:, :, :], spb[:, :, :], -1.0, per_head(ea, 5), ALU.mult, ALU.mult)

            def inverse_root(base, u, rnb):
                dve.wait_ge(s["gsqrt"], base + u + 3)
                dve.reciprocal(rnb[:, u, :], rnb[:, u, :])
                dve.drain()

            def four(bank, n=128):
                return ps[:, bank, 0:4 * n].rearrange("p (h n) -> p h n", h=4)

            def two(bank):
                return ps[:, bank, 0:256].rearrange("p (h n) -> p h n", h=2)

            def chunk(l, c):
                it = l * 4 + c
                cp(m["gB"][:, :, :], over(gdec[:, ds(c, 1), :].rearrange("p a h -> p (a h)"), 128))
                cp(m["bB"][:, :, :], over(beta[:, ds(c, 1), :].rearrange("p a h -> p (a h)"), 128)).then_inc(s["gb"], 1)
                dve.wait_ge(s["decay_mm"], it + 1)
                cp(gc[:, :], ps[:, 4, 0:4])
                dve.drain()
                for h in range(NH):
                    stt(m["DT"][:, h, :], ps[:, 2, 128 * h:128 * h + 128], gc[:, h:h + 1], C("neg"), ALU.subtract, ALU.add)
                dve.tensor_tensor(kde[:, :], four(2)[:, :, 127], gc[:, :], ALU.subtract).then_inc(s["dt_arg"], 1)
                dve.wait_ge(s["exp_done"], it + 1)
                dve.tensor_tensor(bege[:, :], m["bB"][:, :, 0], ecol[:, :], ALU.mult).then_inc(s["bege"], 1)
                dve.wait_ge(s["kkqk"], it + 1)
                dve.tensor_tensor(m["LT"][:, :, :], m["DT"][:, :, :], four(5), ALU.mult)
                dve.tensor_tensor(m["QKT"][:, :, :], m["DT"][:, :, :], four(6), ALU.mult)
                dve.tensor_tensor(m["qc"][:, :, :], m["qc"][:, :, :], m["eG"][:, :, :], ALU.mult)
                dve.drain()
                dve.tensor_tensor(m["LT"][:, :, :], m["LT"][:, :, :], four(3), ALU.mult)
                dve.drain()
                dve.tensor_tensor(m["LK"][:, :, :], m["LT"][:, :, :], per_head(C("lm")[:, 0:128]), ALU.mult)
                dve.drain()
                dve.tensor_tensor(m["U"][:, :, :], per_head(C("ident")), m["LK"][:, :, :], ALU.subtract).then_inc(s["u_up"], 2)
                dve.drain()
                dve.tensor_tensor(m["LK"][:, :, :], m["LT"][:, :, :], per_head(C("lm")[:, 128:256]), ALU.mult)
                dve.wait_ge(s["t_mm"], it + 1)
                cp(m["T"][:, :, :].rearrange("p (a h) n -> p a (h n)", a=2), ps[:, 2:4, 0:256]).then_inc(s["t_up"], 2)

                def level(k, last=False):
                    if not last:
                        dve.wait_ge(s["m_mm"], it * 12 + k * 2)
                        dve.tensor_tensor(m["LK"][:, :, :], m["LT"][:, :, :], per_head(C("lm")[:, ds(k * 128 + 128, 128)]),
                                          ALU.mult)
                    dve.drain()
                    for a in range(2):
                        hs = slice(2 * a, 2 * a + 2)
                        if not last:
                            dve.wait_ge(s["tm_mm"], it * 10 + k * 2 + a - 1)
                            dve.tensor_tensor(m["T"][:, hs], m["T"][:, hs], two(2 + a), ALU.subtract).then_inc(s["t_up"], 1)
                        dve.wait_ge(s["mu_mm"], it * 12 + k * 2 + a - 1)
                        dve.tensor_tensor(m["U"][:, hs], m["U"][:, hs], two(5 + a), ALU.subtract).then_inc(s["u_up"], 1)

                with dve.Fori(1, 6) as k:
                    level(k)
                level(6, last=True)
                dve.wait_ge(s["vn_mm"], it + 1)
                cp(m["VN"][:, :, :], four(2)).then_inc(s["vn_sb"], 1)
                dve.wait_ge(s["s_mm"], it + 1)
                for h in range(NH):
                    last = stt(m["S"][:, h, :], m["S"][:, h, :], m["eG"][:, h, 127:128], ps[:, 4, 128 * h:128 * h + 128],
                               ALU.mult, ALU.add)
                last.then_inc(s["state_done"], 1)

            def sample_chunk(l):
                q = slice(0, NS)

                def four_s(bank):
                    return ps[0:NS, bank, 0:128].rearrange("p (h n) -> p h n", h=4)

                cp(t["gB"][q], over(gdec[q, 4, :], 128))
                cp(t["bB"][q], over(beta[q, 4, :], NS)).then_inc(s["x_gb"], 1)
                dve.wait_ge(s["x_decay"], l + 1)
                cp(sgc[q, :], ps[q, 4, 0:4])
                dve.drain()
                for h in range(NH):
                    stt(t["DT"][q, h, :], ps[q, 2, NS * h:NS * h + NS], sgc[q, h:h + 1], C("neg4", NS), ALU.subtract, ALU.add)
                dve.tensor_tensor(skde[q, :], ps[q, 4, 4:8], sgc[q, :], ALU.subtract).then_inc(s["x_dt"], 1)
                dve.wait_ge(s["x_act"], l * 5 + 2)
                dve.tensor_tensor(sbege[q, :], t["bB"][q, :, 0], secol[q, :], ALU.mult).then_inc(s["x_bege"], 1)
                dve.wait_ge(s["x_kkqk"], l + 1)
                dve.tensor_tensor(t["LT"][q], t["DT"][q], four_s(5), ALU.mult)
                dve.tensor_tensor(t["QKT"][q], t["DT"][q], four_s(6), ALU.mult)
                dve.drain()
                dve.tensor_tensor(t["LT"][q], t["LT"][q], four_s(3), ALU.mult)
                dve.drain()
                dve.tensor_tensor(t["LK"][q], t["LT"][q], per_head(C("lm", NS)[:, 0:NS]), ALU.mult)
                dve.drain()
                dve.tensor_tensor(t["U"][q], per_head(C("ident", NS)[:, 0:NS]), t["LK"][q], ALU.subtract).then_inc(s["x_u"], 1)
                dve.drain()
                dve.tensor_tensor(t["LK"][q], t["LT"][q], per_head(C("lm", NS)[:, 128:128 + NS]), ALU.mult)
                dve.wait_ge(s["x_t"], l + 1)
                cp(t["T"][q], four_s(6)).then_inc(s["x_lt"], 1)
                dve.wait_ge(s["x_mu"], l + 1)
                dve.tensor_tensor(t["U"][q], t["U"][q], four_s(5), ALU.subtract).then_inc(s["x_u"], 1)
                dve.tensor_tensor(t["WQ"][:, :, :, 4:8], t["qc"][:, :, :].rearrange("p h (b t) -> p h b t", b=8),
                                  t["eG"][:, :, :].rearrange("p h (b t) -> p h b t", b=8), ALU.mult).then_inc(s["x_qe"], 1)
                dve.wait_ge(s["x_ws"], l + 1)
                wsq = ps[:, 2, 0:256].rearrange("p (h b u) -> p h b u", h=4, b=8)
                cp(t["QS"][:, :, :].rearrange("p h (b t) -> p h b t", b=8), wsq[:, :, :, 4:8])
                dve.tensor_scalar(t["nW"][:, :, :].rearrange("p h (b t) -> p h b t", b=8), wsq[:, :, :, 0:4], -1.0, None,
                                  ALU.mult).then_inc(s["x_nw"], 1)
                for h in range(NH):
                    last = t["eG"][:, h, :].rearrange("p (b t) -> p b t", b=8)[:, :, 3]
                    dve.tensor_tensor(t["st"][:, h], t["st"][:, h], over(last, 128), ALU.mult)
                dve.wait_ge(s["x_vn"], l + 1)
                cp(t["VN"][q], ps[q, 3, :].rearrange("p (h n) -> p h n", h=4)).then_inc(s["x_vnsb"], 1)
                dve.wait_ge(s["x_o"], l + 1)
                dve.tensor_tensor(hT[:, 0:4, SEQ:NT], t["QS"][:, :, :], four(4, NS), ALU.add).then_inc(s["x_so"], 1)
                dve.drain()
                for h in range(NH):
                    if h >= 2:
                        dve.wait_ge(s["x_s"], l * 4 + h - 1)
                    dve.tensor_tensor(vblk[h % 2][q], per_head(t["VN"][q, h, :], 8), over(C("bsel", NS), 128),
                                      ALU.mult).then_inc(s["x_vb"], 1)
                    if h >= 1:
                        add_state(l, h - 1)
                add_state(l, 3)
                dve.wait_ge(s["delta_out"], l * 16 + 16)
                alone(dve)

            def add_state(l, h):
                dve.wait_ge(s["x_s"], l * 4 + h + 1)
                at = 3072 if h % 2 else 0
                dve.tensor_tensor(t["st"][:, h], t["st"][:, h], flat[:, at:at + 1024].rearrange("p (b v) -> p b v", b=8),
                                  ALU.add).then_inc(s["st_new"], 1)

            def group_c(l, g):
                G = l * 2 + g
                scale = 32 ** -0.5
                for pair in range(2):
                    for quad in range(4):
                        h2, mp = quad // 2, quad % 2
                        rows = slice(32 * quad, 32 * quad + 32)
                        off = 128 * pair + (2 * pair + h2) * 8 + mp * 4
                        dst = qc_all.rearrange("p (b x) -> p b x", b=4)[rows, :, off:off + 4]
                        src = z[rows, 22 + pair, ds(g * 16 + SEQ, 16)].rearrange("p (b t) -> p b t", b=4)
                        last = cp(dst, src)
                last.then_inc(s["cq"], 1)
                for n in range(16):
                    dve.wait_ge(s["ck_free"], G * 16 + n + 5)
                    dve.wait_ge(s["cs_mm"], G * 16 + n + 1)
                    cp(c_kt[:, n % 2, 1, :], ps[:, 5 + 2 * (n % 2), :]).then_inc(s["kt_v"], 1)
                dve.wait_ge(s["csn"], G + 1)
                stt(c_s[:, 0:PAST], flat[:, 0:PAST], scale, bias_c[:, 0:PAST], ALU.mult, ALU.add)
                stt(c_s[:, PAST:PAST + NS], ps[:, 4, 0:NS], scale, bias_cn[:, ds(g, 1), :].rearrange("p a n -> p (a n)"),
                    ALU.mult, ALU.add)
                dve.drain()
                dve.reduce_max(c_mx[:, 0:1], c_s[:, :], AX)
                dve.drain()
                dve.tensor_scalar(c_mx[:, 1:2], c_mx[:, 0:1], -1.0, None, ALU.mult).then_inc(s["c_max"], 1)
                dve.wait_ge(s["c_exp"], G + 1)
                dve.reciprocal(c_mx[:, 3:4], c_mx[:, 2:3])
                dve.drain()
                dve.tensor_scalar(comb[:, :], C("comb"), c_mx[:, 3:4], sign, ALU.mult, ALU.mult).then_inc(s["comb"], 1)
                dve.wait_ge(s["c_pv_mm"], G + 1)
                for pair in range(2):
                    for h2 in range(2):
                        rows = slice(64 * h2, 64 * h2 + 64)
                        dst = hT[rows, 6 + pair, ds(g * 16 + SEQ, 16)].rearrange("p (b t) -> p b t", b=4)
                        at = 16 * pair + 4 * (2 * pair + h2)
                        src = ps[rows, 6, 0:128].rearrange("p (b x) -> p b x", b=4)[:, :, at:at + 4]
                        last = cp(dst, src)
                last.then_inc(s["c_group_done"], 1)

            def sample_b(l):
                scale = 64 ** -0.5
                dve.memset(qb_all, 0.0)
                dve.drain()
                for pair in range(2):
                    for h2 in range(2):
                        rows = slice(64 * h2, 64 * h2 + 64)
                        off = 128 * pair + (2 * pair + h2) * 4
                        dst = qb_all.rearrange("p (b x) -> p b x", b=8)[rows, :, off:off + 4]
                        last = cp(dst, z[rows, 16 + pair, SEQ:NT].rearrange("p (b t) -> p b t", b=8))
                last.then_inc(s["bq"], 1)
                for b in range(NB_S):
                    dve.wait_ge(s["bk_free"], l * 8 + b + 3)
                    dve.wait_ge(s["bs_mm"], l * 8 + b + 1)
                    cp(b_kt[:, b % 2, 1, :], flat[:, 3072:3072 + KEYS_B]).then_inc(s["bkt_v"], 1)
                dve.wait_ge(s["bsn"], l + 1)
                stt(b_s[:, 0:KEYS_B], flat[:, 0:KEYS_B], scale, bias_b[:, :], ALU.mult, ALU.add)
                stt(b_s[:, KEYS_B:KEYS_B + NS], ps[:, 2, 0:NS], scale, bias_bn[:, :], ALU.mult, ALU.add)
                dve.drain()
                dve.reduce_max(c_mx[:, 0:1], b_s[:, :], AX)
                dve.drain()
                dve.tensor_scalar(c_mx[:, 1:2], c_mx[:, 0:1], -1.0, None, ALU.mult).then_inc(s["b_max"], 1)
                dve.wait_ge(s["b_exp"], l + 1)
                dve.reciprocal(c_mx[:, 3:4], c_mx[:, 2:3])
                dve.drain()
                dve.tensor_scalar(b_s[:, :], b_s[:, :], c_mx[:, 3:4], None, ALU.mult).then_inc(s["bp"], 1)
                dve.wait_ge(s["b_pv_mm"], l + 1)
                for pair in range(2):
                    for h2 in range(2):
                        rows = slice(64 * h2, 64 * h2 + 64)
                        dst = hT[rows, 4 + pair, SEQ:NT].rearrange("p (b t) -> p b t", b=8)
                        at = 16 * pair + 4 * (2 * pair + h2)
                        src = ps[rows, 0, 0:256].rearrange("p (b x) -> p b x", b=8)[:, :, at:at + 4]
                        last = cp(dst, src)
                last.then_inc(s["b_out"], 1)

            def prompt(l):
                def logits(u):
                    par, wid, n = u % 2, 128 * (u % 4 + 1), maps(u)
                    dve.wait_ge(s["p_mm"], l * 32 + u + 1)
                    if u >= 2:
                        dve.wait_ge(s["ppt_mm"], l * 32 + u - 1)
                    scale = (64 if u < 16 else 32) ** -0.5
                    for mp in range(n):
                        stt(p_s[:, par, mp, 0:wid], ps[:, 2 * par + mp, 0:wid], scale, strips[:, u // 4, SEQ - wid:SEQ],
                            ALU.mult, ALU.add)
                    dve.drain()
                    dve.reduce_max(p_mx[:, par, 0:n], p_s[:, par, 0:n, 0:wid], AX)
                    dve.drain()
                    dve.tensor_scalar(p_mx[:, par, 2:2 + n], p_mx[:, par, 0:n], -1.0, None, ALU.mult).then_inc(s["p_max"], 1)

                def weights(u):
                    par, wid, n = u % 2, 128 * (u % 4 + 1), maps(u)
                    dve.wait_ge(s["p_exp"], l * 32 + u + 1)
                    dve.reciprocal(p_mx[:, par, 6:6 + n], p_mx[:, par, 4:4 + n])
                    dve.drain()
                    p0, p1 = p_s[:, par, 0, 0:wid], p_s[:, par, 1, 0:wid]
                    last = dve.tensor_scalar(p0, p0, p_mx[:, par, 6:7], None, ALU.mult)
                    if n == 2:
                        dve.tensor_scalar(p_mx[:, par, 5:6], p_mx[:, par, 7:8], lam, -1.0, ALU.mult, ALU.mult)
                        dve.drain()
                        last = stt(p0, p1, p_mx[:, par, 5:6], p0, ALU.mult, ALU.add)
                    last.then_inc(s["p_soft"], 1)

                def result(u):
                    head = u // 4
                    rows = slice(64 * (head % 2), 64 * (head % 2) + 64)
                    dve.wait_ge(s["po_mm"], l * 32 + u + 1)
                    cp(hT[rows, 4 + head // 2, 128 * (u % 4):128 * (u % 4) + 128], ps[rows, 6 + u % 2, 0:128])\
                        .then_inc(s["p_out"], 1)

                for u in range(34):
                    if u < 32:
                        logits(u)
                    if 1 <= u < 33:
                        weights(u - 1)
                    if u >= 2:
                        result(u - 2)

            with dve.Fori(0, DEPTH) as l:
                cp(lay_conv[:, :], cols_conv[:, ds(l * 48, 48)])
                cp(lay_norm[:, :], cols_norm[:, ds(l * LV, LV)])
                cp(lam, lam_all[:, ds(l, 1)])
                cp(lay_rows[:, :], key_rows[:, ds(l, 1), :].rearrange("p l n -> p (l n)"))
                cp(ea, a_log_c[:, ds(l * 4, 4)])
                cp(dtb, dt_c[:, ds(l * 4, 4)])
                cp(lay_ba[:, :, :], all_ba[:, ds(l, 1)].rearrange("p l k n -> p (l k) n"))
                dve.drain()
                dve.tensor_scalar(sign, C("m1"), lam, -1.0, ALU.mult, ALU.mult)
                dve.tensor_tensor(cnorm, lay_norm[:, 25:26], C("oml")[:, ds(l, 1)], ALU.mult)
                dve.drain()
                dve.tensor_tensor(sign, sign, C("m0"), ALU.add).then_inc(s["layer_vecs"], 1)
                norm(l * 3, lay_norm[:, 0:8])
                ffn(l, 0)
                dve.wait_ge(s["conv_in_mm"], l + 1)
                cp(xs[:, :, :, 0:3], ps[:, 6, 0:288].rearrange("p (c b j) -> p c b j", c=12, b=8))
                norm(l * 3 + 1, lay_norm[:, 8:16])
                project(l)
                with dve.Fori(0, 2) as j:
                    for u in range(2):
                        inverse_root(l * 14 + j * 2, u, rn)
                        q = tile_of(z, j * 2 + u)
                        stt(q, q, DK ** -0.5, rn[:, u, :], ALU.mult, ALU.mult).then_inc(s["gdone"], 1)
                with dve.Fori(0, 2) as j:
                    for u in range(2):
                        inverse_root(l * 14 + 4 + j * 2, u, rn)
                        k = tile_of(z, j * 2 + u + 4)
                        dve.tensor_tensor(k, k, rn[:, u, :], ALU.mult).then_inc(s["gdone"], 1)
                dve.wait_ge(s["rows_out"], l * 160 + 160)
                alone(dve)
                dve.drain()
                dve.memset(m["S"][:, :, :], 0.0).then_inc(s["state_done"], 1)
                with dve.Fori(0, 4) as c:
                    chunk(l, c)
                sample_chunk(l)
                with dve.Fori(0, 2) as j:
                    for u in range(2):
                        inverse_root(l * 14 + 8 + j * 2, u, rn2)
                        o = tile_of(hT, j * 2 + u)
                        stt(o, o, lay_norm[:, 24:25], rn2[:, u, :], ALU.mult, ALU.mult)
                        dve.drain()
                        dve.tensor_tensor(o, o, tile_of(z, j * 2 + u + 12), ALU.mult).then_inc(s["gdone"], 1)
                dve.memset(qc_all, 0.0)
                dve.drain()
                with dve.Fori(0, 2) as g:
                    group_c(l, g)
                sample_b(l)
                prompt(l)
                for u in range(2):
                    inverse_root(l * 14 + 12, u, rn2)
                    o = hT[:, 6 + u, :]
                    stt(o, o, cnorm, rn2[:, u, :], ALU.mult, ALU.mult).then_inc(s["gdone"], 1)
                for o in range(8):
                    dve.wait_ge(s["out_done"], l * 8 + o + 1)
                    dve.tensor_tensor(tok(xT[:, o, :]), tok(xT[:, o, :]), both(2 * (o % 4)), ALU.add).then_inc(s["x_out"], 1)
                dve.drain().then_inc(s["x_new"], 1)
                norm(l * 3 + 2, lay_norm[:, 16:24])
                ffn(l, 1)
            norm(6, cols_norm[:, 2 * LV:2 * LV + 8])
            for b in range(5):
                n = 128 if b < 4 else NS
                dve.wait_ge(s["y_mm"], b + 1)
                at = 1024 * (b % 2)
                cp(y_rows[0:n, b, :], flat[0:n, at:at + 1024]).then_inc(s["y_rows"], 1)


NAMES = ("x_prompt", "x_sample", "state_delta", "state_conv", "cache_win_k", "cache_win_v", "cache_k", "cache_v",
         "page_table", "w_in", "conv_w", "a_log", "dt_bias", "a_norm_w", "lambda_q1", "lambda_k1", "lambda_q2",
         "lambda_k2", "c_norm_w", "rel_bias", "w_out", "norm_ffn1", "w1_gate", "w1_up", "w1_down", "norm_mix",
         "norm_ffn2", "w2_gate", "w2_up", "w2_down", "final_norm")
OUTS = (("y_p", (1, SEQ, D)), ("y_s", (NB_S, T_S, D)), ("delta_p", (DEPTH, 1, NH, DK, DK)),
        ("delta_s", (DEPTH, NB_S, NH, DK, DK)), ("conv_p", (DEPTH, 1, 3, CONV_CH)), ("conv_s", (DEPTH, NB_S, 3, CONV_CH)),
        ("wk_p", (DEPTH, 1, SEQ, 4, 64)), ("wk_s", (DEPTH, NB_S, T_S, 4, 64)), ("wv_p", (DEPTH, 1, SEQ, 4, 64)),
        ("wv_s", (DEPTH, NB_S, T_S, 4, 64)), ("k_p", (DEPTH, 1, SEQ, 4, 64)), ("k_s", (DEPTH, NB_S, T_S, 4, 64)),
        ("v_p", (DEPTH, 1, SEQ, 4, 64)), ("v_s", (DEPTH, NB_S, T_S, 4, 64)))


def kernel(**inputs):
    import concourse.bacc as bacc
    from concourse.bass_utils import run_bass_kernel_spmd

    nc = bacc.Bacc("TRN2", target_bir_lowering=False, num_devices=1)
    consts, buckets, pick = constant_arrays()
    given = {name: inputs[name] for name in NAMES}
    given.update(consts=consts, buckets=buckets, pick=pick)
    arrays, handles = {}, {}
    for name, value in given.items():
        a = np.ascontiguousarray(value)
        arrays["in_" + name] = a
        handles[name] = nc.dram_tensor("in_" + name, a.shape, mybir.dt.from_np(a.dtype), kind="ExternalInput").ap()
    outs = {name: nc.dram_tensor("out_" + name, shape, F32, kind="ExternalOutput").ap() for name, shape in OUTS}
    scratch = nc.dram_tensor("bias_tables", (8, U_TAB), F32, kind="Internal").ap()
    trunk(nc, handles, outs, scratch)
    r = run_bass_kernel_spmd(nc, [arrays], core_ids=[0])
    return tuple(r.results[0]["out_" + name] for name, _ in OUTS)
```

```python
from contextlib import ExitStack

import numpy as np

import concourse.bass as bass
from concourse import mybir

F32 = mybir.dt.float32
I32 = mybir.dt.int32
U32 = mybir.dt.uint32
ACT = mybir.ActivationFunctionType
ALU = mybir.AluOpType
AX = mybir.AxisListType.X
ds = bass.ds

D, DEPTH, FF, EPS = 1024, 2, 2816, 1e-6
SEQ, NB_S, T_S = 512, 8, 4
NS = NB_S * T_S
NT = SEQ + NS
HALF = NT // 2
KD = D // 128
NF = FF // 128
NH, DK, CONV_CH, CONV_W = 4, 128, 1536, 4
D_IN = 3592
BA_COL, BC_COL = 2048, 2056
NZ = 28
PAST, PAGE, PAGES, POOL_PAGES = 2048, 128, 16, 160
U_TAB = 2304
U_MAX = PAST + T_S - 1
NEG = -1.0e30
RING = 4
ARENA = 9904
KEYS_B = 896
LV = 26


def columns():
    at, where = 0, {}
    for name, n in (("ident", 128), ("ones", 128), ("tri", 128), ("neg", 128), ("blk64", 128), ("flip", 128),
                    ("lm", 7 * 128), ("tri4", 32), ("neg4", 32), ("blk4", 32), ("bsel", 8), ("comb", 64),
                    ("offc", 16), ("offb", 8), ("m0", 1), ("m1", 1), ("eps", 1), ("one", 1), ("lam0", 2), ("oml", 2), ("p32", 1)):
        where[name] = (at, at + n)
        at += n
    return where, at


def constant_arrays():
    where, n = columns()
    c = np.zeros((128, n), np.float32)

    def put(name, a):
        lo, hi = where[name]
        c[:a.shape[0], lo:hi] = a.reshape(a.shape[0], -1)

    p = np.arange(128)
    put("ident", np.eye(128))
    put("ones", np.ones((128, 128)))
    put("tri", (p[:, None] <= p[None, :]).astype(np.float32))
    put("neg", np.where(p[:, None] <= p[None, :], 0.0, NEG))
    put("blk64", (p[:, None] // 64 == p[None, :] // 64).astype(np.float32))
    put("flip", (p[:, None] + p[None, :] == 127).astype(np.float32))
    lm = np.zeros((128, 7, 128), np.float32)
    for k in range(7):
        b = 1 << k
        j, i = p[:, None], p[None, :]
        lm[:, k] = (j // (2 * b) == i // (2 * b)) & ((i // b) % 2 == 1) & ((j // b) % 2 == 0)
    put("lm", lm)
    q = np.arange(NS)
    same = q[:, None] // T_S == q[None, :] // T_S
    put("tri4", (same & (q[:, None] <= q[None, :])).astype(np.float32))
    put("neg4", np.where(same & (q[:, None] <= q[None, :]), 0.0, NEG))
    put("blk4", same.astype(np.float32))
    put("bsel", (q[:, None] // T_S == np.arange(8)[None, :]).astype(np.float32))
    b4, hh, mm, tt = p // 32, p // 8 % 4, p // 4 % 2, p % 4
    r = np.arange(64)
    put("comb", ((b4[:, None] == r[None, :] // 16) & (hh[:, None] == r[None, :] // 4 % 4)
                 & (tt[:, None] == r[None, :] % 4)).astype(np.float32))
    offc = np.zeros((128, 2, 8), np.float32)
    for g in range(2):
        offc[:, g] = np.where(np.arange(8)[None, :] == 4 * g + b4[:, None], 0.0, NEG)
    put("offc", offc)
    put("offb", np.where(np.arange(8)[None, :] == p[:, None] // 16, 0.0, NEG))
    put("m0", (mm == 0).astype(np.float32)[:, None])
    put("m1", (mm == 1).astype(np.float32)[:, None])
    put("eps", np.full((128, 1), EPS))
    put("one", np.ones((128, 1)))
    lam0 = np.array([0.8 - 0.6 * np.exp(-0.3 * l) for l in range(DEPTH)])
    put("lam0", np.tile(lam0, (128, 1)))
    put("oml", np.tile(1.0 - lam0, (128, 1)))
    put("p32", (p % 32)[:, None])
    dist = U_MAX - np.arange(U_TAB)
    dc = np.maximum(dist, 0)
    scaled = np.log(np.maximum(dc, 1).astype(np.float32) / np.float32(16)) / np.float32(np.log(2048 / 16))
    large = np.minimum(16 + (scaled.astype(np.float32) * np.float32(16)).astype(np.int32), 31)
    bucket = np.where(dc < 16, dc, large)
    e = np.zeros((34, U_TAB), np.float32)
    e[bucket, np.arange(U_TAB)] = 1.0
    count = ((dist >= 0) & (dist <= 128)).astype(int) + ((dist >= 0) & (dist <= 512) & (dist % 4 == 0)) \
        + ((dist >= 0) & (dist <= 2048) & (dist % 16 == 0))
    e[32] = np.where(count > 0, np.log(np.maximum(count, 1)), NEG)
    e[33] = np.where(dist >= 0, 0.0, NEG)
    pick = np.zeros((2, 8), np.float32)
    pick[0, :4] = 1.0
    pick[1, 4:] = 1.0
    return c, e, pick


SIGNALS = (
    "b_exp", "b_max", "b_out", "b_pv", "b_pv_mm", "ba_mm", "ba_sb", "bege", "bk_free", "bk_in0", "bk_in1",
    "bkt_a", "bkt_v", "bp", "bpt_mm", "bpt_sb", "bq", "bs_mm", "bsn", "bv_free", "bv_in0", "bv_in1", "c_exp",
    "c_group_done", "c_max", "c_pv", "c_pv_mm", "ck_free", "ck_in0", "ck_in1", "ck_in2", "ck_in3", "comb",
    "conv_acc", "conv_done", "conv_in", "conv_in_mm", "conv_rows", "conv_rows_mm", "conv_tail", "cpt_mm",
    "cpt_sb", "cq", "cs_mm", "csn", "cv_free", "cv_in0", "cv_in1", "cv_in2", "cv_in3", "decay_mm",
    "delta_out", "down_done", "down_free", "down_half", "dt_arg", "dt_exp", "exp_done", "gb", "gdone", "gmm",
    "gsq", "gsqrt", "gu_done", "gu_free", "h_done", "in_bias", "in_const", "in_lam", "in_pages", "in_rows",
    "in_strip", "in_vec", "in_x", "kkqk", "kt_a", "kt_v", "kv_done", "lam_exp", "lam_sums", "layer_vecs",
    "m_mm", "m_sb", "mu_mm", "nw_sb", "o_mm", "o_out", "out_done", "p_exp", "p_max", "p_mm", "p_out",
    "p_soft", "passed", "po_mm", "ppt_mm", "ppt_sb", "proj_a", "proj_done", "proj_v", "rms", "rows_a",
    "rows_mm", "rows_out", "rows_v", "s_mm", "setup_ev", "setup_mm", "silu", "soft", "sq_added", "sq_done",
    "ssq_done", "st_in", "st_new", "st_out", "staged_kv", "staged_q", "state_done", "t_mm", "t_up",
    "table_out", "tm_mm", "tokm", "u_up", "vn_mm", "vn_sb", "w_loaded0", "w_loaded1", "w_mm", "x_act",
    "x_bege", "x_decay", "x_dt", "x_gb", "x_kkqk", "x_lt", "x_m", "x_mu", "x_new", "x_nw", "x_o", "x_out",
    "x_qe", "x_s", "x_so", "x_t", "x_u", "x_vb", "x_vn", "x_vnsb", "x_w", "x_ws", "y_mm", "y_out", "y_rows",
)


def trunk(nc, A, O, scratch):
    where, n_const = columns()
    with ExitStack() as ctx:
        def sb(name, *shape, dt=F32):
            return ctx.enter_context(nc.sbuf_tensor(name, [128, *shape], dt))

        xT = sb("residual", KD, NT)
        hT = sb("normed_or_mixed", KD, NT)
        work = sb("hidden_or_projected", NZ * NT)
        wslot = sb("weight_slots", 2, 2048)
        strips = sb("prompt_bias", 8, SEQ)
        bias_c = sb("sample_bias_c", PAST)
        bias_cn = sb("sample_bias_c_new", 2, NS)
        bias_b = sb("sample_bias_b", KEYS_B)
        bias_bn = sb("sample_bias_b_new", NS)
        vtok = sb("values_by_token", 5, 512)
        k_rows = sb("keys_by_token", 5, 512)
        con = sb("constants", n_const)
        cols_conv = sb("conv_columns", 2 * 48)
        cols_norm = sb("norm_columns", 60)
        lay_conv = sb("layer_conv", 48)
        lay_norm = sb("layer_norm", LV)
        lay_ba = sb("layer_ba_weights", KD, 8)
        all_ba = sb("ba_weights", DEPTH, KD, 8)
        small = sb("small", 160)
        page_of = sb("page_of_row", 32, dt=I32)
        key_rows = sb("cache_rows", DEPTH, 32, dt=U32)
        lay_rows = sb("layer_cache_rows", 32, dt=U32)
        row_f = sb("cache_rows_f32", 32)
        arena = sb("arena", ARENA)

        ps = ctx.enter_context(nc.psum_tensor("banks", [128, 8, 512], F32))
        flat = ps[:, :, :].rearrange("p b n -> p (b n)")

        def C(name, rows=128):
            lo, hi = where[name]
            return con[0:rows, lo:hi]

        def carve(tensor, start, *shape):
            n = int(np.prod(shape))
            v = tensor[:, start:start + n]
            if len(shape) == 2:
                v = v.rearrange("p (a b) -> p a b", a=shape[0])
            if len(shape) == 3:
                v = v.rearrange("p (a b c) -> p a b c", a=shape[0], b=shape[1])
            return v, start + n

        hidden, _ = carve(work, 0, NF, NT)
        gated, _ = carve(work, NF * NT, 2, NT)
        z, _ = carve(work, 0, NZ, NT)
        x_rows, _ = carve(work, 0, 5, D)
        bucket_rows, e_end = carve(work, 5 * D, U_TAB)
        table, t_end = carve(work, e_end, U_TAB)
        strip_raw, s_end = carve(work, 0, 8, SEQ)
        win_b, _ = carve(work, s_end + 1100, U_MAX + 1)
        win_c, _ = carve(work, t_end, U_MAX + 1)
        assert s_end + 1100 >= 5 * D and s_end + 1100 + U_MAX + 1 <= NZ * NT
        vec_rows_a, r_end = carve(arena, 0, 128)
        vec_rows_b, r_end = carve(arena, r_end, 128)
        relb, r_end = carve(arena, r_end, 8)
        lam_rows, r_end = carve(arena, r_end, 4, DEPTH * 32)
        lam_prod, r_end = carve(arena, r_end, 2, DEPTH * 32)
        y_rows, _ = carve(work, 0, 5, D)

        a_log_c, dt_c = small[:, 0:8], small[:, 8:16]
        lam_sum, lam_all = small[:, 16:20], small[:, 20:22]
        lam, cnorm = small[:, 22:23], small[:, 23:24]
        ea, dtb = small[:, 24:28], small[:, 28:32]
        ba, _ = carve(small, 32, 5, 8)
        beta, _ = carve(small, 72, 5, 4)
        gdec, _ = carve(small, 92, 5, 4)
        spa, _ = carve(small, 112, 5, 4)
        spb, _ = carve(small, 132, 5, 4)
        sign = small[:, 152:153]

        at = 0
        conv_tail, at = carve(arena, at, 12, 27)
        conv_in, at = carve(arena, at, CONV_CH)
        xs, at = carve(arena, at, 12, 8, 7)
        cvt, at = carve(arena, at, 2, NT)
        sq, at = carve(arena, at, 2, NT)
        rn, at = carve(arena, at, 2, NT)
        assert at <= 15 * 512
        conv_out, at = carve(arena, 15 * 512, CONV_CH)

        at = 0
        names = ("qc", "kc", "vc", "gB", "bB", "DT", "eG", "LT", "LK", "QKT", "KB", "VB", "KD", "M", "U", "T", "nW", "VN", "S")
        m = {}
        for n in names:
            m[n], at = carve(arena, at, NH, 128)
        gc, at = carve(arena, at, 4)
        kde, at = carve(arena, at, 4)
        ecol, at = carve(arena, at, 4)
        bege, at = carve(arena, at, 4)
        assert at <= ARENA
        at = 0
        t = {}
        t["st"] = arena[:, 0:4096].rearrange("p (h b v) -> p h b v", h=4, b=8)
        at = 4096
        for n in ("qc", "kc", "vc", "eG", "DT", "LT", "LK", "QKT", "M", "U", "T", "nW", "QS"):
            t[n], at = carve(arena, at, NH, NS)
        for n in ("gB", "KB", "VB", "KD", "VN"):
            t[n], at = carve(arena, at, NH, 128)
        t["WQ"], at = carve(arena, at, NH, 8, 8)
        t["bB"], at = carve(arena, at, NH, NS)
        sgc, at = carve(arena, at, 4)
        skde, at = carve(arena, at, 4)
        secol, at = carve(arena, at, 4)
        sbege, at = carve(arena, at, 4)
        assert at <= ARENA
        vblk = carve(work, 0, 8, 128)[0], carve(work, 1024, 8, 128)[0]

        dead = 16 * NT
        c_rows, at = carve(work, 0, RING, 4, 256)
        c_kt, at = carve(work, at, 2, 2, 512)
        c_s, at = carve(work, at, PAST + NS)
        assert at <= dead
        b_rows, at = carve(work, 0, 2, 8, 256)
        b_kt, at = carve(work, at, 2, 2, KEYS_B)
        b_s, at = carve(work, at, KEYS_B + NS)
        assert at <= dead
        pv_rows, at = carve(work, RING * 1024, 8, 256)
        assert RING * 1024 == 2 * 8 * 256
        sq2, _ = carve(work, RING * 1024, 2, NT)
        rn4 = k_rows[:, :, :].rearrange("p b n -> p (b n)")[:, 0:4 * NT].rearrange("p (i n) -> p i n", i=4)
        comb, at = carve(arena, 0, 64)
        c_mx, start = carve(arena, at, 9)
        c_pt, at = carve(arena, start, 17, 64)
        qc_all = arena[:, ARENA - 1152:ARENA]
        b_pt, at = carve(arena, start, 9, 128)
        qb_all, at = arena[:, at:at + 2176], at + 2176
        assert at <= 4096
        cv_rows, v_end = carve(arena, 4096, RING, 4, 256)
        bv_rows, v_end = carve(arena, 4096, 2, 8, 256)
        assert v_end <= ARENA - 1152

        def qc_of(b, pair):
            return qc_all[:, 256 * b + 128 * pair:256 * b + 128 * pair + 128]

        def qb_of(b, pair):
            return qb_all[:, 256 * b + 128 * pair:256 * b + 128 * pair + 128]

        def maps(u):
            return 1 if u < 16 else 2

        def qk_of(u, mp):
            head = u // 4 % 4
            if u < 16:
                return 16 + head // 2, 18 + head // 2, 64 * (head % 2), 64
            return 22 + head // 2, 24 + head // 2, 64 * (head % 2) + 32 * mp, 32

        p_s = arena[:, at:at + 2048].rearrange("p (u m k) -> p u m k", u=2, m=2)
        at += 2048
        p_pt, at = carve(arena, at, 2, 4, 128)
        p_mx, at = carve(arena, at, 2, 8)
        assert at <= ARENA

        s = {}
        for n in SIGNALS:
            s[n] = ctx.enter_context(nc.semaphore(n))
        block = ctx.enter_context(nc.Block())

        def alone(eng):
            eng.sem_inc(s["passed"], 1)

        def window_block(blk):
            return (128 * blk, 128) if blk < 4 else (512 + 96 * (blk - 4), 96)

        def half(bank, h):
            return ps[:, bank + h, 0:HALF]

        def both(bank):
            return ps[:, bank:bank + 2, 0:HALF]

        def tok(v):
            return v.rearrange("p (h n) -> p h n", h=2)

        def over(v, n):
            return v.unsqueeze(2).broadcast_to([v.shape[0], v.shape[1], n])

        def per_head(v, n=4):
            return v.unsqueeze(1).broadcast_to([v.shape[0], n, v.shape[1]])

        @block.sync
        def _(sp):
            def ld(dst, src, name, inc=16):
                return sp.dma_start(dst, src).then_inc(s[name], inc)

            ld(con[:, :], A["consts"], "in_const")
            ld(x_rows[:, 0:4, :], A["x_prompt"][0].rearrange("(t p) d -> p t d", p=128), "in_x")
            ld(x_rows[0:NS, 4, :], A["x_sample"].rearrange("b t d -> (b t) d"), "in_x")
            ld(vec_rows_a[0:96, :], A["conv_w"].rearrange("l j (c p) -> (l j c) p", p=128), "in_vec")
            for l in range(DEPTH):
                for i, name in enumerate(("norm_ffn1", "norm_mix", "norm_ffn2")):
                    ld(vec_rows_b[LV * l + 8 * i:LV * l + 8 * i + 8, :],
                       A[name][l].rearrange("(k p) -> k p", p=128), "in_vec")
                ld(vec_rows_b[LV * l + 24:LV * l + 25, :], A["a_norm_w"][l:l + 1], "in_vec")
                for h in range(2):
                    ld(vec_rows_b[LV * l + 25:LV * l + 26, 64 * h:64 * h + 64], A["c_norm_w"][l:l + 1], "in_vec")
            ld(vec_rows_b[2 * LV:2 * LV + 8, :], A["final_norm"].rearrange("(k p) -> k p", p=128), "in_vec")
            ld(relb[0:32, :], A["rel_bias"], "in_bias")
            ld(relb[32:34, :], A["pick"], "in_bias")
            ld(bucket_rows[0:34, :], A["buckets"], "in_bias")
            for i, name in enumerate(("lambda_q1", "lambda_k1", "lambda_q2", "lambda_k2")):
                ld(lam_rows[:, i, :], A[name].rearrange("l d -> (l d)").partition_broadcast(128), "in_lam")
            ld(a_log_c, A["a_log"].rearrange("l h -> (l h)").partition_broadcast(128), "in_lam")
            ld(dt_c, A["dt_bias"].rearrange("l h -> (l h)").partition_broadcast(128), "in_lam")
            for l in range(DEPTH):
                ld(all_ba[:, l], A["w_in"][l, :, BA_COL:BC_COL].rearrange("(k p) n -> p k n", p=128), "in_lam")
            for pg in range(4):
                src = bass.AP(tensor=A["page_table"].tensor, offset=pg, ap=[[0, 32], [4, 32]])
                sp.dma_start(page_of[32 * pg:32 * pg + 32, :], src, allow_slow_non_contiguous=True).then_inc(s["in_pages"], 16)
            def load_gate(l, w, f, slot):
                for i, name in enumerate((f"w{w + 1}_gate", f"w{w + 1}_up")):
                    dst = wslot[:, slot, 1024 * i:1024 * i + 1024].rearrange("p (k n) -> p k n", k=KD)
                    src = A[name][ds(l, 1), :, ds(f * 128, 128)].rearrange("l (k p) n -> p (l k) n", p=128)
                    ld(dst, src, f"w_loaded{slot}")

            def load_down(l, w, o, slot):
                dst = wslot[:, slot, 0:11 * 128].rearrange("p (k n) -> p k n", k=11)
                src = A[f"w{w + 1}_down"][ds(l, 1), slot * 1408:slot * 1408 + 1408, ds(o * 128, 128)]
                ld(dst, src.rearrange("l (k p) n -> p (l k) n", p=128), f"w_loaded{slot}", 32)

            def load_wide(l, name, col, slot):
                dst = wslot[:, slot, :].rearrange("p (k n) -> p k n", k=KD)
                src = A[name][ds(l, 1), :, ds(col, 256)].rearrange("l (k p) n -> p (l k) n", p=128)
                ld(dst, src, f"w_loaded{slot}", 32)

            def ffn_loads(l, w):
                it = l * 2 + w
                for slot in range(2):
                    if w == 0:
                        sp.wait_ge(s["down_half" if slot == 0 else "down_done"], it * 8 + 1)
                    else:
                        sp.wait_ge(s["out_done"], l * 8 + 6 + 2 * slot)
                    load_gate(l, w, slot, slot)
                with sp.Fori(1, 11) as j:
                    for slot in range(2):
                        sp.wait_ge(s["gu_done"], it * 22 + j * 2 + slot - 1)
                        load_gate(l, w, j * 2 + slot, slot)
                for slot in range(2):
                    sp.wait_ge(s["gu_done"], it * 22 + 21 + slot)
                    load_down(l, w, 0, slot)
                with sp.Fori(1, 8) as o:
                    for slot in range(2):
                        sp.wait_ge(s["down_half" if slot == 0 else "down_done"], it * 8 + o + 1)
                        load_down(l, w, o, slot)

            with sp.Fori(0, DEPTH) as l:
                sp.wait_ge(s["x_new"], l * 3 + 1)
                ld(conv_in[0:24, :], A["state_conv"][ds(l, 1)].rearrange("l b j c -> (l b j) c"), "conv_in")
                ffn_loads(l, 0)
                for slot in range(2):
                    sp.wait_ge(s["down_half" if slot == 0 else "down_done"], l * 16 + 8 + 1)
                    load_wide(l, "w_in", slot * 256, slot)
                with sp.Fori(1, 4) as j:
                    for slot in range(2):
                        sp.wait_ge(s["proj_done"], l * 28 + 4 * j + 2 * slot - 2)
                        load_wide(l, "w_in", j * 512 + slot * 256, slot)
                with sp.Fori(4, 7) as j:
                    for slot in range(2):
                        sp.wait_ge(s["proj_done"], l * 28 + 4 * j + 2 * slot - 2)
                        load_wide(l, "w_in", j * 512 + slot * 256 + 8, slot)
                for slot in range(2):
                    sp.wait_ge(s["proj_done"], l * 28 + 26 + 2 * slot)
                    load_wide(l, "w_out", slot * 256, slot)
                sp.wait_ge(s["state_done"], l * 5 + 5)
                for h in range(NH):
                    ld(t["st"][:, h], A["state_delta"][ds(l, 1), :, h].rearrange("l b k v -> k (l b) v"), "st_in")
                def load_window(name, dst, n, slot, sem):
                    rows = A[name][ds(l, 1), ds(n, 1)].rearrange("l b p h d -> (l b p) (h d)")
                    ld(dst[:, slot, 0:4, :], rows[1536:2048].rearrange("(p r) c -> p r c", r=4), sem)
                    ld(dst[0:96, slot, 4:8, :], rows[0:1536].rearrange("(a r) c -> a r c", r=16)[:, 0:4, :], sem)

                sp.wait_ge(s["ck_free"], l * 32 + 32 + 4)
                for slot in range(2):
                    load_window("cache_win_k", b_rows, slot, slot, f"bk_in{slot}")
                sp.wait_ge(s["cv_free"], l * 32 + 32 + 4)
                for slot in range(2):
                    load_window("cache_win_v", bv_rows, slot, slot, f"bv_in{slot}")
                for name, dst, tag in (("cache_win_k", b_rows, "bk"), ("cache_win_v", bv_rows, "bv")):
                    with sp.Fori(1, 4) as j:
                        for slot in range(2):
                            sp.wait_ge(s[tag + "_free"], l * 8 + j * 2 + slot + 1)
                            alone(sp)
                            load_window(name, dst, j * 2 + slot, slot, f"{tag}_in{slot}")
                for slot in range(2):
                    sp.wait_ge(s["out_done"], l * 8 + 2 + 2 * slot)
                    load_wide(l, "w_out", 512 + slot * 256, slot)
                ffn_loads(l, 1)

        @block.gpsimd
        def _(gp):
            def st(dst, src, name):
                return gp.dma_start(dst, src).then_inc(s[name], 16)

            with gp.Fori(0, DEPTH) as l:
                gp.wait_ge(s["rows_a"], l * 5 + 5)
                gp.wait_ge(s["rows_v"], l * 5 + 5)
                for out_p, out_s, src in ((O["wk_p"], O["wk_s"], k_rows[:, :, 0:256]), (O["wv_p"], O["wv_s"], vtok[:, :, 0:256]),
                                          (O["k_p"], O["k_s"], k_rows[:, :, 256:512]), (O["v_p"], O["v_s"], vtok[:, :, 256:512])):
                    st(out_p[ds(l, 1)].rearrange("l b (t p) h d -> p (l b t) (h d)", p=128), src[:, 0:4, :], "rows_out")
                    st(out_s[ds(l, 1)].rearrange("l b t h d -> (l b t) (h d)"), src[0:NS, 4, :], "rows_out")
                gp.wait_ge(s["conv_rows"], l + 1)
                st(O["conv_p"][ds(l, 1)].rearrange("l b j c -> (l b j) c"), conv_out[0:3, :], "rows_out")
                st(O["conv_s"][ds(l, 1)].rearrange("l b j c -> (l b j) c"), conv_out[3:27, :], "rows_out")
                gp.wait_ge(s["state_done"], l * 5 + 5)
                st(O["delta_p"][ds(l, 1)].rearrange("l b h k v -> k (l b h) v"), m["S"][:, :, :], "delta_out")
                for h in range(NH):
                    gp.wait_ge(s["st_new"], l * 4 + h + 1)
                    st(O["delta_s"][ds(l, 1), :, h].rearrange("l b k v -> k (l b) v"), t["st"][:, h], "st_out")

                def load_chunk(name, n):
                    tag, dst = ("ck", c_rows) if name == "cache_k" else ("cv", cv_rows)
                    gp.wait_ge(s[tag + "_free"], l * 32 + n + 1)
                    alone(gp)
                    rows = A[name].rearrange("l n (k r) h d -> (l n k) (r h d)", r=4)
                    gp.indirect_dma_start(dst[:, n % RING].rearrange("p r c -> p (r c)"), None, rows,
                                          bass.IndirectOffsetOnAxis(ap=lay_rows[:, n:n + 1], axis=0))\
                        .then_inc(s[f"{tag}_in{n % RING}"], 16)

                gp.wait_ge(s["layer_vecs"], l + 1)
                for n in range(0, 12):
                    load_chunk("cache_k", n)
                for n in range(4):
                    load_chunk("cache_v", n)
                    load_chunk("cache_k", 12 + n)
                for n in range(4):
                    load_chunk("cache_v", 4 + n)
                    load_chunk("cache_k", 16 + n)
                for n in range(8, 16):
                    load_chunk("cache_v", n)
                for n in range(20, 28):
                    load_chunk("cache_k", n)
                for n in range(4):
                    load_chunk("cache_v", 16 + n)
                    load_chunk("cache_k", 28 + n)
                for n in range(20, 32):
                    load_chunk("cache_v", n)
            gp.wait_ge(s["y_rows"], 5)
            st(O["y_p"][0].rearrange("(t p) d -> p t d", p=128), y_rows[:, 0:4, :], "y_out")
            st(O["y_s"].rearrange("b t d -> (b t) d"), y_rows[0:NS, 4, :], "y_out")
            gp.wait_ge(s["y_out"], 32)
            gp.wait_ge(s["rows_out"], DEPTH * 160)
            gp.wait_ge(s["delta_out"], DEPTH * 16)
            gp.wait_ge(s["st_out"], DEPTH * 64)

        @block.tensor
        def _(pe):
            ident = C("ident")
            for name in ("down_half", "down_done"):
                pe.sem_inc(s[name], 1)
            for name in ("gmm", "bk_free", "bv_free", "cs_mm", "bs_mm"):
                pe.sem_inc(s[name], 2)
            for name in ("ck_free", "cv_free"):
                pe.sem_inc(s[name], RING)

            def turn(out, in_, rows=128):
                return pe.transpose(out, in_, ident[0:rows, 0:rows])

            pe.wait_ge(s["in_const"], 16)
            pe.wait_ge(s["in_x"], 32)
            for i in range(1, 6):
                if i > 2:
                    pe.wait_ge(s["setup_ev"], i - 2)
                bank = 2 * (i % 2)
                n = 128 if i < 5 else NS
                for k in range(KD):
                    mm = turn(flat[:, 512 * bank + n * k:512 * bank + n * k + n],
                              x_rows[0:n, i - 1, 128 * k:128 * k + 128], n)
                mm.then_inc(s["setup_mm"], 1)
            pe.wait_ge(s["setup_ev"], 4)
            pe.wait_ge(s["in_vec"], 16 * (1 + DEPTH * 6 + 1))
            turn(ps[:, 0, 0:96], vec_rows_a[0:96, :], 96)
            turn(ps[:, 0, 96:156], vec_rows_b[0:60, :], 60).then_inc(s["setup_mm"], 1)
            pe.wait_ge(s["in_bias"], 48)
            for c in range(5):
                i, n = 7 + c, min(512, U_TAB - 512 * c)
                pe.wait_ge(s["setup_ev"], i - 2)
                pe.matmul(ps[0:8, 2 * (i % 2), 0:n], relb[0:34, :], bucket_rows[0:34, 512 * c:512 * c + n],
                          start=True, stop=True).then_inc(s["setup_mm"], 1)
            pe.wait_ge(s["in_strip"], 128)
            for h in range(8):
                i = 12 + h
                pe.wait_ge(s["setup_ev"], i - 2)
                pe.matmul(ps[:, 2 * (i % 2), :], C("flip"), strip_raw[:, h, :],
                          start=True, stop=True).then_inc(s["setup_mm"], 1)

            def norm(n):
                pe.wait_ge(s["sq_added"], n * 8 + 9)
                for h in range(2):
                    mm = pe.matmul(half(0, h), C("ones"), gated[:, 0, h * HALF:(h + 1) * HALF], start=True, stop=True)
                mm.then_inc(s["ssq_done"], 1)

            def ffn(l, w):
                it = l * 2 + w
                fill = l * 47 + 28 * w

                def gate_up(j, slot):
                    pe.wait_ge(s[f"w_loaded{slot}"], (fill + j + 1) * 32)
                    pe.wait_ge(s["gu_free"], it * 22 + j * 2 + slot + 1)
                    for i in range(2):
                        for k in range(KD):
                            if isinstance(j, int) and slot == 0 and i == 0:
                                pe.wait_ge(s["h_done"], (l * 3 + 2 * w) * 8 + k + 1)
                            at = 1024 * i + 128 * k
                            for h in range(2):
                                mm = pe.matmul(half(4 * slot + 2 * i, h), wslot[:, slot, at:at + 128],
                                               hT[:, k, h * HALF:(h + 1) * HALF], start=k == 0, stop=k == KD - 1)
                    mm.then_inc(s["gu_done"], 1)

                for slot in range(2):
                    gate_up(0, slot)
                with pe.Fori(1, 11) as j:
                    for slot in range(2):
                        gate_up(j, slot)
                pe.wait_ge(s["gu_free"], it * 22 + 22 + 2)
                alone(pe)
                with pe.Fori(0, 4) as j:
                    for u in range(2):
                        pe.wait_ge(s["down_free"], it * 8 + j * 2 + u + 1)
                        for part in range(2):
                            pe.wait_ge(s[f"w_loaded{part}"], (fill + 11 + j * 2 + u + 1) * 32)
                            for q in range(11):
                                for h in range(2):
                                    mm = pe.matmul(half(4 * u, h), wslot[:, part, 128 * q:128 * q + 128],
                                                   hidden[:, 11 * part + q, h * HALF:(h + 1) * HALF],
                                                   start=part == 0 and q == 0, stop=part == 1 and q == 10)
                            mm.then_inc(s["down_done" if part else "down_half"], 1)

            def square_sums(base, u, ones, sqb, bank=0):
                pe.wait_ge(s["gsq"], base + u + 1)
                pe.wait_ge(s["gsqrt"], base + u + 1)
                for h in range(2):
                    mm = pe.matmul(half(bank + 2 * u, h), ones, sqb[:, u, h * HALF:(h + 1) * HALF],
                                   start=True, stop=True)
                mm.then_inc(s["gmm"], 1)

            def project(l):
                def fill(j, slot, bank, back):
                    pe.wait_ge(s[f"w_loaded{slot}"], (l * 47 + 19 + j + 1) * 32)
                    for u in range(2):
                        pe.wait_ge(s["proj_v" if u else "proj_a"], l * 14 + j * 2 + slot + 3 - back)
                        for k in range(KD):
                            if isinstance(j, int) and slot == 0 and u == 0:
                                pe.wait_ge(s["h_done"], (l * 3 + 1) * 8 + k + 1)
                            at = 256 * k + 128 * u
                            for h in range(2):
                                mm = pe.matmul(half(bank + 2 * u, h), wslot[:, slot, at:at + 128],
                                               hT[:, k, h * HALF:(h + 1) * HALF], start=k == 0, stop=k == KD - 1)
                        mm.then_inc(s["proj_done"], 1)

                for slot in range(2):
                    fill(0, slot, 4 * slot, 2)
                with pe.Fori(1, 3) as j:
                    for slot in range(2):
                        fill(j, slot, 4 * slot, 2)
                with pe.Fori(3, 7) as j:
                    for slot in range(2):
                        fill(j, slot, 0, 1)
                        square_sums(l * 14 + j * 2 - 6, slot, C("ones"), sq, 4)
                pe.wait_ge(s["proj_a"], l * 14 + 16)
                pe.wait_ge(s["proj_v"], l * 14 + 16)
                for b in range(5):
                    n = 128 if b < 4 else NS
                    for k in range(KD):
                        mm = pe.matmul(ps[0:n, 0, 8 * b:8 * b + 8], hT[:, k, 128 * b:128 * b + n], lay_ba[:, k, :],
                                       start=k == 0, stop=k == KD - 1)
                mm.then_inc(s["ba_mm"], 1)
                for b in range(5):
                    n = 128 if b < 4 else NS
                    a = 2 + 2 * (b % 2)
                    if b == 1:
                        pe.wait_ge(s["gsqrt"], l * 14 + 10)
                    if b >= 2:
                        pe.wait_ge(s["rows_a"], l * 5 + b - 1)
                        pe.wait_ge(s["rows_v"], l * 5 + b - 1)
                    for i, tile in enumerate((18, 19, 20, 21, 24, 25, 26, 27)):
                        mm = turn(ps[0:n, a + i // 4, 128 * (i % 4):128 * (i % 4) + 128], z[:, tile, 128 * b:128 * b + n])
                    mm.then_inc(s["rows_mm"], 1)
                pe.wait_ge(s["conv_tail"], l + 1)
                pe.wait_ge(s["rows_v"], l * 5 + 4)
                for c in range(12):
                    mm = turn(ps[0:27, 5 + c // 4, 128 * (c % 4):128 * (c % 4) + 128], conv_tail[:, c, :])
                mm.then_inc(s["conv_rows_mm"], 1)

            def chunk(l, c):
                it = l * 4 + c
                pe.wait_ge(s["staged_kv"], it + 1)
                for h in range(NH):
                    turn(ps[:, 0, 128 * h:128 * h + 128], m["kc"][:, h, :])
                    mm = turn(ps[:, 1, 128 * h:128 * h + 128], m["vc"][:, h, :])
                mm.then_inc(s["tokm"], 1)
                pe.wait_ge(s["gb"], it + 1)
                pe.wait_ge(s["o_out"], it + 1)
                for h in range(NH):
                    hs = slice(128 * h, 128 * h + 128)
                    pe.matmul(ps[:, 2, hs], m["gB"][:, h, :], C("tri"), start=True, stop=True)
                    pe.matmul(ps[:, 3, hs], m["bB"][:, h, :], ident, start=True, stop=True)
                pe.matmul(ps[:, 4, 0:4], C("tri"), m["gB"][:, :, 0], start=True, stop=True).then_inc(s["decay_mm"], 1)
                for h in range(NH):
                    hs = slice(128 * h, 128 * h + 128)
                    pe.matmul(ps[:, 5, hs], m["kc"][:, h, :], m["kc"][:, h, :], start=True, stop=True)
                pe.wait_ge(s["staged_q"], it + 1)
                for h in range(NH):
                    hs = slice(128 * h, 128 * h + 128)
                    mm = pe.matmul(ps[:, 6, hs], m["kc"][:, h, :], m["qc"][:, h, :], start=True, stop=True)
                mm.then_inc(s["kkqk"], 1)
                pe.wait_ge(s["u_up"], it * 14 + 2)
                for h in range(NH):
                    mm = turn(ps[:, 2 + h // 2, 128 * (h % 2):128 * (h % 2) + 128], m["U"][:, h, :])
                mm.then_inc(s["t_mm"], 1)

                def level(k, last=False):
                    for a in range(2):
                        pe.wait_ge(s["t_up"], it * 12 + k * 2 + a - 1)
                        for i in range(2):
                            mm = pe.matmul(ps[:, 4 if a else 7, 128 * i:128 * i + 128], m["LK"][:, 2 * a + i, :],
                                           m["T"][:, 2 * a + i, :], start=True, stop=True)
                        mm.then_inc(s["m_mm"], 1)
                    for a in range(2):
                        pe.wait_ge(s["m_sb"], it * 12 + k * 2 + a - 1)
                        pe.wait_ge(s["u_up"], it * 14 + k * 2 + a - 1)
                        if not last:
                            for i in range(2):
                                mm = pe.matmul(ps[:, 2 + a, 128 * i:128 * i + 128], m["U"][:, 2 * a + i, :],
                                               m["M"][:, 2 * a + i, :], start=True, stop=True)
                            mm.then_inc(s["tm_mm"], 1)
                        for i in range(2):
                            mm = pe.matmul(ps[:, 5 + a, 128 * i:128 * i + 128], m["M"][:, 2 * a + i, :],
                                           m["U"][:, 2 * a + i, :], start=True, stop=True)
                        mm.then_inc(s["mu_mm"], 1)

                with pe.Fori(1, 6) as k:
                    level(k)
                level(6, last=True)
                pe.wait_ge(s["u_up"], it * 14 + 14)
                pe.wait_ge(s["kv_done"], it + 1)
                for h in range(NH):
                    mm = pe.matmul(ps[:, 7, 128 * h:128 * h + 128], m["KB"][:, h, :], m["U"][:, h, :], start=True, stop=True)
                mm.then_inc(s["w_mm"], 1)
                pe.wait_ge(s["nw_sb"], it + 1)
                for h in range(NH):
                    hs = slice(128 * h, 128 * h + 128)
                    pe.matmul(ps[:, 2, hs], m["U"][:, h, :], m["VB"][:, h, :], start=True, stop=False)
                    mm = pe.matmul(ps[:, 2, hs], m["nW"][:, h, :], m["S"][:, h, :], start=False, stop=True)
                mm.then_inc(s["vn_mm"], 1)
                pe.wait_ge(s["vn_sb"], it + 1)
                for h in range(NH):
                    hs = slice(128 * h, 128 * h + 128)
                    pe.matmul(ps[:, 3, hs], m["S"][:, h, :], m["qc"][:, h, :], start=True, stop=False)
                    mm = pe.matmul(ps[:, 3, hs], m["VN"][:, h, :], m["QKT"][:, h, :], start=False, stop=True)
                mm.then_inc(s["o_mm"], 1)
                for h in range(NH):
                    mm = pe.matmul(ps[:, 7, 128 * h:128 * h + 128], m["KD"][:, h, :], m["VN"][:, h, :], start=True, stop=True)
                mm.then_inc(s["s_mm"], 1)

            def sample_chunk(l):
                pe.wait_ge(s["x_act"], l * 5 + 1)
                for h in range(NH):
                    turn(ps[0:NS, 0, 128 * h:128 * h + 128], t["kc"][:, h, :])
                    mm = turn(ps[0:NS, 1, 128 * h:128 * h + 128], t["vc"][:, h, :])
                pe.wait_ge(s["x_gb"], l + 1)
                for h in range(NH):
                    hs = slice(NS * h, NS * h + NS)
                    pe.matmul(ps[:, 2, hs], t["gB"][0:NS, h, :], C("tri4", NS), start=True, stop=True)
                    pe.matmul(ps[0:NS, 3, hs], t["bB"][0:NS, h, :], ident[0:NS, 0:NS], start=True, stop=True)
                pe.matmul(ps[0:NS, 4, 0:4], C("tri4", NS), t["gB"][0:NS, :, 0], start=True, stop=True)
                pe.matmul(ps[0:NS, 4, 4:8], C("blk4", NS), t["gB"][0:NS, :, 0], start=True, stop=True).then_inc(s["x_decay"], 1)
                for h in range(NH):
                    hs = slice(NS * h, NS * h + NS)
                    pe.matmul(ps[0:NS, 5, hs], t["kc"][:, h, :], t["kc"][:, h, :], start=True, stop=True)
                    mm = pe.matmul(ps[0:NS, 6, hs], t["kc"][:, h, :], t["qc"][:, h, :], start=True, stop=True)
                mm.then_inc(s["x_kkqk"], 1)
                pe.wait_ge(s["x_u"], l * 2 + 1)
                alone(pe)
                for h in range(NH):
                    mm = turn(ps[0:NS, 6, NS * h:NS * h + NS], t["U"][0:NS, h, :], NS)
                mm.then_inc(s["x_t"], 1)
                pe.wait_ge(s["x_lt"], l + 1)
                alone(pe)
                for h in range(NH):
                    mm = pe.matmul(ps[0:NS, 7, NS * h:NS * h + NS], t["LK"][0:NS, h, :], t["T"][0:NS, h, :], start=True, stop=True)
                mm.then_inc(s["x_m"], 1)
                pe.wait_ge(s["x_act"], l * 5 + 4)
                alone(pe)
                for h in range(NH):
                    mm = pe.matmul(ps[0:NS, 5, NS * h:NS * h + NS], t["M"][0:NS, h, :], t["U"][0:NS, h, :], start=True, stop=True)
                mm.then_inc(s["x_mu"], 1)
                pe.wait_ge(s["x_u"], l * 2 + 2)
                for h in range(NH):
                    mm = pe.matmul(ps[:, 7, NS * h:NS * h + NS], t["KB"][0:NS, h, :], t["U"][0:NS, h, :], start=True, stop=True)
                mm.then_inc(s["x_w"], 1)
                pe.wait_ge(s["x_act"], l * 5 + 5)
                pe.wait_ge(s["x_qe"], l + 1)
                pe.wait_ge(s["st_in"], l * 64 + 64)
                for h in range(NH):
                    for b in range(NB_S):
                        mm = pe.matmul(ps[:, 2, 64 * h + 8 * b:64 * h + 8 * b + 8], t["st"][:, h, b, :], t["WQ"][:, h, b, :],
                                       start=True, stop=True)
                mm.then_inc(s["x_ws"], 1)
                pe.wait_ge(s["x_nw"], l + 1)
                alone(pe)
                for h in range(NH):
                    hs = slice(128 * h, 128 * h + 128)
                    pe.matmul(ps[0:NS, 3, hs], t["U"][0:NS, h, :], t["VB"][0:NS, h, :], start=True, stop=False)
                    mm = pe.matmul(ps[0:NS, 3, hs], t["nW"][:, h, :], ident, start=False, stop=True)
                mm.then_inc(s["x_vn"], 1)
                pe.wait_ge(s["x_vnsb"], l + 1)
                alone(pe)
                for h in range(NH):
                    mm = pe.matmul(ps[:, 4, NS * h:NS * h + NS], t["VN"][0:NS, h, :], t["QKT"][0:NS, h, :], start=True, stop=True)
                mm.then_inc(s["x_o"], 1)
                for h in range(NH):
                    pe.wait_ge(s["x_vb"], l * 4 + h + 1)
                    if h >= 2:
                        pe.wait_ge(s["st_new"], l * 4 + h - 1)
                    for i in range(2):
                        mm = pe.matmul(ps[:, (6 if h % 2 else 0) + i, :], t["KD"][0:NS, h, :],
                                       vblk[h % 2][0:NS, 4 * i:4 * i + 4, :], start=True, stop=True)
                    mm.then_inc(s["x_s"], 1)

            def group_c(l, g):
                G = l * 2 + g
                pe.wait_ge(s["cq"], G + 1)

                def scores(n):
                    pe.wait_ge(s["kt_a"], G * 16 + n + 1)
                    pe.wait_ge(s["kt_v"], G * 16 + n + 1)
                    for pair in range(2):
                        mm = pe.matmul(ps[:, n % 4, :], qc_of(n // 4, pair), c_kt[:, n % 2, pair, :],
                                       start=n < 4 and pair == 0, stop=n >= 12 and pair == 1)
                    mm.then_inc(s["cs_mm"], 1)

                for n in range(16):
                    pe.wait_ge(s[f"ck_in{n % RING}"], (G * 4 + n // RING + 1) * 16)
                    if n >= 2:
                        pe.wait_ge(s["kt_a"], G * 16 + n - 1)
                        pe.wait_ge(s["kt_v"], G * 16 + n - 1)
                    for pair in range(2):
                        for pg in range(4):
                            mm = turn(ps[:, 4 + 2 * (n % 2) + pair, 128 * pg:128 * pg + 128],
                                      c_rows[:, n % RING, pg, 128 * pair:128 * pair + 128])
                    mm.then_inc(s["ck_free"], 1)
                    if n >= 1:
                        scores(n - 1)
                scores(15)
                for b in range(4):
                    for pair in range(2):
                        mm = pe.matmul(ps[:, 4, 0:NS], qc_of(b, pair), z[:, 24 + pair, SEQ:NT],
                                       start=b == 0 and pair == 0, stop=b == 3 and pair == 1)
                mm.then_inc(s["csn"], 1)
                pe.wait_ge(s["comb"], G + 1)
                for blk in range(16):
                    pe.matmul(ps[:, blk // 8, 64 * (blk % 8):64 * (blk % 8) + 64], c_s[:, 128 * blk:128 * blk + 128],
                              comb[:, :], start=True, stop=True)
                pe.matmul(ps[0:NS, 2, 0:64], c_s[:, PAST:PAST + NS], comb[:, :], start=True, stop=True).then_inc(s["cpt_mm"], 1)
                pe.wait_ge(s["cpt_sb"], G + 1)
                for n in range(16):
                    b, kc = n // 4, n % 4
                    pe.wait_ge(s[f"cv_in{n % RING}"], (G * 4 + n // RING + 1) * 16)
                    out = ps[0:16, 4 + b // 2, 256 * (b % 2):256 * (b % 2) + 256]
                    if kc == 0:
                        alone(pe)
                        pe.matmul(out, c_pt[0:NS, 16, 16 * b:16 * b + 16], vtok[0:NS, 4, 256:512], start=True, stop=False)
                    for pg in range(4):
                        mm = pe.matmul(out, c_pt[:, 4 * kc + pg, 16 * b:16 * b + 16], cv_rows[:, n % RING, pg, :],
                                       start=False, stop=kc == 3 and pg == 3)
                    mm.then_inc(s["cv_free"], 1)
                pe.wait_ge(s["c_pv"], G + 1)
                alone(pe)
                for b in range(4):
                    for pair in range(2):
                        mm = turn(ps[:, 6, 32 * b + 16 * pair:32 * b + 16 * pair + 16],
                                  pv_rows[0:16, b, 128 * pair:128 * pair + 128], 16)
                mm.then_inc(s["c_pv_mm"], 1)

            def sample_b(l):
                pe.wait_ge(s["bq"], l + 1)

                def scores(b):
                    pe.wait_ge(s["bkt_a"], l * 8 + b + 1)
                    pe.wait_ge(s["bkt_v"], l * 8 + b + 1)
                    for pair in range(2):
                        for i, n in ((0, 512), (1, 384)):
                            mm = pe.matmul(ps[:, i, 0:n], qb_of(b, pair), b_kt[:, b % 2, pair, 512 * i:512 * i + n],
                                           start=b == 0 and pair == 0, stop=b == 7 and pair == 1)
                    mm.then_inc(s["bs_mm"], 1)

                for b in range(NB_S):
                    pe.wait_ge(s[f"bk_in{b % 2}"], (l * 4 + b // 2 + 1) * 32)
                    if b >= 1:
                        pe.wait_ge(s["bkt_a"], l * 8 + b)
                        pe.wait_ge(s["bkt_v"], l * 8 + b)
                    for pair in range(2):
                        for blk in range(8):
                            lo, n = window_block(blk)
                            at = 2048 + 1024 * pair + lo
                            mm = turn(flat[:, at:at + n], b_rows[0:n, b % 2, blk, 128 * pair:128 * pair + 128], n)
                    mm.then_inc(s["bk_free"], 1)
                    if b >= 1:
                        scores(b - 1)
                scores(7)
                for b in range(NB_S):
                    for pair in range(2):
                        mm = pe.matmul(ps[:, 2, 0:NS], qb_of(b, pair), z[:, 18 + pair, SEQ:NT],
                                       start=b == 0 and pair == 0, stop=b == 7 and pair == 1)
                mm.then_inc(s["bsn"], 1)
                pe.wait_ge(s["bp"], l + 1)
                for blk in range(8):
                    lo, n = window_block(blk)
                    turn(flat[0:n, 128 * blk:128 * blk + 128], b_s[:, lo:lo + n])
                turn(ps[0:NS, 2, 0:128], b_s[:, KEYS_B:KEYS_B + NS]).then_inc(s["bpt_mm"], 1)
                pe.wait_ge(s["bpt_sb"], l + 1)
                for b in range(NB_S):
                    pe.wait_ge(s[f"bv_in{b % 2}"], (l * 4 + b // 2 + 1) * 32)
                    out = ps[0:16, 4 + b // 2, 256 * (b % 2):256 * (b % 2) + 256]
                    alone(pe)
                    pe.matmul(out, b_pt[0:NS, 8, 16 * b:16 * b + 16], vtok[0:NS, 4, 0:256], start=True, stop=False)
                    for blk in range(8):
                        n = window_block(blk)[1]
                        mm = pe.matmul(out, b_pt[0:n, blk, 16 * b:16 * b + 16], bv_rows[0:n, b % 2, blk, :],
                                       start=False, stop=blk == 7)
                    mm.then_inc(s["bv_free"], 1)
                pe.wait_ge(s["b_pv"], l + 1)
                alone(pe)
                for b in range(NB_S):
                    for pair in range(2):
                        mm = turn(ps[:, 0, 32 * b + 16 * pair:32 * b + 16 * pair + 16],
                                  pv_rows[0:16, b, 128 * pair:128 * pair + 128], 16)
                mm.then_inc(s["b_pv_mm"], 1)

            def prompt(l):
                def scores(u):
                    if u >= 2:
                        pe.wait_ge(s["p_max"], l * 32 + u - 1)
                    for mp in range(maps(u)):
                        tq, tk, lo, n = qk_of(u, mp)
                        q0, wid = 128 * (u % 4), 128 * (u % 4 + 1)
                        mm = pe.matmul(ps[:, 2 * (u % 2) + mp, 0:wid], z[lo:lo + n, tq, q0:q0 + 128], z[lo:lo + n, tk, 0:wid],
                                       start=True, stop=True)
                    mm.then_inc(s["p_mm"], 1)

                def turned(u):
                    pe.wait_ge(s["p_soft"], l * 32 + u + 1)
                    if u >= 2:
                        pe.wait_ge(s["ppt_sb"], l * 32 + u - 1)
                    for kb in range(u % 4 + 1):
                        mm = turn(ps[:, 4 + u % 2, 128 * kb:128 * kb + 128], p_s[:, u % 2, 0, 128 * kb:128 * kb + 128])
                    mm.then_inc(s["ppt_mm"], 1)

                def values(u):
                    pe.wait_ge(s["ppt_sb"], l * 32 + u + 1)
                    if u >= 2:
                        pe.wait_ge(s["p_out"], l * 32 + u - 1)
                    v0 = 128 * (u // 8)
                    for kb in range(u % 4 + 1):
                        mm = pe.matmul(ps[:, 6 + u % 2, 0:128], vtok[:, kb, v0:v0 + 128], p_pt[:, u % 2, kb, :],
                                       start=kb == 0, stop=kb == u % 4)
                    mm.then_inc(s["po_mm"], 1)

                pe.wait_ge(s["b_out"], l + 1)
                scores(0)
                for u in range(32 + 2):
                    if u < 31:
                        scores(u + 1)
                    if 1 <= u < 33:
                        turned(u - 1)
                    if u >= 2:
                        values(u - 2)

            def w_out(l):
                def part(o, ks):
                    for k in ks:
                        at = 256 * k + 128 * (o % 2)
                        for h in range(2):
                            mm = pe.matmul(half(2 * (o % 4), h), wslot[:, o // 2 % 2, at:at + 128],
                                           hT[:, k, h * HALF:(h + 1) * HALF], start=k == 0, stop=k == KD - 1)
                    if ks[-1] == KD - 1:
                        mm.then_inc(s["out_done"], 1)

                pe.wait_ge(s["p_out"], l * 32 + 32)
                pe.wait_ge(s["w_loaded0"], (l * 47 + 26 + 1) * 32)
                part(0, range(6))
                for u in range(2):
                    square_sums(l * 14 + 12, u, C("blk64"), sq2, 4)
                part(1, range(6))
                pe.wait_ge(s["gdone"], l * 14 + 16)
                for o in range(2):
                    part(o, range(6, KD))
                for o in range(2, 8):
                    pe.wait_ge(s[f"w_loaded{o // 2 % 2}"], (l * 47 + 26 + o // 4 + 1) * 32)
                    if o >= 4:
                        pe.wait_ge(s["x_out"], l * 8 + o - 3)
                    part(o, range(KD))

            pe.wait_ge(s["setup_ev"], 19)
            with pe.Fori(0, DEPTH) as l:
                norm(l * 3)
                ffn(l, 0)
                pe.wait_ge(s["conv_in"], (l + 1) * 16)
                alone(pe)
                for c in range(12):
                    mm = turn(ps[:, 6, 24 * c:24 * c + 24], conv_in[0:24, 128 * c:128 * c + 128], 24)
                mm.then_inc(s["conv_in_mm"], 1)
                norm(l * 3 + 1)
                project(l)
                with pe.Fori(0, 4) as c:
                    chunk(l, c)
                sample_chunk(l)
                pe.wait_ge(s["st_new"], l * 4 + 4)
                alone(pe)
                for i in range(4):
                    pe.wait_ge(s["gsq"], l * 14 + 8 + i + 1)
                    for h in range(2):
                        mm = pe.matmul(half(2 * i, h), C("ones"), sq2[:, i % 2, h * HALF:(h + 1) * HALF],
                                       start=True, stop=True)
                    mm.then_inc(s["gmm"], 1)
                pe.wait_ge(s["gsqrt"], l * 14 + 8 + 4 + 2)
                alone(pe)
                with pe.Fori(0, 2) as g:
                    group_c(l, g)
                sample_b(l)
                prompt(l)
                w_out(l)
                norm(l * 3 + 2)
                ffn(l, 1)
            norm(6)
            pe.wait_ge(s["h_done"], 56)
            for b in range(5):
                n = 128 if b < 4 else NS
                if b >= 2:
                    pe.wait_ge(s["y_rows"], b - 1)
                for k in range(KD):
                    at = 1024 * (b % 2) + 128 * k
                    mm = turn(flat[0:n, at:at + 128], hT[:, k, 128 * b:128 * b + n])
                mm.then_inc(s["y_mm"], 1)

        @block.scalar
        def _(act):
            for name in ("gsqrt", "conv_done", "proj_a"):
                act.sem_inc(s[name], 2)
            act.sem_inc(s["o_out"], 1)
            eps, one = C("eps"), C("one")

            def copy(out, in_, scale=1.0):
                return act.activation(out, in_, ACT.Copy, scale=scale)

            act.wait_ge(s["in_lam"], 16 * 8)
            act.wait_ge(s["in_const"], 16)
            act.activation(a_log_c, a_log_c, ACT.Exp)
            act.wait_ge(s["lam_sums"], 1)
            act.activation(lam_sum, lam_sum, ACT.Exp).then_inc(s["lam_exp"], 1)

            def square(n, k, done, count):
                act.wait_ge(s[done], count)
                act.wait_ge(s["sq_added"], n * 8 + k + 1)
                alone(act)
                act.activation(gated[:, 1, :], xT[:, ds(k, 1), :].rearrange("p a n -> p (a n)"), ACT.Square)\
                    .then_inc(s["sq_done"], 1)

            def norm(n):
                act.wait_ge(s["ssq_done"], n + 1)
                act.activation(tok(gated[:, 0, :]), both(0), ACT.Sqrt, bias=eps, scale=1.0 / D).then_inc(s["rms"], 1)

            def ffn(l, w):
                it = l * 2 + w
                with act.Fori(0, 11) as j:
                    for slot in range(2):
                        act.wait_ge(s["gu_done"], it * 22 + j * 2 + slot + 1)
                        act.wait_ge(s["gu_free"], it * 22 + j * 2 + slot + 1)
                        act.activation(tok(gated[:, slot, :]), both(4 * slot), ACT.Silu).then_inc(s["silu"], 1)
                with act.Fori(0, 8) as o:
                    square(l * 3 + 2 * w + 1, o, "down_free", it * 8 + o + 3)

            def tile_of(v, i):
                return v[:, ds(i, 1), :].rearrange("p a n -> p (a n)")

            def square_of(base, u, src, sqb):
                act.wait_ge(s["gmm"], base + u + 1)
                act.activation(sqb[:, u, :], src, ACT.Square).then_inc(s["gsq"], 1)

            def root_of(base, u, rnb, scale, bank=0):
                act.wait_ge(s["gmm"], base + u + 3)
                act.wait_ge(s["gdone"], base + u + 1)
                act.activation(tok(rnb[:, u, :]), both(bank + 2 * u), ACT.Sqrt, bias=eps, scale=scale).then_inc(s["gsqrt"], 1)

            def project(l):
                def evacuate(j, slot, bank):
                    act.wait_ge(s["proj_done"], l * 28 + j * 4 + slot * 2 + 1)
                    dst = z[:, ds(j * 4 + slot * 2, 1), :].rearrange("p a (h n) -> p (a h) n", h=2)
                    copy(dst, both(bank)).then_inc(s["proj_a"], 1)

                with act.Fori(0, 3) as j:
                    for slot in range(2):
                        evacuate(j, slot, 4 * slot)
                        for u in range(2):
                            act.wait_ge(s["conv_acc"], l * 12 + j * 4 + slot * 2 + u + 1)
                            alone(act)
                            act.activation(tile_of(z, j * 4 + slot * 2 + u), cvt[:, u, :], ACT.Silu)\
                                .then_inc(s["conv_done"], 1)
                act.drain()
                with act.Fori(3, 7) as j:
                    for slot in range(2):
                        square_of(l * 14 + j * 2 - 6, slot, tile_of(z, j * 2 - 6 + slot), sq)
                        evacuate(j, slot, 0)
                        root_of(l * 14 + j * 2 - 6, slot, rn, 1.0, 4)
                act.wait_ge(s["ba_sb"], l + 1)
                act.activation(beta[:, :, :], ba[:, :, 0:4], ACT.Sigmoid)
                act.activation(spa[:, :, :], spa[:, :, :], ACT.Exp)
                act.drain()
                act.activation(spa[:, :, :], spa[:, :, :], ACT.Ln, bias=one).then_inc(s["soft"], 1)
                for b in range(5):
                    n = 128 if b < 4 else NS
                    act.wait_ge(s["rows_mm"], l * 5 + b + 1)
                    a = 3 + 2 * (b % 2)
                    copy(k_rows[0:n, b, 256:512], ps[0:n, a, 0:256])
                    copy(vtok[0:n, b, 256:512], ps[0:n, a, 256:512]).then_inc(s["rows_v"], 1)
                act.wait_ge(s["conv_rows_mm"], l + 1)
                copy(conv_out[0:27, :], flat[0:27, 2560:2560 + CONV_CH]).then_inc(s["conv_rows"], 1)

            def two(bank):
                return ps[:, bank, 0:256].rearrange("p (h n) -> p h n", h=2)

            def stage(c, names, done):
                for name in names:
                    i = ("qc", "kc", "vc").index(name)
                    last = copy(m[name][:, :, :], z[:, 4 * i:4 * i + 4, ds(c * 128, 128)])
                last.then_inc(s[done], 1)

            def chunk(l, c, more):
                it = l * 4 + c
                act.wait_ge(s["dt_arg"], it + 1)
                act.activation(m["DT"][:, :, :], m["DT"][:, :, :], ACT.Exp).then_inc(s["dt_exp"], 1)
                act.activation(m["eG"][:, :, :], ps[:, 2, :].rearrange("p (h n) -> p h n", h=4), ACT.Exp)
                act.activation(ecol[:, :], gc[:, :], ACT.Exp)
                act.activation(kde[:, :], kde[:, :], ACT.Exp).then_inc(s["exp_done"], 1)
                act.wait_ge(s["bege"], it + 1)
                act.wait_ge(s["tokm"], it + 1)
                for h in range(NH):
                    hs = slice(128 * h, 128 * h + 128)
                    copy(m["KB"][:, h, :], ps[:, 0, hs], bege[:, h:h + 1])
                    copy(m["KD"][:, h, :], ps[:, 0, hs], kde[:, h:h + 1])
                    last = copy(m["VB"][:, h, :], ps[:, 1, hs], m["bB"][:, h, 0:1])
                last.then_inc(s["kv_done"], 1)
                with act.Fori(1, 7) as k:
                    for a in range(2):
                        act.wait_ge(s["m_mm"], it * 12 + k * 2 + a - 1)
                        copy(m["M"][:, 2 * a:2 * a + 2, :], two(4 if a else 7)).then_inc(s["m_sb"], 1)
                act.wait_ge(s["w_mm"], it + 1)
                copy(m["nW"][:, :, :], ps[:, 7, :].rearrange("p (h n) -> p h n", h=4), -1.0).then_inc(s["nw_sb"], 1)
                if more:
                    stage(c + 1, ("kc", "vc"), "staged_kv")
                act.wait_ge(s["o_mm"], it + 1)
                if more:
                    stage(c + 1, ("qc",), "staged_q")
                copy(hT[:, 0:4, ds(c * 128, 128)], ps[:, 3, :].rearrange("p (h n) -> p h n", h=4)).then_inc(s["o_out"], 1)

            def sample_chunk(l):
                act.wait_ge(s["state_done"], l * 5 + 5)
                for i, name in enumerate(("qc", "kc", "vc")):
                    last = copy(t[name][:, :, :], z[:, 4 * i:4 * i + 4, SEQ:NT])
                last.then_inc(s["x_act"], 1)
                act.wait_ge(s["x_dt"], l + 1)
                act.activation(t["DT"][0:NS], t["DT"][0:NS], ACT.Exp)
                act.activation(t["eG"][:, :, :], ps[:, 2, 0:128].rearrange("p (h n) -> p h n", h=4), ACT.Exp)
                act.activation(secol[0:NS, :], sgc[0:NS, :], ACT.Exp)
                act.activation(skde[0:NS, :], skde[0:NS, :], ACT.Exp).then_inc(s["x_act"], 1)
                act.wait_ge(s["x_bege"], l + 1)
                for h in range(NH):
                    hs = slice(128 * h, 128 * h + 128)
                    copy(t["KB"][0:NS, h, :], ps[0:NS, 0, hs], sbege[0:NS, h:h + 1])
                    copy(t["KD"][0:NS, h, :], ps[0:NS, 0, hs], skde[0:NS, h:h + 1])
                    last = copy(t["VB"][0:NS, h, :], ps[0:NS, 1, hs], t["bB"][0:NS, h, 0:1])
                last.then_inc(s["x_act"], 1)
                act.wait_ge(s["x_m"], l + 1)
                copy(t["M"][0:NS], ps[0:NS, 7, 0:128].rearrange("p (h n) -> p h n", h=4)).then_inc(s["x_act"], 1)
                act.wait_ge(s["x_w"], l + 1)
                copy(t["WQ"][:, :, :, 0:4], ps[:, 7, 0:128].rearrange("p (h b t) -> p h b t", h=4, b=8)).then_inc(s["x_act"], 1)

            def group_c(l, g):
                G = l * 2 + g
                for n in range(16):
                    act.wait_ge(s["ck_free"], G * 16 + n + 5)
                    act.wait_ge(s["cs_mm"], G * 16 + n + 1)
                    copy(c_kt[:, n % 2, 0, :], ps[:, 4 + 2 * (n % 2), :]).then_inc(s["kt_a"], 1)
                act.wait_ge(s["c_max"], G + 1)
                act.activation(c_s[:, :], c_s[:, :], ACT.Exp, bias=c_mx[:, 1:2], accum_out=c_mx[:, 2:3]).then_inc(s["c_exp"], 1)
                act.wait_ge(s["cpt_mm"], G + 1)
                copy(c_pt[:, 0:16, :], flat[:, 0:1024].rearrange("p (k n) -> p k n", k=16))
                copy(c_pt[0:NS, 16, :], ps[0:NS, 2, 0:64]).then_inc(s["cpt_sb"], 1)
                act.wait_ge(s["cv_free"], G * 16 + 20)
                copy(pv_rows[0:16, 0:4, :], flat[0:16, 2048:3072].rearrange("p (b n) -> p b n", b=4)).then_inc(s["c_pv"], 1)

            def sample_b(l):
                for b in range(NB_S):
                    act.wait_ge(s["bk_free"], l * 8 + b + 3)
                    act.wait_ge(s["bs_mm"], l * 8 + b + 1)
                    copy(b_kt[:, b % 2, 0, :], flat[:, 2048:2048 + KEYS_B]).then_inc(s["bkt_a"], 1)
                act.wait_ge(s["b_max"], l + 1)
                act.activation(b_s[:, :], b_s[:, :], ACT.Exp, bias=c_mx[:, 1:2], accum_out=c_mx[:, 2:3]).then_inc(s["b_exp"], 1)
                act.wait_ge(s["bpt_mm"], l + 1)
                copy(b_pt[:, 0:4, :], flat[:, 0:512].rearrange("p (k n) -> p k n", k=4))
                copy(b_pt[0:96, 4:8, :], flat[0:96, 512:1024].rearrange("p (k n) -> p k n", k=4))
                copy(b_pt[0:NS, 8, :], ps[0:NS, 2, 0:128]).then_inc(s["bpt_sb"], 1)
                act.wait_ge(s["bv_free"], l * 8 + 10)
                copy(pv_rows[0:16, :, :], flat[0:16, 2048:4096].rearrange("p (b n) -> p b n", b=8)).then_inc(s["b_pv"], 1)

            def prompt(l):
                for u in range(33):
                    if u < 32:
                        wid = 128 * (u % 4 + 1)
                        act.wait_ge(s["p_max"], l * 32 + u + 1)
                        for mp in range(maps(u)):
                            row = p_s[:, u % 2, mp, 0:wid]
                            last = act.activation(row, row, ACT.Exp, bias=p_mx[:, u % 2, 2 + mp:3 + mp],
                                                  accum_out=p_mx[:, u % 2, 4 + mp:5 + mp])
                        last.then_inc(s["p_exp"], 1)
                    if u >= 1:
                        v = u - 1
                        n = v % 4 + 1
                        act.wait_ge(s["ppt_mm"], l * 32 + v + 1)
                        if v >= 2:
                            act.wait_ge(s["po_mm"], l * 32 + v - 1)
                        copy(p_pt[:, v % 2, 0:n, :], ps[:, 4 + v % 2, 0:128 * n].rearrange("p (k n) -> p k n", k=n))\
                            .then_inc(s["ppt_sb"], 1)

            act.wait_ge(s["x_new"], 1)
            for k in range(KD):
                act.activation(hT[:, k, :], xT[:, k, :], ACT.Square).then_inc(s["sq_done"], 1)
            act.wait_ge(s["setup_ev"], 11)
            act.dma_start(scratch[:, :], table[0:8, :]).then_inc(s["table_out"], 16)
            act.wait_ge(s["table_out"], 16)
            for h in range(8):
                src = bass.AP(tensor=scratch.tensor, offset=h * U_TAB + U_MAX - 384 - 127, ap=[[1, 128], [1, SEQ]])
                act.dma_start(strip_raw[:, h, :], src).then_inc(s["in_strip"], 16)
            for step in range(T_S):
                off = T_S - 1 - step
                for b in range(4):
                    act.dma_start(win_c[32 * b + step:32 * b + 32:4, 0:PAST + T_S],
                                  bass.AP(tensor=scratch.tensor, offset=4 * U_TAB + off,
                                          ap=[[U_TAB, 4], [0, 2], [1, PAST + T_S]])).then_inc(s["in_rows"], 16)
                act.dma_start(win_b[step:128:4, 0:PAST + T_S],
                              bass.AP(tensor=scratch.tensor, offset=off,
                                      ap=[[0, 8], [U_TAB, 4], [1, PAST + T_S]])).then_inc(s["in_rows"], 16)
            with act.Fori(0, DEPTH) as l:
                norm(l * 3)
                ffn(l, 0)
                norm(l * 3 + 1)
                project(l)
                act.wait_ge(s["gdone"], l * 14 + 10)
                alone(act)
                stage(0, ("kc", "vc"), "staged_kv")
                stage(0, ("qc",), "staged_q")
                with act.Fori(0, 3) as c:
                    chunk(l, c, True)
                chunk(l, 3, False)
                sample_chunk(l)
                act.activation(z[:, 12:16, :], z[:, 12:16, :], ACT.Silu)
                act.wait_ge(s["x_so"], l + 1)
                alone(act)
                act.drain()
                for i in range(4):
                    act.wait_ge(s["gmm"], l * 14 + 8 + i + 1)
                    act.activation(sq2[:, i % 2, :], hT[:, i, :], ACT.Square).then_inc(s["gsq"], 1)
                for i in range(4):
                    act.wait_ge(s["gmm"], l * 14 + 8 + i + 3)
                    act.activation(tok(rn4[:, i, :]), both(2 * i), ACT.Sqrt, bias=eps, scale=1.0 / DK).then_inc(s["gsqrt"], 1)
                with act.Fori(0, 2) as g:
                    group_c(l, g)
                sample_b(l)
                prompt(l)
                act.wait_ge(s["p_out"], l * 32 + 32)
                for u in range(2):
                    square_of(l * 14 + 12, u, hT[:, 6 + u, :], sq2)
                for u in range(2):
                    root_of(l * 14 + 12, u, rn4, 1.0 / 64, 4)
                for o in range(8):
                    square(l * 3 + 2, o, "x_out", l * 8 + o + 1)
                norm(l * 3 + 2)
                ffn(l, 1)
            norm(6)

        @block.vector
        def _(dve):
            for name in ("gu_free", "down_free", "proj_v", "gdone"):
                dve.sem_inc(s[name], 2)
            dve.sem_inc(s["sq_added"], 1)
            cp = dve.tensor_copy
            stt = dve.scalar_tensor_tensor

            dve.memset(small[:, 32:160], 0.0)
            dve.drain()
            dve.wait_ge(s["in_const"], 16)
            dve.wait_ge(s["in_lam"], 16 * 8)
            for i in range(2):
                dve.tensor_tensor(lam_prod[:, i, :], lam_rows[:, 2 * i, :], lam_rows[:, 2 * i + 1, :], ALU.mult)
            dve.drain()
            for i in range(2):
                for l in range(DEPTH):
                    last = dve.reduce_sum(small[:, 16 + 2 * i + l:17 + 2 * i + l], lam_prod[:, i, 32 * l:32 * l + 32], AX)
            last.then_inc(s["lam_sums"], 1)
            dve.wait_ge(s["lam_exp"], 1)
            dve.tensor_tensor(lam_all, lam_sum[:, 0:2], lam_sum[:, 2:4], ALU.subtract)
            dve.drain()
            dve.tensor_tensor(lam_all, lam_all, C("lam0"), ALU.add)
            for i in range(1, 6):
                n = 128 if i < 5 else NS
                dve.wait_ge(s["setup_mm"], i)
                at = 1024 * (i % 2)
                cp(xT[:, :, 128 * (i - 1):128 * (i - 1) + n],
                   flat[:, at:at + 8 * n].rearrange("p (k n) -> p k n", k=KD)).then_inc(s["setup_ev"], 1)
            dve.drain().then_inc(s["x_new"], 1)
            dve.wait_ge(s["setup_mm"], 6)
            cp(cols_conv[:, :], ps[:, 0, 0:96])
            cp(cols_norm[:, :], ps[:, 0, 96:156]).then_inc(s["setup_ev"], 1)
            for c in range(5):
                i, n = 7 + c, min(512, U_TAB - 512 * c)
                dve.wait_ge(s["setup_mm"], i)
                cp(table[0:8, 512 * c:512 * c + n], ps[0:8, 2 * (i % 2), 0:n]).then_inc(s["setup_ev"], 1)
            dve.memset(gated[:, 0, :], 0.0)
            for k in range(KD):
                dve.wait_ge(s["sq_done"], k + 1)
                dve.drain()
                dve.tensor_tensor(gated[:, 0, :], gated[:, 0, :], hT[:, k, :], ALU.add).then_inc(s["sq_added"], 1)
            for h in range(8):
                i = 12 + h
                dve.wait_ge(s["setup_mm"], i)
                cp(strips[:, h, :], ps[:, 2 * (i % 2), :]).then_inc(s["setup_ev"], 1)
            dve.wait_ge(s["in_rows"], 16 * 5 * T_S)
            for g in range(2):
                dve.tensor_tensor(bias_cn[:, g, :].rearrange("p (b t) -> p b t", b=8), per_head(win_c[:, PAST:PAST + T_S], 8),
                                  over(C("offc")[:, 8 * g:8 * g + 8], T_S), ALU.add)
            dve.tensor_tensor(bias_bn[:, :].rearrange("p (b t) -> p b t", b=8), per_head(win_b[:, PAST:PAST + T_S], 8),
                              over(C("offb"), T_S), ALU.add)
            cp(bias_b[:, 0:512].rearrange("p (r k) -> p r k", r=4), win_b[:, 1536:PAST].rearrange("p (k r) -> p r k", r=4))
            cp(bias_b[:, 512:KEYS_B].rearrange("p (r k) -> p r k", r=4),
               win_b[:, 0:1536].rearrange("p (k r) -> p r k", r=16)[:, 0:4, :])
            cp(bias_c[:, 0:PAST].rearrange("p (c r k) -> p c r k", c=4, r=4),
               win_c[:, 0:PAST].rearrange("p (c k r) -> p c r k", c=4, r=4))
            dve.wait_ge(s["in_pages"], 64)
            cp(row_f[:, :], page_of[:, :])
            dve.drain()
            dve.tensor_scalar(row_f[:, :], row_f[:, :], float(PAGE // 4), C("p32"), ALU.mult, ALU.add)
            dve.drain()
            for l in range(DEPTH):
                dve.tensor_scalar(key_rows[:, l, :], row_f[:, :], float(l * POOL_PAGES * PAGE // 4), None, ALU.add)
            dve.drain()

            def add_square(n, k):
                dve.wait_ge(s["sq_done"], n * 8 + k + 1)
                dve.tensor_tensor(gated[:, 0, :], gated[:, 0, :], gated[:, 1, :], ALU.add).then_inc(s["sq_added"], 1)
                dve.drain()

            def norm(n, gains):
                dve.wait_ge(s["rms"], n + 1)
                rstd = gated[:, 0, :]
                dve.reciprocal(rstd, rstd)
                dve.drain()
                for k in range(KD):
                    stt(hT[:, k, :], xT[:, k, :], gains[:, k:k + 1], rstd, ALU.mult, ALU.mult).then_inc(s["h_done"], 1)

            def ffn(l, w):
                it = l * 2 + w
                with dve.Fori(0, 11) as j:
                    for slot in range(2):
                        dve.wait_ge(s["silu"], it * 22 + j * 2 + slot + 1)
                        dst = hidden[:, ds(j * 2 + slot, 1), :].rearrange("p a (h n) -> p (a h) n", h=2)
                        dve.tensor_tensor(dst, tok(gated[:, slot, :]), both(4 * slot + 2), ALU.mult).then_inc(s["gu_free"], 1)
                dve.drain()
                dve.memset(gated[:, 0, :], 0.0)
                dve.drain()
                with dve.Fori(0, 4) as j:
                    for u in range(2):
                        dve.wait_ge(s["down_done"], it * 8 + j * 2 + u + 2)
                        x = xT[:, ds(j * 2 + u, 1), :].rearrange("p a (h n) -> p (a h) n", h=2)
                        stt(x, both(4 * u), 0.5, x, ALU.mult, ALU.add).then_inc(s["down_free"], 1)
                        add_square(l * 3 + 2 * w + 1, j * 2 + u)
                dve.drain().then_inc(s["x_new"], 1)

            def tile_of(v, i):
                return v[:, ds(i, 1), :].rearrange("p a n -> p (a n)")

            def tile_pair(v, g):
                return v[:, ds(g * 2, 2), :]

            def inverse_root(base, u, rnb):
                dve.wait_ge(s["gsqrt"], base + u + 3)
                dve.reciprocal(rnb[:, u, :], rnb[:, u, :])
                dve.drain()

            def project(l):
                def evacuate(j, slot, bank):
                    dve.wait_ge(s["proj_done"], l * 28 + j * 4 + slot * 2 + 2)
                    dst = z[:, ds(j * 4 + slot * 2 + 1, 1), :].rearrange("p a (h n) -> p (a h) n", h=2)
                    cp(dst, both(bank + 2)).then_inc(s["proj_v"], 1)

                def convolve(c, u):
                    zc, acc = tile_of(z, c), cvt[:, u, :]
                    zs = zc[:, SEQ:NT].rearrange("p (b t) -> p b t", b=8)
                    acc_s = acc[:, SEQ:NT].rearrange("p (b t) -> p b t", b=8)
                    xc = xs[:, ds(c, 1), :, :].rearrange("p a b t -> p (a b) t")
                    tail = conv_tail[:, ds(c, 1), :].rearrange("p a n -> p (a n)")
                    cp(tail[:, 0:3], zc[:, SEQ - 3:SEQ])
                    cp(tail[:, 3:27].rearrange("p (b j) -> p b j", b=8), zs[:, :, 1:4])
                    cp(xc[:, :, 3:7], zs)
                    dve.wait_ge(s["conv_done"], l * 12 + c + 1)
                    for tap in (3, 2, 1, 0):
                        cw = lay_conv[:, ds(c + 12 * tap, 1)]
                        d = 3 - tap
                        if tap == 3:
                            dve.tensor_scalar(acc[:, 0:SEQ], zc[:, 0:SEQ], cw, None, ALU.mult)
                            dve.drain()
                            last = dve.tensor_scalar(acc_s, xc[:, :, 3:7], cw, None, ALU.mult)
                        else:
                            dve.drain()
                            stt(acc[:, d:SEQ], zc[:, 0:SEQ - d], cw, acc[:, d:SEQ], ALU.mult, ALU.add)
                            last = stt(acc_s, xc[:, :, tap:tap + 4], cw, acc_s, ALU.mult, ALU.add)
                    last.then_inc(s["conv_acc"], 1)

                with dve.Fori(0, 3) as j:
                    for slot in range(2):
                        evacuate(j, slot, 4 * slot)
                        dve.wait_ge(s["proj_a"], l * 14 + j * 2 + slot + 3)
                        convolve(j * 4 + slot * 2, 0)
                        convolve(j * 4 + slot * 2 + 1, 1)
                with dve.Fori(3, 5) as j:
                    for slot in range(2):
                        evacuate(j, slot, 0)
                        inverse_root(l * 14 + j * 2 - 6, slot, rn)
                        q = tile_of(z, j * 2 - 6 + slot)
                        stt(q, q, DK ** -0.5, rn[:, slot, :], ALU.mult, ALU.mult).then_inc(s["gdone"], 1)
                with dve.Fori(5, 7) as j:
                    for slot in range(2):
                        evacuate(j, slot, 0)
                        inverse_root(l * 14 + j * 2 - 6, slot, rn)
                        k = tile_of(z, j * 2 - 6 + slot)
                        dve.tensor_tensor(k, k, rn[:, slot, :], ALU.mult).then_inc(s["gdone"], 1)
                dve.drain().then_inc(s["conv_tail"], 1)
                dve.wait_ge(s["ba_mm"], l + 1)
                cp(ba[:, 0:4, :], ps[:, 0, 0:32].rearrange("p (b n) -> p b n", b=4))
                cp(ba[0:NS, 4, :], ps[0:NS, 0, 32:40])
                dve.drain()
                dve.tensor_tensor(spb[:, :, :], ba[:, :, 4:8], per_head(dtb, 5), ALU.add)
                dve.drain()
                stt(spa[:, :, :], spb[:, :, :], -1.0, spb[:, :, :], ALU.mult, ALU.min).then_inc(s["ba_sb"], 1)
                for b in range(5):
                    n = 128 if b < 4 else NS
                    dve.wait_ge(s["rows_mm"], l * 5 + b + 1)
                    a = 2 + 2 * (b % 2)
                    cp(k_rows[0:n, b, 0:256], ps[0:n, a, 0:256])
                    cp(vtok[0:n, b, 0:256], ps[0:n, a, 256:512]).then_inc(s["rows_a"], 1)
                dve.wait_ge(s["soft"], l + 1)
                stt(spb[:, :, :], spb[:, :, :], 0.0, spa[:, :, :], ALU.max, ALU.add)
                dve.drain()
                stt(gdec[:, :, :], spb[:, :, :], -1.0, per_head(ea, 5), ALU.mult, ALU.mult)

            def four(bank, n=128):
                return ps[:, bank, 0:4 * n].rearrange("p (h n) -> p h n", h=4)

            def two(bank):
                return ps[:, bank, 0:256].rearrange("p (h n) -> p h n", h=2)

            def spread(c):
                cp(m["gB"][:, :, :], over(gdec[:, ds(c, 1), :].rearrange("p a h -> p (a h)"), 128))
                cp(m["bB"][:, :, :], over(beta[:, ds(c, 1), :].rearrange("p a h -> p (a h)"), 128)).then_inc(s["gb"], 1)

            def chunk(l, c, more):
                it = l * 4 + c
                dve.wait_ge(s["decay_mm"], it + 1)
                cp(gc[:, :], ps[:, 4, 0:4])
                dve.drain()
                for h in range(NH):
                    stt(m["DT"][:, h, :], ps[:, 2, 128 * h:128 * h + 128], gc[:, h:h + 1], C("neg"), ALU.subtract, ALU.add)
                dve.tensor_tensor(kde[:, :], four(2)[:, :, 127], gc[:, :], ALU.subtract).then_inc(s["dt_arg"], 1)
                dve.wait_ge(s["dt_exp"], it + 1)
                dve.wait_ge(s["kkqk"], it + 1)
                dve.tensor_tensor(m["LT"][:, :, :], m["DT"][:, :, :], four(5), ALU.mult)
                dve.drain()
                dve.tensor_tensor(m["LT"][:, :, :], m["LT"][:, :, :], four(3), ALU.mult)
                dve.drain()
                dve.tensor_tensor(m["LK"][:, :, :], m["LT"][:, :, :], per_head(C("lm")[:, 0:128]), ALU.mult)
                dve.wait_ge(s["exp_done"], it + 1)
                dve.tensor_tensor(bege[:, :], m["bB"][:, :, 0], ecol[:, :], ALU.mult).then_inc(s["bege"], 1)
                dve.drain()
                dve.tensor_tensor(m["U"][:, :, :], per_head(C("ident")), m["LK"][:, :, :], ALU.subtract).then_inc(s["u_up"], 2)
                dve.drain()
                dve.tensor_tensor(m["LK"][:, :, :], m["LT"][:, :, :], per_head(C("lm")[:, 128:256]), ALU.mult)
                dve.tensor_tensor(m["QKT"][:, :, :], m["DT"][:, :, :], four(6), ALU.mult)
                dve.wait_ge(s["t_mm"], it + 1)
                dve.wait_ge(s["rows_out"], l * 160 + 160)
                cp(m["T"][:, :, :].rearrange("p (a h) n -> p a (h n)", a=2), ps[:, 2:4, 0:256]).then_inc(s["t_up"], 2)
                dve.tensor_tensor(m["qc"][:, :, :], m["qc"][:, :, :], m["eG"][:, :, :], ALU.mult)

                def level(k, last=False):
                    if not last:
                        dve.wait_ge(s["m_mm"], it * 12 + k * 2)
                        dve.tensor_tensor(m["LK"][:, :, :], m["LT"][:, :, :], per_head(C("lm")[:, ds(k * 128 + 128, 128)]),
                                          ALU.mult)
                    dve.drain()
                    for a in range(2):
                        hs = slice(2 * a, 2 * a + 2)
                        if not last:
                            dve.wait_ge(s["tm_mm"], it * 10 + k * 2 + a - 1)
                            dve.tensor_tensor(m["T"][:, hs], m["T"][:, hs], two(2 + a), ALU.subtract).then_inc(s["t_up"], 1)
                        dve.wait_ge(s["mu_mm"], it * 12 + k * 2 + a - 1)
                        dve.tensor_tensor(m["U"][:, hs], m["U"][:, hs], two(5 + a), ALU.subtract).then_inc(s["u_up"], 1)

                with dve.Fori(1, 6) as k:
                    level(k)
                level(6, last=True)
                dve.wait_ge(s["vn_mm"], it + 1)
                cp(m["VN"][:, :, :], four(2)).then_inc(s["vn_sb"], 1)
                if more:
                    spread(c + 1)
                dve.wait_ge(s["s_mm"], it + 1)
                for h in range(NH):
                    last = stt(m["S"][:, h, :], m["S"][:, h, :], m["eG"][:, h, 127:128], ps[:, 7, 128 * h:128 * h + 128],
                               ALU.mult, ALU.add)
                last.then_inc(s["state_done"], 1)

            def sample_chunk(l):
                q = slice(0, NS)

                def four_s(bank):
                    return ps[0:NS, bank, 0:128].rearrange("p (h n) -> p h n", h=4)

                cp(t["gB"][q], over(gdec[q, 4, :], 128))
                cp(t["bB"][q], over(beta[q, 4, :], NS)).then_inc(s["x_gb"], 1)
                dve.wait_ge(s["x_decay"], l + 1)
                cp(sgc[q, :], ps[q, 4, 0:4])
                dve.drain()
                for h in range(NH):
                    stt(t["DT"][q, h, :], ps[q, 2, NS * h:NS * h + NS], sgc[q, h:h + 1], C("neg4", NS), ALU.subtract, ALU.add)
                dve.tensor_tensor(skde[q, :], ps[q, 4, 4:8], sgc[q, :], ALU.subtract).then_inc(s["x_dt"], 1)
                dve.wait_ge(s["x_act"], l * 5 + 2)
                dve.tensor_tensor(sbege[q, :], t["bB"][q, :, 0], secol[q, :], ALU.mult).then_inc(s["x_bege"], 1)
                dve.wait_ge(s["x_kkqk"], l + 1)
                dve.tensor_tensor(t["LT"][q], t["DT"][q], four_s(5), ALU.mult)
                dve.tensor_tensor(t["QKT"][q], t["DT"][q], four_s(6), ALU.mult)
                dve.drain()
                dve.tensor_tensor(t["LT"][q], t["LT"][q], four_s(3), ALU.mult)
                dve.drain()
                dve.tensor_tensor(t["LK"][q], t["LT"][q], per_head(C("lm", NS)[:, 0:NS]), ALU.mult)
                dve.drain()
                dve.tensor_tensor(t["U"][q], per_head(C("ident", NS)[:, 0:NS]), t["LK"][q], ALU.subtract).then_inc(s["x_u"], 1)
                dve.drain()
                dve.tensor_tensor(t["LK"][q], t["LT"][q], per_head(C("lm", NS)[:, 128:128 + NS]), ALU.mult)
                dve.wait_ge(s["x_t"], l + 1)
                cp(t["T"][q], four_s(6)).then_inc(s["x_lt"], 1)
                dve.wait_ge(s["x_mu"], l + 1)
                dve.tensor_tensor(t["U"][q], t["U"][q], four_s(5), ALU.subtract).then_inc(s["x_u"], 1)
                dve.tensor_tensor(t["WQ"][:, :, :, 4:8], t["qc"][:, :, :].rearrange("p h (b t) -> p h b t", b=8),
                                  t["eG"][:, :, :].rearrange("p h (b t) -> p h b t", b=8), ALU.mult).then_inc(s["x_qe"], 1)
                dve.wait_ge(s["x_ws"], l + 1)
                wsq = ps[:, 2, 0:256].rearrange("p (h b u) -> p h b u", h=4, b=8)
                cp(t["QS"][:, :, :].rearrange("p h (b t) -> p h b t", b=8), wsq[:, :, :, 4:8])
                dve.tensor_scalar(t["nW"][:, :, :].rearrange("p h (b t) -> p h b t", b=8), wsq[:, :, :, 0:4], -1.0, None,
                                  ALU.mult).then_inc(s["x_nw"], 1)
                for h in range(NH):
                    last = t["eG"][:, h, :].rearrange("p (b t) -> p b t", b=8)[:, :, 3]
                    dve.tensor_tensor(t["st"][:, h], t["st"][:, h], over(last, 128), ALU.mult)
                dve.wait_ge(s["x_vn"], l + 1)
                cp(t["VN"][q], ps[q, 3, :].rearrange("p (h n) -> p h n", h=4)).then_inc(s["x_vnsb"], 1)
                dve.wait_ge(s["x_o"], l + 1)
                dve.tensor_tensor(hT[:, 0:4, SEQ:NT], t["QS"][:, :, :], four(4, NS), ALU.add).then_inc(s["x_so"], 1)
                dve.drain()
                for h in range(NH):
                    if h >= 2:
                        dve.wait_ge(s["x_s"], l * 4 + h - 1)
                    dve.tensor_tensor(vblk[h % 2][q], per_head(t["VN"][q, h, :], 8), over(C("bsel", NS), 128),
                                      ALU.mult).then_inc(s["x_vb"], 1)
                    if h >= 1:
                        add_state(l, h - 1)
                add_state(l, 3)
                dve.wait_ge(s["delta_out"], l * 16 + 16)
                alone(dve)

            def add_state(l, h):
                dve.wait_ge(s["x_s"], l * 4 + h + 1)
                at = 3072 if h % 2 else 0
                dve.tensor_tensor(t["st"][:, h], t["st"][:, h], flat[:, at:at + 1024].rearrange("p (b v) -> p b v", b=8),
                                  ALU.add).then_inc(s["st_new"], 1)

            def group_c(l, g):
                G = l * 2 + g
                scale = 32 ** -0.5
                for pair in range(2):
                    for quad in range(4):
                        h2, mp = quad // 2, quad % 2
                        rows = slice(32 * quad, 32 * quad + 32)
                        off = 128 * pair + (2 * pair + h2) * 8 + mp * 4
                        dst = qc_all.rearrange("p (b x) -> p b x", b=4)[rows, :, off:off + 4]
                        src = z[rows, 22 + pair, ds(g * 16 + SEQ, 16)].rearrange("p (b t) -> p b t", b=4)
                        last = cp(dst, src)
                last.then_inc(s["cq"], 1)

                def logits(kc):
                    cols = slice(512 * kc, 512 * kc + 512)
                    dve.wait_ge(s["cs_mm"], G * 16 + 12 + kc + 1 + 2)
                    stt(c_s[:, cols], ps[:, kc, :], scale, bias_c[:, cols], ALU.mult, ALU.add)
                    dve.drain()
                    dve.reduce_max(c_mx[:, 4 + kc:5 + kc], c_s[:, cols], AX)

                for n in range(16):
                    dve.wait_ge(s["ck_free"], G * 16 + n + 5)
                    dve.wait_ge(s["cs_mm"], G * 16 + n + 1)
                    cp(c_kt[:, n % 2, 1, :], ps[:, 5 + 2 * (n % 2), :]).then_inc(s["kt_v"], 1)
                    if n == 14:
                        dve.wait_ge(s["st_out"], l * 64 + 64)
                        alone(dve)
                    if n >= 14:
                        logits(n - 14)
                for kc in (2, 3):
                    logits(kc)
                dve.wait_ge(s["csn"], G + 1)
                stt(c_s[:, PAST:PAST + NS], ps[:, 4, 0:NS], scale, bias_cn[:, ds(g, 1), :].rearrange("p a n -> p (a n)"),
                    ALU.mult, ALU.add)
                dve.drain()
                dve.reduce_max(c_mx[:, 8:9], c_s[:, PAST:PAST + NS], AX)
                dve.drain()
                dve.reduce_max(c_mx[:, 0:1], c_mx[:, 4:9], AX)
                dve.drain()
                dve.tensor_scalar(c_mx[:, 1:2], c_mx[:, 0:1], -1.0, None, ALU.mult).then_inc(s["c_max"], 1)
                dve.wait_ge(s["c_exp"], G + 1)
                dve.reciprocal(c_mx[:, 3:4], c_mx[:, 2:3])
                dve.drain()
                dve.tensor_scalar(comb[:, :], C("comb"), c_mx[:, 3:4], sign, ALU.mult, ALU.mult).then_inc(s["comb"], 1)
                for u in range(2):
                    inverse_root(l * 14 + 8 + g * 2, u, tile_pair(rn4, g))
                    o = tile_of(hT, g * 2 + u)
                    dve.tensor_tensor(o, o, tile_of(rn4, g * 2 + u), ALU.mult).then_inc(s["gdone"], 1)
                dve.wait_ge(s["c_pv_mm"], G + 1)
                for pair in range(2):
                    for h2 in range(2):
                        rows = slice(64 * h2, 64 * h2 + 64)
                        dst = hT[rows, 6 + pair, ds(g * 16 + SEQ, 16)].rearrange("p (b t) -> p b t", b=4)
                        at = 16 * pair + 4 * (2 * pair + h2)
                        src = ps[rows, 6, 0:128].rearrange("p (b x) -> p b x", b=4)[:, :, at:at + 4]
                        last = cp(dst, src)
                last.then_inc(s["c_group_done"], 1)

            def sample_b(l):
                scale = 64 ** -0.5
                dve.memset(qb_all, 0.0)
                dve.drain()
                for pair in range(2):
                    for h2 in range(2):
                        rows = slice(64 * h2, 64 * h2 + 64)
                        off = 128 * pair + (2 * pair + h2) * 4
                        dst = qb_all.rearrange("p (b x) -> p b x", b=8)[rows, :, off:off + 4]
                        last = cp(dst, z[rows, 16 + pair, SEQ:NT].rearrange("p (b t) -> p b t", b=8))
                last.then_inc(s["bq"], 1)
                for b in range(NB_S):
                    dve.wait_ge(s["bk_free"], l * 8 + b + 3)
                    dve.wait_ge(s["bs_mm"], l * 8 + b + 1)
                    cp(b_kt[:, b % 2, 1, :], flat[:, 3072:3072 + KEYS_B]).then_inc(s["bkt_v"], 1)
                dve.wait_ge(s["bsn"], l + 1)
                stt(b_s[:, 0:KEYS_B], flat[:, 0:KEYS_B], scale, bias_b[:, :], ALU.mult, ALU.add)
                stt(b_s[:, KEYS_B:KEYS_B + NS], ps[:, 2, 0:NS], scale, bias_bn[:, :], ALU.mult, ALU.add)
                dve.drain()
                dve.reduce_max(c_mx[:, 0:1], b_s[:, :], AX)
                dve.drain()
                dve.tensor_scalar(c_mx[:, 1:2], c_mx[:, 0:1], -1.0, None, ALU.mult).then_inc(s["b_max"], 1)
                dve.wait_ge(s["b_exp"], l + 1)
                dve.reciprocal(c_mx[:, 3:4], c_mx[:, 2:3])
                dve.drain()
                dve.tensor_scalar(b_s[:, :], b_s[:, :], c_mx[:, 3:4], None, ALU.mult).then_inc(s["bp"], 1)
                dve.wait_ge(s["b_pv_mm"], l + 1)
                for pair in range(2):
                    for h2 in range(2):
                        rows = slice(64 * h2, 64 * h2 + 64)
                        dst = hT[rows, 4 + pair, SEQ:NT].rearrange("p (b t) -> p b t", b=8)
                        at = 16 * pair + 4 * (2 * pair + h2)
                        src = ps[rows, 0, 0:256].rearrange("p (b x) -> p b x", b=8)[:, :, at:at + 4]
                        last = cp(dst, src)
                last.then_inc(s["b_out"], 1)

            def prompt(l):
                def logits(u):
                    par, wid, n = u % 2, 128 * (u % 4 + 1), maps(u)
                    dve.wait_ge(s["p_mm"], l * 32 + u + 1)
                    if u >= 2:
                        dve.wait_ge(s["ppt_mm"], l * 32 + u - 1)
                    scale = (64 if u < 16 else 32) ** -0.5
                    for mp in range(n):
                        stt(p_s[:, par, mp, 0:wid], ps[:, 2 * par + mp, 0:wid], scale, strips[:, u // 4, SEQ - wid:SEQ],
                            ALU.mult, ALU.add)
                    dve.drain()
                    dve.reduce_max(p_mx[:, par, 0:n], p_s[:, par, 0:n, 0:wid], AX)
                    dve.drain()
                    dve.tensor_scalar(p_mx[:, par, 2:2 + n], p_mx[:, par, 0:n], -1.0, None, ALU.mult).then_inc(s["p_max"], 1)

                def weights(u):
                    par, wid, n = u % 2, 128 * (u % 4 + 1), maps(u)
                    dve.wait_ge(s["p_exp"], l * 32 + u + 1)
                    dve.reciprocal(p_mx[:, par, 6:6 + n], p_mx[:, par, 4:4 + n])
                    dve.drain()
                    p0, p1 = p_s[:, par, 0, 0:wid], p_s[:, par, 1, 0:wid]
                    last = dve.tensor_scalar(p0, p0, p_mx[:, par, 6:7], None, ALU.mult)
                    if n == 2:
                        dve.tensor_scalar(p_mx[:, par, 5:6], p_mx[:, par, 7:8], lam, -1.0, ALU.mult, ALU.mult)
                        dve.drain()
                        last = stt(p0, p1, p_mx[:, par, 5:6], p0, ALU.mult, ALU.add)
                    last.then_inc(s["p_soft"], 1)

                def result(u):
                    head = u // 4
                    rows = slice(64 * (head % 2), 64 * (head % 2) + 64)
                    dve.wait_ge(s["po_mm"], l * 32 + u + 1)
                    cp(hT[rows, 4 + head // 2, 128 * (u % 4):128 * (u % 4) + 128], ps[rows, 6 + u % 2, 0:128])\
                        .then_inc(s["p_out"], 1)

                for u in range(35):
                    if u < 32:
                        logits(u)
                    if 1 <= u < 33:
                        weights(u - 1)
                    if u >= 3:
                        result(u - 3)

            with dve.Fori(0, DEPTH) as l:
                cp(lay_conv[:, :], cols_conv[:, ds(l * 48, 48)])
                cp(lay_norm[:, :], cols_norm[:, ds(l * LV, LV)])
                cp(lam, lam_all[:, ds(l, 1)])
                cp(lay_rows[:, :], key_rows[:, ds(l, 1), :].rearrange("p l n -> p (l n)"))
                cp(ea, a_log_c[:, ds(l * 4, 4)])
                cp(dtb, dt_c[:, ds(l * 4, 4)])
                cp(lay_ba[:, :, :], all_ba[:, ds(l, 1)].rearrange("p l k n -> p (l k) n"))
                dve.drain()
                dve.tensor_scalar(sign, C("m1"), lam, -1.0, ALU.mult, ALU.mult)
                dve.tensor_tensor(cnorm, lay_norm[:, 25:26], C("oml")[:, ds(l, 1)], ALU.mult)
                dve.drain()
                dve.tensor_tensor(sign, sign, C("m0"), ALU.add).then_inc(s["layer_vecs"], 1)
                norm(l * 3, lay_norm[:, 0:8])
                ffn(l, 0)
                dve.wait_ge(s["conv_in_mm"], l + 1)
                cp(xs[:, :, :, 0:3], ps[:, 6, 0:288].rearrange("p (c b j) -> p c b j", c=12, b=8))
                norm(l * 3 + 1, lay_norm[:, 8:16])
                project(l)
                dve.drain()
                dve.memset(m["S"][:, :, :], 0.0).then_inc(s["state_done"], 1)
                spread(0)
                with dve.Fori(0, 3) as c:
                    chunk(l, c, True)
                chunk(l, 3, False)
                sample_chunk(l)
                dve.memset(qc_all, 0.0)
                dve.wait_ge(s["gsq"], l * 14 + 8 + 4)
                alone(dve)
                for i in range(4):
                    stt(hT[:, i, :], hT[:, i, :], lay_norm[:, 24:25], z[:, 12 + i, :], ALU.mult, ALU.mult)
                dve.drain()
                with dve.Fori(0, 2) as g:
                    group_c(l, g)
                sample_b(l)
                prompt(l)
                for u in range(2):
                    inverse_root(l * 14 + 12, u, rn4)
                    o = hT[:, 6 + u, :]
                    stt(o, o, cnorm, rn4[:, u, :], ALU.mult, ALU.mult).then_inc(s["gdone"], 1)
                dve.drain()
                dve.memset(gated[:, 0, :], 0.0)
                dve.drain()
                for o in range(8):
                    dve.wait_ge(s["out_done"], l * 8 + o + 1)
                    dve.tensor_tensor(tok(xT[:, o, :]), tok(xT[:, o, :]), both(2 * (o % 4)), ALU.add).then_inc(s["x_out"], 1)
                    add_square(l * 3 + 2, o)
                dve.drain().then_inc(s["x_new"], 1)
                norm(l * 3 + 2, lay_norm[:, 16:24])
                ffn(l, 1)
            norm(6, cols_norm[:, 2 * LV:2 * LV + 8])
            for b in range(5):
                n = 128 if b < 4 else NS
                dve.wait_ge(s["y_mm"], b + 1)
                at = 1024 * (b % 2)
                cp(y_rows[0:n, b, :], flat[0:n, at:at + 1024]).then_inc(s["y_rows"], 1)


NAMES = ("x_prompt", "x_sample", "state_delta", "state_conv", "cache_win_k", "cache_win_v", "cache_k", "cache_v",
         "page_table", "w_in", "conv_w", "a_log", "dt_bias", "a_norm_w", "lambda_q1", "lambda_k1", "lambda_q2",
         "lambda_k2", "c_norm_w", "rel_bias", "w_out", "norm_ffn1", "w1_gate", "w1_up", "w1_down", "norm_mix",
         "norm_ffn2", "w2_gate", "w2_up", "w2_down", "final_norm")
OUTS = (("y_p", (1, SEQ, D)), ("y_s", (NB_S, T_S, D)), ("delta_p", (DEPTH, 1, NH, DK, DK)),
        ("delta_s", (DEPTH, NB_S, NH, DK, DK)), ("conv_p", (DEPTH, 1, 3, CONV_CH)), ("conv_s", (DEPTH, NB_S, 3, CONV_CH)),
        ("wk_p", (DEPTH, 1, SEQ, 4, 64)), ("wk_s", (DEPTH, NB_S, T_S, 4, 64)), ("wv_p", (DEPTH, 1, SEQ, 4, 64)),
        ("wv_s", (DEPTH, NB_S, T_S, 4, 64)), ("k_p", (DEPTH, 1, SEQ, 4, 64)), ("k_s", (DEPTH, NB_S, T_S, 4, 64)),
        ("v_p", (DEPTH, 1, SEQ, 4, 64)), ("v_s", (DEPTH, NB_S, T_S, 4, 64)))


def kernel(**inputs):
    import concourse.bacc as bacc
    from concourse.bass_utils import run_bass_kernel_spmd

    nc = bacc.Bacc("TRN2", target_bir_lowering=False, num_devices=1)
    consts, buckets, pick = constant_arrays()
    given = {name: inputs[name] for name in NAMES}
    given.update(consts=consts, buckets=buckets, pick=pick)
    arrays, handles = {}, {}
    for name, value in given.items():
        a = np.ascontiguousarray(value)
        arrays["in_" + name] = a
        handles[name] = nc.dram_tensor("in_" + name, a.shape, mybir.dt.from_np(a.dtype), kind="ExternalInput").ap()
    outs = {name: nc.dram_tensor("out_" + name, shape, F32, kind="ExternalOutput").ap() for name, shape in OUTS}
    scratch = nc.dram_tensor("bias_tables", (8, U_TAB), F32, kind="Internal").ap()
    trunk(nc, handles, outs, scratch)
    r = run_bass_kernel_spmd(nc, [arrays], core_ids=[0])
    return tuple(r.results[0]["out_" + name] for name, _ in OUTS)
```
